# Optimizing a Trainium2 kernel written in Bass

```python
import math
import jax, jax.numpy as jnp
from jax import lax
import numpy as np

'''One inference step of a 4-layer hybrid streaming encoder trunk, run for two request groups sharing the same weights.

Layer i uses token mixer (i mod 2): even layers = chunk-banded sliding-window GQA with attention sinks and ALiBi, odd layers = Mamba-2 SSD. Every token-mixing sub-layer also carries a parallel 4-head cross-attention group into 256 memory tokens. One combined input projection and one output projection per layer, sandwich RMSNorm, squared-ReLU MLP after every layer.

Inputs:
  x_prompt (BATCH, SEQ, D_MODEL), x_sample (DEC_BATCH, DEC_SEQ, D_MODEL), mem_prompt (BATCH, N_MEM, D_MODEL)
  cache_swa_k / cache_swa_v (N_ATTN_LAYERS, DEC_BATCH, min(WINDOW, PAST_LEN), N_KV_HEADS, HEAD_DIM)
  state_ssm  (N_SSM_LAYERS, DEC_BATCH, SSM_HEADS, SSM_HEAD_DIM, D_STATE)
  state_conv (N_SSM_LAYERS, DEC_BATCH, CONV_W - 1, CONV_DIM)
  cache_mem_k / cache_mem_v (DEPTH, DEC_BATCH, N_MEM, MEM_HEADS, MEM_HEAD_DIM)
  followed by the weights.
Output tuple:
  y_prompt (BATCH, SEQ, D_MODEL), y_sample (DEC_BATCH, DEC_SEQ, D_MODEL),
  prompt_swa_k, prompt_swa_v (N_ATTN_LAYERS, BATCH, min(WINDOW, SEQ), N_KV_HEADS, HEAD_DIM)  last window rows,
  prompt_ssm (N_SSM_LAYERS, BATCH, SSM_HEADS, SSM_HEAD_DIM, D_STATE)  final SSD state,
  prompt_conv (N_SSM_LAYERS, BATCH, CONV_W - 1, CONV_DIM)  last conv input rows,
  prompt_mem_k, prompt_mem_v (DEPTH, BATCH, N_MEM, MEM_HEADS, MEM_HEAD_DIM),
  sample_swa_k, sample_swa_v (N_ATTN_LAYERS, DEC_BATCH, DEC_SEQ, N_KV_HEADS, HEAD_DIM)  new rows,
  sample_ssm (N_SSM_LAYERS, DEC_BATCH, SSM_HEADS, SSM_HEAD_DIM, D_STATE)  updated state,
  sample_conv (N_SSM_LAYERS, DEC_BATCH, CONV_W - 1, CONV_DIM)  updated conv buffer.
'''

D_MODEL = 1024
BATCH = 1
SEQ = 512
DEPTH = 2
DEC_BATCH = 1
DEC_SEQ = 64
PAST_LEN = 256

CHUNK = 64
N_HEADS = 24
N_KV_HEADS = 3
HEAD_DIM = 64
GQA_GROUP = N_HEADS // N_KV_HEADS
WINDOW = 128
WINDOW_CHUNKS = WINDOW // CHUNK
Q_WIDTH = N_HEADS * HEAD_DIM
KV_WIDTH = N_KV_HEADS * HEAD_DIM
N_MEM = 256
MEM_HEADS = 4
MEM_HEAD_DIM = 128
MEM_WIDTH = MEM_HEADS * MEM_HEAD_DIM
SSM_INNER = 1536
SSM_HEAD_DIM = 64
SSM_HEADS = SSM_INNER // SSM_HEAD_DIM
SSM_GROUPS = 8
D_STATE = 128
CONV_W = 4
CONV_DIM = SSM_INNER + 2 * SSM_GROUPS * D_STATE
MIX_WIDTH = Q_WIDTH + MEM_WIDTH
D_FF = 4 * D_MODEL
IN_ATTN = Q_WIDTH + 2 * KV_WIDTH + MEM_WIDTH
IN_SSM = SSM_INNER + CONV_DIM + SSM_HEADS + MEM_WIDTH
N_ATTN_LAYERS = (DEPTH + 1) // 2
N_SSM_LAYERS = DEPTH // 2
EPS = 1e-6

kernel_name = 'hybrid_swa_ssd_memory_stream_step'

def rmsnorm(x, w):
    xf = x.astype(jnp.float32)
    y = xf * lax.rsqrt(jnp.mean(xf * xf, axis=-1, keepdims=True) + EPS)
    return (y * w.astype(jnp.float32)).astype(x.dtype)

def alibi_slopes():
    s = 2.0 ** (-8.0 * np.arange(1, N_HEADS + 1) / N_HEADS)
    return jnp.asarray(s, dtype=jnp.float32).reshape(N_KV_HEADS, GQA_GROUP)

def sink_probs(scores, sink):
    m = jnp.maximum(jnp.max(scores, axis=-1, keepdims=True), sink)
    p = jnp.exp(scores - m)
    return p / (jnp.sum(p, axis=-1, keepdims=True) + jnp.exp(sink - m))

def swa_prompt(q, k, v, sink):
    b, l = q.shape[:2]
    nc = l // CHUNK
    span = (WINDOW_CHUNKS + 1) * CHUNK
    qb = q.reshape(b, nc, CHUNK, N_KV_HEADS, GQA_GROUP, HEAD_DIM)
    pad = ((0, 0), (WINDOW_CHUNKS * CHUNK, 0), (0, 0), (0, 0))
    kp = jnp.pad(k, pad).reshape(b, nc + WINDOW_CHUNKS, CHUNK, N_KV_HEADS, HEAD_DIM)
    vp = jnp.pad(v, pad).reshape(b, nc + WINDOW_CHUNKS, CHUNK, N_KV_HEADS, HEAD_DIM)
    kb = jnp.concatenate([kp[:, w:w + nc] for w in range(WINDOW_CHUNKS + 1)], axis=2)
    vb = jnp.concatenate([vp[:, w:w + nc] for w in range(WINDOW_CHUNKS + 1)], axis=2)
    s = jnp.einsum('bcqkgd,bcskd->bckgqs', qb, kb).astype(jnp.float32) / math.sqrt(HEAD_DIM)
    dist = WINDOW_CHUNKS * CHUNK + jnp.arange(CHUNK)[:, None] - jnp.arange(span)[None, :]
    bias = -alibi_slopes()[:, :, None, None] * jnp.abs(dist).astype(jnp.float32)
    key_pos = (jnp.arange(nc)[:, None] - WINDOW_CHUNKS) * CHUNK + jnp.arange(span)[None, :]
    valid = (key_pos >= 0)[None, :, None, None, None, :]
    s = jnp.where(valid, s + bias[None, None], -jnp.inf)
    sk = sink.astype(jnp.float32).reshape(N_KV_HEADS, GQA_GROUP)[None, None, :, :, None, None]
    p = sink_probs(s, sk)
    o = jnp.einsum('bckgqs,bcskd->bcqkgd', p.astype(v.dtype), vb)
    return o.reshape(b, l, Q_WIDTH)

def swa_sample(q, k, v, cache_k, cache_v, sink):
    b, l = q.shape[:2]
    keep = cache_k.shape[1]
    kk = jnp.concatenate([cache_k.astype(k.dtype), k], axis=1)
    vv = jnp.concatenate([cache_v.astype(v.dtype), v], axis=1)
    qh = q.reshape(b, l, N_KV_HEADS, GQA_GROUP, HEAD_DIM)
    s = jnp.einsum('bqkgd,bskd->bkgqs', qh, kk).astype(jnp.float32) / math.sqrt(HEAD_DIM)
    dist = keep + jnp.arange(l)[:, None] - jnp.arange(keep + l)[None, :]
    bias = -alibi_slopes()[:, :, None, None] * jnp.abs(dist).astype(jnp.float32)
    sk = sink.astype(jnp.float32).reshape(N_KV_HEADS, GQA_GROUP)[None, :, :, None, None]
    p = sink_probs(s + bias[None], sk)
    o = jnp.einsum('bkgqs,bskd->bqkgd', p.astype(v.dtype), vv)
    return o.reshape(b, l, Q_WIDTH)

def cross_attend(cq, mem_k, mem_v):
    b, l = cq.shape[:2]
    qh = cq.reshape(b, l, MEM_HEADS, MEM_HEAD_DIM)
    s = jnp.einsum('bqhd,bmhd->bhqm', qh, mem_k.astype(cq.dtype)).astype(jnp.float32) / math.sqrt(MEM_HEAD_DIM)
    p = jax.nn.softmax(s, axis=-1)
    o = jnp.einsum('bhqm,bmhd->bqhd', p.astype(cq.dtype), mem_v.astype(cq.dtype))
    return o.reshape(b, l, MEM_WIDTH)

def ssd(x, dt, A, Bm, Cm, h0, block):
    b, l = x.shape[:2]
    hg = SSM_HEADS // SSM_GROUPS
    nc = l // block
    xf = x.astype(jnp.float32).reshape(b, nc, block, SSM_GROUPS, hg, SSM_HEAD_DIM)
    dtf = dt.astype(jnp.float32).reshape(b, nc, block, SSM_GROUPS, hg)
    Bf = Bm.astype(jnp.float32).reshape(b, nc, block, SSM_GROUPS, D_STATE)
    Cf = Cm.astype(jnp.float32).reshape(b, nc, block, SSM_GROUPS, D_STATE)
    acs = jnp.cumsum(dtf * A.astype(jnp.float32).reshape(SSM_GROUPS, hg), axis=2)
    xdt = xf * dtf[..., None]
    causal = jnp.tril(jnp.ones((block, block), dtype=bool))[:, :, None, None]
    diff = acs[:, :, :, None] - acs[:, :, None, :]
    decay = jnp.exp(jnp.where(causal, diff, -jnp.inf))
    cb = jnp.einsum('bcqgn,bcsgn->bcqsg', Cf, Bf)
    y_diag = jnp.einsum('bcqsg,bcqsgh,bcsghp->bcqghp', cb, decay, xdt)
    decay_end = jnp.exp(acs[:, :, -1:] - acs)
    states = jnp.einsum('bcsgn,bcsgh,bcsghp->bcghpn', Bf, decay_end, xdt)
    block_decay = jnp.exp(acs[:, :, -1])

    def step(h, inp):
        s_c, d_c = inp
        return h * d_c[..., None, None] + s_c, h

    h_init = h0.astype(jnp.float32).reshape(b, SSM_GROUPS, hg, SSM_HEAD_DIM, D_STATE)
    h_last, h_in = lax.scan(step, h_init, (jnp.moveaxis(states, 1, 0), jnp.moveaxis(block_decay, 1, 0)))
    h_in = jnp.moveaxis(h_in, 0, 1)
    y_off = jnp.einsum('bcqgn,bcghpn,bcqgh->bcqghp', Cf, h_in, jnp.exp(acs))
    y = (y_diag + y_off).reshape(b, l, SSM_HEADS, SSM_HEAD_DIM)
    return y.astype(x.dtype), h_last.reshape(b, SSM_HEADS, SSM_HEAD_DIM, D_STATE)

def ssm_mixer(z, xbc, dt_raw, conv_hist, h0, conv_w, conv_b, dt_bias, a_log, d_skip, norm_w, block):
    b, l = z.shape[:2]
    xpad = jnp.concatenate([conv_hist.astype(xbc.dtype), xbc], axis=1)
    new_conv = xpad[:, xpad.shape[1] - (CONV_W - 1):]
    conv = lax.conv_general_dilated(xpad, conv_w[:, None, :].astype(xbc.dtype), window_strides=(1,), padding='VALID',
                                    dimension_numbers=('NWC', 'WIO', 'NWC'), feature_group_count=CONV_DIM)
    u = jax.nn.silu(conv + conv_b.astype(xbc.dtype))
    xs, Bm, Cm = jnp.split(u, [SSM_INNER, SSM_INNER + SSM_GROUPS * D_STATE], axis=-1)
    dt = jax.nn.softplus(dt_raw.astype(jnp.float32) + dt_bias.astype(jnp.float32))
    A = -jnp.exp(a_log.astype(jnp.float32))
    xh = xs.reshape(b, l, SSM_HEADS, SSM_HEAD_DIM)
    y, h_last = ssd(xh, dt, A, Bm.reshape(b, l, SSM_GROUPS, D_STATE), Cm.reshape(b, l, SSM_GROUPS, D_STATE), h0, block)
    y = (y + d_skip.astype(xs.dtype)[:, None] * xh).reshape(b, l, SSM_INNER) * jax.nn.silu(z)
    y = rmsnorm(y.reshape(b, l, SSM_GROUPS, SSM_INNER // SSM_GROUPS), norm_w.reshape(SSM_GROUPS, SSM_INNER // SSM_GROUPS))
    return y.reshape(b, l, SSM_INNER), new_conv, h_last

def trunk(x, mem_k, mem_v, swa_k_cache, swa_v_cache, ssm_cache, conv_cache, prompt, p):
    b, l, _ = x.shape
    new_k, new_v, new_h, new_conv = [], [], [], []
    for i in range(DEPTH):
        j = i // 2
        h = rmsnorm(x, p['norm_mix_pre'][i])
        if i % 2 == 0:
            proj = h @ p['w_in_attn'][j]
            q, k, v, cq = jnp.split(proj, [Q_WIDTH, Q_WIDTH + KV_WIDTH, Q_WIDTH + 2 * KV_WIDTH], axis=-1)
            q = q.reshape(b, l, N_HEADS, HEAD_DIM)
            k = k.reshape(b, l, N_KV_HEADS, HEAD_DIM)
            v = v.reshape(b, l, N_KV_HEADS, HEAD_DIM)
            if prompt:
                a = swa_prompt(q, k, v, p['attn_sinks'][j])
                keep = min(WINDOW, l)
                new_k.append(k[:, l - keep:])
                new_v.append(v[:, l - keep:])
            else:
                a = swa_sample(q, k, v, swa_k_cache[j], swa_v_cache[j], p['attn_sinks'][j])
                new_k.append(k)
                new_v.append(v)
        else:
            proj = h @ p['w_in_ssm'][j]
            z, xbc, dt_raw, cq = jnp.split(proj, [SSM_INNER, SSM_INNER + CONV_DIM, SSM_INNER + CONV_DIM + SSM_HEADS], axis=-1)
            if prompt:
                hist = jnp.zeros((b, CONV_W - 1, CONV_DIM), x.dtype)
                h0 = jnp.zeros((b, SSM_HEADS, SSM_HEAD_DIM, D_STATE), jnp.float32)
                block = CHUNK
            else:
                hist = conv_cache[j]
                h0 = ssm_cache[j]
                block = l
            a, cs, hs = ssm_mixer(z, xbc, dt_raw, hist, h0, p['conv_w'][j], p['conv_b'][j], p['dt_bias'][j],
                                  p['a_log'][j], p['d_skip'][j], p['ssm_norm'][j], block)
            new_conv.append(cs)
            new_h.append(hs)
        c = cross_attend(cq, mem_k[i], mem_v[i])
        mix = jnp.concatenate([a, c], axis=-1) @ p['w_out'][i]
        x = x + rmsnorm(mix, p['norm_mix_post'][i])
        h = rmsnorm(x, p['norm_ffn_pre'][i])
        f = jnp.square(jax.nn.relu(h @ p['w_up'][i])) @ p['w_down'][i]
        x = x + rmsnorm(f, p['norm_ffn_post'][i])
    return x, jnp.stack(new_k), jnp.stack(new_v), jnp.stack(new_h), jnp.stack(new_conv)

def setup_inputs(seed: int = 0) -> dict:
    key = jax.random.key(seed)
    ks = jax.random.split(key, 32)
    f32 = jnp.float32

    def nrm(k, shape, scale):
        return jax.random.normal(k, shape, f32) * scale

    swa_keep = min(WINDOW, PAST_LEN)
    dt0 = jnp.exp(jax.random.uniform(ks[19], (N_SSM_LAYERS, SSM_HEADS), f32, math.log(1e-3), math.log(1e-1)))
    return {
        'x_prompt': nrm(ks[0], (BATCH, SEQ, D_MODEL), 1.0),
        'x_sample': nrm(ks[1], (DEC_BATCH, DEC_SEQ, D_MODEL), 1.0),
        'mem_prompt': nrm(ks[2], (BATCH, N_MEM, D_MODEL), 1.0),
        'cache_swa_k': nrm(ks[3], (N_ATTN_LAYERS, DEC_BATCH, swa_keep, N_KV_HEADS, HEAD_DIM), 1.0),
        'cache_swa_v': nrm(ks[4], (N_ATTN_LAYERS, DEC_BATCH, swa_keep, N_KV_HEADS, HEAD_DIM), 1.0),
        'state_ssm': nrm(ks[5], (N_SSM_LAYERS, DEC_BATCH, SSM_HEADS, SSM_HEAD_DIM, D_STATE), 0.1),
        'state_conv': nrm(ks[6], (N_SSM_LAYERS, DEC_BATCH, CONV_W - 1, CONV_DIM), 1.0),
        'cache_mem_k': nrm(ks[7], (DEPTH, DEC_BATCH, N_MEM, MEM_HEADS, MEM_HEAD_DIM), 1.0),
        'cache_mem_v': nrm(ks[8], (DEPTH, DEC_BATCH, N_MEM, MEM_HEADS, MEM_HEAD_DIM), 1.0),
        'norm_mix_pre': 1.0 + nrm(ks[9], (DEPTH, D_MODEL), 0.05),
        'norm_mix_post': 1.0 + nrm(ks[10], (DEPTH, D_MODEL), 0.05),
        'norm_ffn_pre': 1.0 + nrm(ks[11], (DEPTH, D_MODEL), 0.05),
        'norm_ffn_post': 1.0 + nrm(ks[12], (DEPTH, D_MODEL), 0.05),
        'w_in_attn': nrm(ks[13], (N_ATTN_LAYERS, D_MODEL, IN_ATTN), D_MODEL ** -0.5),
        'attn_sinks': nrm(ks[14], (N_ATTN_LAYERS, N_HEADS), 0.5),
        'w_in_ssm': nrm(ks[15], (N_SSM_LAYERS, D_MODEL, IN_SSM), D_MODEL ** -0.5),
        'conv_w': nrm(ks[16], (N_SSM_LAYERS, CONV_W, CONV_DIM), 0.5),
        'conv_b': nrm(ks[17], (N_SSM_LAYERS, CONV_DIM), 0.02),
        'dt_bias': dt0 + jnp.log(-jnp.expm1(-dt0)),
        'a_log': jnp.log(jax.random.uniform(ks[18], (N_SSM_LAYERS, SSM_HEADS), f32, 1.0, 16.0)),
        'd_skip': 1.0 + nrm(ks[20], (N_SSM_LAYERS, SSM_HEADS), 0.1),
        'ssm_norm': 1.0 + nrm(ks[21], (N_SSM_LAYERS, SSM_INNER), 0.05),
        'mem_norm': 1.0 + nrm(ks[22], (DEPTH, D_MODEL), 0.05),
        'w_mem_kv': nrm(ks[23], (DEPTH, D_MODEL, 2 * MEM_WIDTH), D_MODEL ** -0.5),
        'w_out': nrm(ks[24], (DEPTH, MIX_WIDTH, D_MODEL), MIX_WIDTH ** -0.5),
        'w_up': nrm(ks[25], (DEPTH, D_MODEL, D_FF), D_MODEL ** -0.5),
        'w_down': nrm(ks[26], (DEPTH, D_FF, D_MODEL), D_FF ** -0.5),
    }

def reference(x_prompt, x_sample, mem_prompt, cache_swa_k, cache_swa_v, state_ssm, state_conv, cache_mem_k, cache_mem_v,
              norm_mix_pre, norm_mix_post, norm_ffn_pre, norm_ffn_post, w_in_attn, attn_sinks, w_in_ssm, conv_w, conv_b,
              dt_bias, a_log, d_skip, ssm_norm, mem_norm, w_mem_kv, w_out, w_up, w_down):
    p = dict(norm_mix_pre=norm_mix_pre, norm_mix_post=norm_mix_post, norm_ffn_pre=norm_ffn_pre,
             norm_ffn_post=norm_ffn_post, w_in_attn=w_in_attn, attn_sinks=attn_sinks, w_in_ssm=w_in_ssm,
             conv_w=conv_w, conv_b=conv_b, dt_bias=dt_bias, a_log=a_log, d_skip=d_skip, ssm_norm=ssm_norm,
             w_out=w_out, w_up=w_up, w_down=w_down)
    bp = mem_prompt.shape[0]
    mk, mv = [], []
    for i in range(DEPTH):
        kv = rmsnorm(mem_prompt, mem_norm[i]) @ w_mem_kv[i]
        k_i, v_i = jnp.split(kv, [MEM_WIDTH], axis=-1)
        mk.append(k_i.reshape(bp, N_MEM, MEM_HEADS, MEM_HEAD_DIM))
        mv.append(v_i.reshape(bp, N_MEM, MEM_HEADS, MEM_HEAD_DIM))
    prompt_mem_k = jnp.stack(mk)
    prompt_mem_v = jnp.stack(mv)
    y_prompt, prompt_swa_k, prompt_swa_v, prompt_ssm, prompt_conv = trunk(
        x_prompt, prompt_mem_k, prompt_mem_v, None, None, None, None, True, p)
    y_sample, sample_swa_k, sample_swa_v, sample_ssm, sample_conv = trunk(
        x_sample, cache_mem_k, cache_mem_v, cache_swa_k, cache_swa_v, state_ssm, state_conv, False, p)
    return (y_prompt, y_sample, prompt_swa_k, prompt_swa_v, prompt_ssm, prompt_conv, prompt_mem_k, prompt_mem_v,
            sample_swa_k, sample_swa_v, sample_ssm, sample_conv)


_drawn_inputs = setup_inputs


def setup_inputs(seed=0):
    import zlib

    import numpy as np

    out = dict(_drawn_inputs(seed))
    spreads = {}
    factors = {}
    for name, (base, spread) in spreads.items():
        noise = np.random.default_rng([zlib.crc32(name.encode()), seed]).standard_normal(out[name].shape)
        drawn = base * np.exp(spread * noise) if base else spread * noise
        out[name] = __import__('jax').numpy.asarray(drawn.astype(out[name].dtype))
    for name, factor in factors.items():
        out[name] = (out[name] * factor).astype(out[name].dtype)
    return out
```

```python
from contextlib import ExitStack

import concourse.bass as bass
from concourse import mybir

F32 = mybir.dt.float32
F32R = mybir.dt.float32r
ALU = mybir.AluOpType
ACT = mybir.ActivationFunctionType
AX = mybir.AxisListType

P = 128
D_MODEL, SEQ, DEC = 1024, 512, 64
TOK = DEC + SEQ
HALF = TOK // 2
KT = D_MODEL // P
HEADS, KVH, HD = 24, 3, 64
GROUP = HEADS // KVH
Q_W, KV_W = HEADS * HD, KVH * HD
N_MEM, MEM_H, MEM_D = 256, 4, 128
MEM_W = MEM_H * MEM_D
INNER, SGROUPS, STATE, CONV_W = 1536, 8, 128, 4
CONV_DIM = INNER + 2 * SGROUPS * STATE
MIX_T = (Q_W + MEM_W) // P
D_FF = 4 * D_MODEL
FF_CHUNKS = D_FF // D_MODEL
EPS = 1e-6
BLOCKS = 5
QT = GROUP // 2
SLABS_FF = 2 * KT


def block_cols(b):
    return (0, DEC) if b == 0 else (DEC + (b - 1) * P, DEC + b * P)


class Loop:
    i, per = None, {}


PRIMED = {"tensor": ("seg_done", "diag_done", "off_done", "acc_done", "st_done", "gsum_done"),
          "scalar": ("groot_done",),
          "vector": ("gnorm_done", "yoff_done", "decm_done", "gate_done", "state_done"),
          "gpsimd": ("ytok_done", "hbd_done"), "sync": ("h_stored",)}
PRIMED_NAMES = sum(PRIMED.values(), ())


def at(loop, sem, value):
    value += sem.name in PRIMED_NAMES
    if loop.i is None:
        return value
    assert value > 0, sem.name
    return value + loop.i * loop.per[sem.name]


MEM_SLABS = 2 * MEM_W // P
KV_SLABS = KVH + 2
Q_SLABS = (Q_W + MEM_W) // P
OUT_SLABS = 2 * KT
FF_SLABS = FF_CHUNKS * SLABS_FF
PAIRS = SGROUPS // 2
PH = 2 * HEADS // SGROUPS
XT = PH * HD // P
PAIR_SLABS = XT + 2 + 2 + XT
CQ_SLABS = MEM_W // P
ATTN_SLABS = KV_SLABS + Q_SLABS
SSM_SLABS = 1 + PAIRS * PAIR_SLABS + CQ_SLABS
ALL_SLABS = 2 * MEM_SLABS + ATTN_SLABS + SSM_SLABS + 2 * (OUT_SLABS + FF_SLABS)

C_MIX_PRE, C_MIX_POST, C_FF_PRE, C_FF_POST, C_MEM = 0, 16, 32, 48, 64
C_SINK, C_DTB, C_ALOG = 80, 104, 128
UT = XT + 4
TAPS = CONV_W + 1 + CONV_W - 1
C_CONV = 152
C_PAIR = C_CONV + PAIRS * UT * TAPS
N_PAIR = XT + PH
N_PAR = C_PAIR + PAIRS * N_PAIR

UNITS_J = 5
UNITS = QT * UNITS_J
LAG_T, LAG_PV = 2, 3
SPAN = P + DEC + SEQ


PAST = CONV_W - 1
XP = PAST + DEC + PAST + SEQ
UC = XP - PAST


def conv_cols(b):
    c0, c1 = block_cols(b)
    return (c0, c1) if b == 0 else (c0 + PAST, c1 + PAST)


def ssd_steps(eighths):
    steps, k = [], 0

    def fill(upto):
        nonlocal k
        while k < min(upto, eighths):
            steps.append(("K", k))
            k += 1

    for b in range(BLOCKS):
        steps.append(("A", b))
        fill(b + 1)
    last = min(eighths, UT * KT + 6) if eighths > UT * KT else eighths - 6
    gap = 0
    for b in range(BLOCKS):
        for kind in ("seg", "off", "st", "diag", "acc"):
            if kind != "off":
                gap += 1
                fill(BLOCKS + (last - BLOCKS) * gap // (4 * BLOCKS + 1))
            steps.append((kind, b))
    steps.append(("Q", 0))
    fill(last + (eighths - last) // 3)
    steps.append(("G", 0))
    fill(last + 2 * (eighths - last) // 3)
    steps.append(("N", 0))
    fill(eighths)
    return steps


def attention_steps():
    steps, k, total = [], 0, UNITS + LAG_PV
    for t in range(total):
        if t < UNITS:
            steps.append(("S", t))
        if 0 <= t - LAG_T < UNITS:
            steps.append(("T", t - LAG_T))
        while k < QT * KT and (k + 1) * (total - 1) <= t * QT * KT:
            steps.append(("K", k))
            k += 1
        if 0 <= t - LAG_PV < UNITS:
            steps.append(("V", t - LAG_PV))
    while k < QT * KT:
        steps.append(("K", k))
        k += 1
    return steps


def build(nc, slabs, x_in, mem_in, par_in, mats_in, alibi, ck_in, cv_in, mk_in, mv_in, h_in, outs):
    (y_out, swk_out, swv_out, h_out, conv_out, memk_out, memv_out) = outs
    ctx = ExitStack()
    with ctx:
        base = [nc.sbuf_base]

        def sb_at(name, shape, dt, offset):
            return nc.alloc_sbuf_tensor_at(name, shape, dt, offset=offset)

        class Area:
            def __init__(self, start, end):
                self.p, self.end = start, end

            def take(self, name, shape, dt=F32):
                size = 4
                for n in shape[1:]:
                    size *= n
                start = (self.p + 31) // 32 * 32
                assert start + size <= self.end, (name, start + size - self.end)
                self.p = start + size
                return sb_at(name, shape, dt, start)

        main = Area(nc.sbuf_base, nc.sbuf_usable_end)
        x = main.take("x", [P, KT, TOK])
        raw = main.take("raw", [P, 2, KT, P])
        w_hi = main.take("w_hi", [P, 2, KT, P], F32R)
        w_lo = main.take("w_lo", [P, 2, KT, P], F32R)
        mix = main.take("mix", [P, MIX_T, TOK])
        rstd = main.take("rstd", [P, 2, TOK])
        sq = main.take("sq", [P, 2, TOK])
        par = main.take("par", [P, N_PAR])
        mats = main.take("mats", [P, 4, P])
        eps = main.take("eps", [P, 1])
        kvm1 = main.take("kvm1", [P, MEM_SLABS // 2, N_MEM])
        vm1 = main.take("vm1", [P, 2, MEM_W])
        lo_half = main.p
        main.p = (main.p + 31) // 32 * 32
        big_start = main.p
        big_hi = main.take("big_hi", [P, MIX_T, TOK], F32R)
        big_lo = main.take("big_lo", [P, MIX_T, TOK], F32R)
        spare = main.p
        half = KT * TOK * 4
        area_a = (big_start, big_start + half)
        area_b = (big_start + 2 * half, big_start + 3 * half)
        area_c = (spare, nc.sbuf_usable_end)
        ff = Area(*area_c)
        relu = ff.take("relu", [P, 2, TOK])
        hid = ff.take("hid", [P, 2, TOK])
        ma = Area(*area_a)
        mraw = ma.take("mraw", [P, KT, N_MEM])
        msq = ma.take("msq", [P, 2, N_MEM])
        mv_t = ma.take("mv_t", [P, 2, N_MEM])
        mb = Area(*area_b)
        m_hi = mb.take("m_hi", [P, KT, N_MEM], F32R)
        m_lo = mb.take("m_lo", [P, KT, N_MEM], F32R)
        a1, a2, a3 = Area(*area_a), Area(*area_b), Area(*area_c)
        k_all = a1.take("k_all", [P, KVH, SPAN])
        k_cur = a1.take("k_cur", [P, SPAN])
        v_all = a1.take("v_all", [P, BLOCKS + 1, KVH, HD])
        v_cur = a1.take("v_cur", [P, BLOCKS + 1, HD])
        q_t = a2.take("q_t", [P, QT, TOK])
        v_t = a2.take("v_t", [P, 2, TOK])
        bias = a2.take("bias", [P, 2, 2, 2 * P])
        km0 = a3.take("km0", [P, MEM_H, N_MEM])
        vm0 = a3.take("vm0", [P, 2, MEM_W])
        kms = a3.take("kms", [P, MEM_H, N_MEM])
        vms = a3.take("vms", [P, 2, MEM_W])
        p_t = a3.take("p_t", [P, 2, 4 * P])
        rm = a3.take("rm", [P, N_MEM])
        prob = a3.take("prob", [P, 4, 2, 2 * P])
        sink_cur = a3.take("sink_cur", [P, GROUP])
        stat = a3.take("stat", [P, 4, 4, 2])

        c1, c2, c3 = Area(*area_a), Area(*area_b), Area(*area_c)
        u = c1.take("u", [P, UT, UC])
        heads_cur = c1.take("heads_cur", [P, 5, BLOCKS, PH])
        tails = c1.take("tails", [P, PAIRS, UT, 2, PAST])
        cpar = c1.take("cpar", [P, UT, TAPS])
        skips = c1.take("skips", [P, PH])
        gsq = sb_at("gsq", [P, XT, TOK], F32, (c2.p + 31) // 32 * 32)
        xtok = c2.take("xtok", [P, BLOCKS, XT * P])
        btok = c2.take("btok", [P, BLOCKS, 2, P])
        cbm = c2.take("cbm", [P, BLOCKS, 2, P])
        late = Area(*area_c)
        kms1 = late.take("kms1", [P, MEM_H, N_MEM])
        vms1 = late.take("vms1", [P, 2, MEM_W])
        xp = c3.take("xp", [P, 2, XP])
        th = c3.take("th", [P, UC])
        c3.p = max(c3.p, late.p)
        state = c3.take("state", [P, 2, PH * HD])
        h_next = c3.take("h_next", [P, PH * HD])
        ytok = c3.take("ytok", [P, PH * HD])
        hs = c3.take("hs", [P, 5, BLOCKS, HEADS])
        dts = c3.take("dts", [P, 4, BLOCKS, HEADS])
        ea = c3.take("ea", [P, HEADS])
        zs = c3.take("zs", [P, XT, TOK])
        c_cur = c3.take("c_cur", [P, 2, UC])
        grs = sb_at("grs", [P, 2, TOK], F32, (c3.p + 31) // 32 * 32)
        wseg = c3.take("wseg", [P, PH, P])
        dec = c3.take("dec", [P, PH, P])
        xd = sq[:].rearrange("p s c -> p (s c)").rearrange("p (k h d) -> p k h d", k=3, h=PH)
        hbd = rstd[:, 0, 0:PH * HD]
        YG = MIX_T - MEM_H - XT
        ps = ctx.enter_context(nc.psum_tensor("ps", [P, 8, 512], F32))
        S_BANK, T_BANK, O_BANK, STAT_BANK = 4, 6, 7, 6

        def sem(name):
            return ctx.enter_context(nc.semaphore(name))

        raw_in = [sem(f"raw_in{i}") for i in range(2)]
        hi_done, lo_done = sem("hi_done"), sem("lo_done")
        slab_done = sem("slab_done")
        freed = sem("freed")
        act_hi = sem("act_hi")
        act_ready = sem("act_ready")
        sq_ready, sq_used = sem("sq_ready"), sem("sq_used")
        root_done, rstd_ready = sem("root_done"), sem("rstd_ready")
        scaled = sem("scaled")
        x_done = sem("x_done")
        zeroed = sem("zeroed")
        hid_done = sem("hid_done")
        x_arrived, mem_arrived, const_in, cache_in = sem("x_arrived"), sem("mem_arrived"), sem("const_in"), sem("cache_in")
        mv_used, vm_done = sem("mv_used"), sem("vm_done")
        vt_done, va_done = sem("vt_done"), sem("va_done")
        cur_ready = sem("cur_ready")
        bias_in = [sem(f"bias_in{i}") for i in range(2)]
        s_half = sem("s_half")
        s_done, biased = sem("s_done"), sem("biased")
        max_done, exp_done, normed = sem("max_done"), sem("exp_done"), sem("normed")
        t_done, pt_done = sem("t_done"), sem("pt_done")
        v_done, o_done = sem("v_done"), sem("o_done")
        kms_in, nobody = sem("kms_in"), sem("nobody")
        dt_moved, dt_step, dt_fn = sem("dt_moved"), sem("dt_step"), sem("dt_fn")
        tap_done, conv_done = sem("tap_done"), sem("conv_done")
        tanh_done, u_done = sem("tanh_done"), sem("u_done")
        tails_done = sem("tails_done")
        cur_done = sem("cur_done")
        tok_done, xtok_done, cbm_done, c_done = sem("tok_done"), sem("xtok_done"), sem("cbm_done"), sem("c_done")
        wseg_done, seg_done = sem("wseg_done"), sem("seg_done")
        dec_done, decm_done = sem("dec_done"), sem("decm_done")
        xd_done, diag_done = sem("xd_done"), sem("diag_done")
        off_done, yoff_done, ytok_done = sem("off_done"), sem("yoff_done"), sem("ytok_done")
        st_done, hbd_done, state_done = sem("st_done"), sem("hbd_done"), sem("state_done")
        acc_done, gate_done = sem("acc_done"), sem("gate_done")
        gsq_done, gsum_done, groot_done, gnorm_done = sem("gsq_done"), sem("gsum_done"), sem("groot_done"), sem("gnorm_done")
        h_loaded, h_stored, grec_done = sem("h_loaded"), sem("h_stored"), sem("grec_done")
        dve_self, act_self, pool_self = sem("dve_self"), sem("act_self"), sem("pool_self")
        stored = sem("stored")
        stores = [0]

        def norm_weight(layer, k):
            return C_PAIR + k // XT * N_PAIR + k % XT if layer and k < INNER // P else None

        def halves(ap):
            return ap.rearrange("p (h c) -> p h c", h=2)

        class Count:
            def __init__(self):
                self.s = self.g = self.a = self.c = self.n = self.j = self.x = self.f = self.k = 0

        class Own:
            def __init__(self, eng, sem_):
                self.eng, self.sem, self.n = eng, sem_, 0

            def mark(self, ins):
                self.n += 1
                return ins.then_inc(self.sem, 1)

            def wait(self, loop, n=None):
                self.eng.wait_ge(self.sem, at(loop, self.sem, self.n if n is None else n))

        FF_PER = {"hi_done": SLABS_FF, "lo_done": SLABS_FF, "slab_done": SLABS_FF, "freed": SLABS_FF,
                  "raw_in0": 8 * SLABS_FF, "raw_in1": 8 * SLABS_FF, "act_ready": KT, "act_hi": KT,
                  "hid_done": KT}
        OUT_PER = {"hi_done": 4, "lo_done": 4, "slab_done": 4, "freed": 2, "raw_in0": 32, "raw_in1": 32,
                   "sq_ready": 2, "sq_used": 2}
        ATT_PER = {"hi_done": QT, "lo_done": QT, "slab_done": QT, "freed": QT, "raw_in0": 8 * QT,
                   "raw_in1": 8 * QT, "bias_in0": 8 * QT, "bias_in1": 8 * QT, "s_done": UNITS,
                   "biased": UNITS, "max_done": UNITS, "exp_done": UNITS, "normed": UNITS,
                   "t_done": UNITS, "pt_done": UNITS, "v_done": UNITS, "o_done": 2 * QT,
                   "cur_ready": 1, "s_half": QT, "dve_self": 0}
        STEPS = attention_steps()
        SSM_PER = {"hi_done": PAIR_SLABS, "lo_done": PAIR_SLABS, "slab_done": PAIR_SLABS, "freed": PAIR_SLABS,
                   "raw_in0": 8 * PAIR_SLABS, "raw_in1": 8 * PAIR_SLABS, "tap_done": UT, "conv_done": 3 * UT,
                   "tanh_done": PAIR_SLABS, "u_done": PAIR_SLABS, "tails_done": UT, "cur_done": 1,
                   "c_done": 1, "gsq_done": 1, "gsum_done": 1, "groot_done": 1, "gnorm_done": 1, "grec_done": 1,
                   "h_loaded": 16, "h_stored": 16}
        for s_ in (tok_done, xtok_done, cbm_done, wseg_done, seg_done, dec_done, decm_done, xd_done, diag_done,
                   ytok_done, st_done, state_done, acc_done, gate_done):
            SSM_PER[s_.name] = BLOCKS
        for s_ in (off_done, yoff_done, hbd_done):
            SSM_PER[s_.name] = BLOCKS - 1

        def later(b):
            return b + 1 if b == 0 else b

        def alone(eng):
            eng.sem_inc(nobody, 1)
        X_UNITS, X_SCALE = 3 * MEM_H, (HD / MEM_D) ** 0.5
        O_TOTAL = [2 * QT * KVH + X_UNITS, 2 * QT * KVH + 2 * X_UNITS]

        def prime(eng, name):
            for s in (seg_done, diag_done, off_done, acc_done, st_done, gsum_done, groot_done, gnorm_done, yoff_done,
                      decm_done, gate_done, state_done, ytok_done, hbd_done, h_stored):
                if s.name in PRIMED[name]:
                    eng.sem_inc(s, 1)

        block = ctx.enter_context(nc.Block())

        @block.scalar
        def _(act):
            loop, n = Loop(), Count()
            prime(act, "scalar")

            def split_hi(s):
                if s >= ALL_SLABS:
                    return
                act.wait_ge(raw_in[s % 2], at(loop, raw_in[s % 2], 16 * (s // 2 + 1)))
                if s >= 2:
                    act.wait_ge(slab_done, at(loop, slab_done, s - 1))
                act.activation(w_hi[:, s % 2], raw[:, s % 2], ACT.Copy).then_inc(hi_done, 1)

            def next_slab():
                split_hi(n.s + 2)
                n.s += 1

            def square(src, m, c, cols=None):
                if KT * c + m >= 2:
                    act.wait_ge(sq_used, at(loop, sq_used, KT * c + m - 1))
                dst = sq[:, m % 2, 0:cols] if cols else sq[:, m % 2]
                if len(src.shape) == 3:
                    dst = halves(dst)
                act.activation(dst, src, ACT.Square).then_inc(sq_ready, 1)

            def root(c, dst, psum):
                act.wait_ge(sq_used, KT * (c + 1))
                act.activation(dst, psum, ACT.Sqrt, bias=eps[:, 0:1], scale=1.0 / D_MODEL).then_inc(root_done, 1)

            def make_act(w, first=False):
                for m in range(KT):
                    if not first:
                        act.wait_ge(x_done, KT * n.x + m + 1)
                    act.activation(big_hi[:, KT + m], x[:, m], ACT.Copy, scale=par[:, w + m:w + m + 1]).then_inc(act_hi, 1)
                    square(x[:, m], m, n.c)
                if not first:
                    n.x += 1
                root(n.c, halves(rstd[:, 1]), ps[:, STAT_BANK:STAT_BANK + 2, 0:HALF])
                n.c += 1
                n.a += KT

            def post_root():
                root(n.c, halves(rstd[:, 0]), ps[:, STAT_BANK:STAT_BANK + 2, 0:HALF])
                n.c += 1

            act.wait_ge(zeroed, 1)
            act.wait_ge(const_in, 32)
            split_hi(0)
            split_hi(1)
            act.wait_ge(mem_arrived, 16)
            for layer in range(2):
                for m in range(KT):
                    if layer and m == 0:
                        act.wait_ge(slab_done, MEM_SLABS)
                    act.activation(m_hi[:, m], mraw[:, m], ACT.Copy,
                                   scale=par[:, C_MEM + KT * layer + m:C_MEM + KT * layer + m + 1]).then_inc(act_hi, 1)
                    if layer == 0:
                        square(mraw[:, m], m, 0, N_MEM)
                n.a += KT
                if layer == 0:
                    root(0, rm[:], ps[:, STAT_BANK, 0:N_MEM])
                    n.c += 1
                v_dst = vm1 if layer else vm0
                for k in range(MEM_SLABS):
                    next_slab()
                    if k >= MEM_H:
                        h = k - MEM_H
                        act.wait_ge(mv_used, MEM_H * layer + h + 1)
                        act.activation(v_dst[:, :, h * P:(h + 1) * P],
                                       ps[:, 4 + h % 2, 0:2 * P].rearrange("p (t d) -> p t d", t=2),
                                       ACT.Copy).then_inc(vm_done, 1)
                act.wait_ge(freed, MEM_SLABS * (layer + 1))
                act.dma_start(memk_out[layer], (kvm1 if layer else km0)[:]).then_inc(stored, 16)
                act.wait_ge(vm_done, MEM_H * (layer + 1))
                act.dma_start(memv_out[layer], v_dst[:]).then_inc(stored, 16)
                stores[0] += 2
            act.wait_ge(x_arrived, 16)
            make_act(C_MIX_PRE, first=True)

            n.g += 2 * MEM_SLABS + ATTN_SLABS
            for k in range(KV_SLABS):
                next_slab()
            for j in range(QT):
                next_slab()

            def exps(t):
                n_, j, u = n.n + t, t // UNITS_J, t % UNITS_J
                r = n_ % 4
                act.wait_ge(max_done, at(loop, max_done, n_ + 1))
                if u == 0:
                    parts = [(e, prob[0:DEC, r, e, 0:DEC + P]) for e in range(2)]
                    rows = DEC
                else:
                    e = (u - 1) // 2
                    parts = [(b, prob[:, r, b, P if u % 2 and b == 0 else 0:2 * P]) for b in range(2)]
                    rows = P
                for b, ap in parts:
                    act.activation(ap, ap, ACT.Exp, bias=stat[0:rows, r, 1, b:b + 1],
                                   accum_out=stat[0:rows, r, 2, b:b + 1])
                if u == 0:
                    for e in range(2):
                        ins = act.activation(stat[0:rows, r, 3, e:e + 1], stat[0:rows, r, 0, e:e + 1], ACT.Exp,
                                             scale=-1.0, bias=sink_cur[0:DEC, 2 * j + e:2 * j + e + 1])
                else:
                    ins = act.activation(stat[:, r, 3, :], stat[:, r, 0, :], ACT.Exp, scale=-1.0,
                                         bias=sink_cur[:, 2 * j + e:2 * j + e + 1])
                ins.then_inc(exp_done, 1)

            def copy_t(t):
                n_, u = n.n + t, t % UNITS_J
                act.wait_ge(t_done, at(loop, t_done, n_ + 1))
                if t >= 2:
                    act.wait_ge(v_done, at(loop, v_done, n_ - 1))
                if u == 0:
                    act.activation(p_t[:, n_ % 2, 0:2 * DEC], ps[:, T_BANK, 0:2 * DEC], ACT.Copy)
                    act.activation(p_t[0:DEC, n_ % 2, 2 * DEC:4 * DEC], ps[0:DEC, T_BANK, 2 * DEC:4 * DEC],
                                   ACT.Copy).then_inc(pt_done, 1)
                else:
                    w = 3 * P if u % 2 else 4 * P
                    act.activation(p_t[:, n_ % 2, 0:w], ps[:, T_BANK, 0:w], ACT.Copy).then_inc(pt_done, 1)

            loop.per = ATT_PER
            with act.Fori(0, KVH) as g:
                loop.i = g
                for kind, t in STEPS:
                    if kind == "S":
                        exps(t)
                    elif kind == "T":
                        copy_t(t)
                    elif kind == "K" and t % KT == KT - 1:
                        next_slab()
                loop.i = None
                n.s -= QT
            n.s += KVH * QT
            n.n += KVH * UNITS
            act.dma_start(swk_out[:, :, 0:DEC], k_all[0:HD, :, P:P + DEC]).then_inc(stored, 16)
            act.dma_start(swk_out[:, :, DEC:], k_all[0:HD, :, SPAN - P:]).then_inc(stored, 16)
            act.dma_start(swv_out[0:DEC], v_all[0:DEC, 1]).then_inc(stored, 16)
            act.dma_start(swv_out[DEC:], v_all[:, BLOCKS]).then_inc(stored, 16)
            stores[0] += 4

            def cross():
                def exps(c):
                    n_, u = n.n + c, c % 3
                    act.wait_ge(max_done, n_ + 1)
                    rows = P if u else DEC
                    for b in range(2 if u else 1):
                        ins = act.activation(prob[0:rows, n_ % 4, b], ps[0:rows, S_BANK + n_ % 2, b * N_MEM:(b + 1) * N_MEM],
                                             ACT.Exp, bias=stat[0:rows, n_ % 4, 1, b:b + 1], scale=X_SCALE,
                                             accum_out=stat[0:rows, n_ % 4, 2, b:b + 1])
                    ins.then_inc(exp_done, 1)

                def copy_t(c):
                    n_, w = n.n + c, 4 * P if c % 3 else 2 * DEC
                    act.wait_ge(t_done, n_ + 1)
                    act.wait_ge(v_done, n_ - 1)
                    act.activation(p_t[:, n_ % 2, 0:w], ps[:, T_BANK, 0:w], ACT.Copy).then_inc(pt_done, 1)

                for c in range(X_UNITS + LAG_T):
                    if c < X_UNITS:
                        exps(c)
                    if c >= LAG_T:
                        copy_t(c - LAG_T)
                n.n += X_UNITS
                n.j += X_UNITS

            def out_projection(layer):
                act.wait_ge(o_done, O_TOTAL[layer])
                act.wait_ge(stored, 16 * stores[0])
                for k in range(MIX_T):
                    w = norm_weight(layer, k)
                    scale = 1.0 if w is None else par[:, w:w + 1]
                    act.activation(big_hi[:, k], mix[:, k], ACT.Copy, scale=scale).then_inc(act_hi, 1)
                n.a += MIX_T

                def group(m, g):
                    for _ in range(2):
                        next_slab()
                    act.wait_ge(slab_done, at(loop, slab_done, n.s))
                    square(ps[:, 2 * (g % 2):2 * (g % 2) + 2, 0:HALF], m, n.c)

                for m in range(2):
                    group(m, n.g + m)
                loop.per = OUT_PER
                with act.Fori(0, KT // 2 - 1) as i:
                    loop.i = i
                    for m in range(2, 4):
                        group(m, n.g + m)
                    loop.i = None
                    n.s -= 4
                n.s += OUT_SLABS - 4
                n.g += KT
                post_root()

            def ffn():
                def up():
                    for m in range(KT):
                        next_slab()
                        n.g += 1
                        act.wait_ge(freed, at(loop, freed, n.g))
                        act.activation(big_hi[:, m], relu[:, m % 2], ACT.Square).then_inc(act_hi, 1)

                def down(last):
                    for m in range(KT):
                        next_slab()
                        n.g += 1
                        if last:
                            act.wait_ge(freed, n.g)
                            square(mix[:, m], m, n.c)

                up()
                loop.per = FF_PER
                with act.Fori(0, FF_CHUNKS - 1) as i:
                    loop.i = i
                    down(False)
                    up()
                    loop.i = None
                    n.s -= SLABS_FF
                    n.g -= SLABS_FF
                n.s += (FF_CHUNKS - 1) * SLABS_FF
                n.g += (FF_CHUNKS - 1) * SLABS_FF
                down(True)
                n.f += 1
                post_root()

            cross()
            out_projection(0)
            make_act(C_FF_PRE)
            ffn()
            make_act(C_MIX_PRE + KT)

            def slab_end(k, conv=True):
                next_slab()
                n.g += 1
                if not conv:
                    return
                if k:
                    tanh(k - 1)
                if k < UT:
                    act.wait_ge(freed, at(loop, freed, n.g))
                    if n.k:
                        act.wait_ge(tok_done, at(loop, tok_done, BLOCKS))
                        act.wait_ge(c_done, at(loop, c_done, 1))
                    act.activation(u[:, k], xp[:, k % 2, 0:UC], ACT.Identity, bias=cpar[:, k, CONV_W:CONV_W + 1],
                                   scale=cpar[:, k, 0:1]).then_inc(tap_done, 1)

            def tanh(k):
                if k < UT:
                    act.wait_ge(conv_done, at(loop, conv_done, n.k * 3 * UT + 3 * (k + 1)))
                if n.k or k:
                    act.wait_ge(u_done, at(loop, u_done, n.k * PAIR_SLABS + k))
                src, w = (u[:, k], UC) if k < UT else (zs[:, k - UT], TOK)
                act.activation(th[:, 0:w], src, ACT.Tanh).then_inc(tanh_done, 1)

            next_slab()
            n.g += 1
            for k in range(PAIR_SLABS):
                slab_end(k)
                if k == 0:
                    act.activation(ea[:], par[:, C_ALOG:C_ALOG + HEADS], ACT.Exp).then_inc(dt_fn, 1)
                    act.wait_ge(dt_step, 2)
                    act.activation(dts[:, 1], dts[:, 1], ACT.Exp).then_inc(dt_fn, 1)
                elif k == 1:
                    act.wait_ge(dt_step, 4)
                    act.activation(dts[:, 3], dts[:, 2], ACT.Ln).then_inc(dt_fn, 1)
                elif k == 2:
                    act.wait_ge(dt_moved, 2)
                    for m in range(3):
                        ins = act.activation(hs[:, 2 + m], ps[:, 4 + m, 0:BLOCKS * HEADS].rearrange("p (b h) -> p b h", b=BLOCKS),
                                             ACT.Exp)
                    ins.then_inc(dt_fn, 1)
            tanh(PAIR_SLABS - 1)

            def turn(eighths):
                for kind, b in ssd_steps(eighths):
                    rows = DEC if b == 0 else P
                    if kind == "K":
                        if b % KT == KT - 1:
                            slab_end(b // KT, eighths > CQ_SLABS * KT)
                    elif kind == "A":
                        act.wait_ge(tok_done, at(loop, tok_done, b + 1))
                        if b == 0:
                            act.wait_ge(gsum_done, at(loop, gsum_done, 0))
                            act.wait_ge(off_done, at(loop, off_done, 0))
                        act.activation(xtok[0:rows, b], ps[0:rows, 4 + 2 * (b % 2), 0:XT * P], ACT.Copy).then_inc(xtok_done, 1)
                        if b < 2:
                            ins = act.activation(c_cur[:, b], u[:, XT + 2 + b], ACT.Copy)
                            if b:
                                ins.then_inc(c_done, 1)
                    elif kind == "seg":
                        act.wait_ge(seg_done, at(loop, seg_done, b + 1))
                        act.wait_ge(diag_done, at(loop, diag_done, b))
                        if b == 0:
                            act.wait_ge(gnorm_done, at(loop, gnorm_done, 0))
                        for m in range(2):
                            ins = act.activation(dec[0:rows, 3 * m:3 * m + 3, 0:rows],
                                                 ps[0:rows, 4 + m, 0:3 * rows].rearrange("p (h q) -> p h q", h=3), ACT.Exp)
                        ins.then_inc(dec_done, 1)
                    elif kind == "Q":
                        act.wait_ge(gate_done, at(loop, gate_done, BLOCKS))
                        for m in range(XT):
                            ins = act.activation(gsq[:, m], mix[:, YG + m], ACT.Square)
                        ins.then_inc(gsq_done, 1)
                    elif kind == "G":
                        act.wait_ge(gsum_done, at(loop, gsum_done, 1))
                        act.activation(grs[:].rearrange("p g (h c) -> p (g h) c", h=2), ps[:, 4:8, 0:HALF], ACT.Sqrt,
                                       bias=eps[:, 0:1], scale=SGROUPS / INNER).then_inc(groot_done, 1)
                if eighths > CQ_SLABS * KT:
                    tanh(PAIR_SLABS - 1)

            loop.per = SSM_PER
            n.k = 1
            with act.Fori(0, PAIRS - 1) as i:
                loop.i = i
                turn(PAIR_SLABS * KT)
                loop.i = None
                n.s -= PAIR_SLABS
                n.g -= PAIR_SLABS
            loop.i = PAIRS - 1
            turn(CQ_SLABS * KT)
            loop.i = None
            n.s += (PAIRS - 1) * PAIR_SLABS
            n.g += (PAIRS - 1) * PAIR_SLABS
            cross()
            act.wait_ge(h_stored, at(loop, h_stored, 16 * (PAIRS + 1)))
            out_projection(1)
            make_act(C_FF_PRE + KT)
            ffn()


        @block.tensor
        def _(pe):
            loop, n = Loop(), Count()
            prime(pe, "tensor")

            def stats(m, c, cols=TOK):
                if m == 0 and c > 0:
                    pe.wait_ge(root_done, c)
                pe.wait_ge(sq_ready, at(loop, sq_ready, KT * c + m + 1))
                for h in range(2 if cols == TOK else 1):
                    w = HALF if cols == TOK else cols
                    ins = pe.matmul(ps[:, STAT_BANK + h, 0:w], mats[:, 1], sq[:, m % 2, h * w:(h + 1) * w],
                                    start=(m == 0), stop=(m == KT - 1), skip_group_check=True)
                ins.then_inc(sq_used, 1)

            def begin(s, g, first=True):
                pe.wait_ge(lo_done, at(loop, lo_done, s + 1))
                if first and g >= 2:
                    pe.wait_ge(freed, at(loop, freed, g - 1))

            def eighth(s, g, kt, hi, lo, k0=0, cols=TOK, start=True, stop=True):
                spans = [(0, HALF), (HALF, TOK)] if cols == TOK else [(0, cols)]
                for w, a in ((w_hi, hi), (w_hi, lo), (w_lo, hi)):
                    for h, (lo_c, hi_c) in enumerate(spans):
                        ins = pe.matmul(ps[:, 2 * (g % 2) + h, 0:hi_c - lo_c], w[:, s % 2, kt],
                                        a[:, k0 + kt, lo_c:hi_c],
                                        start=(start and kt == 0 and w is w_hi and a is hi),
                                        stop=(stop and kt == KT - 1 and w is w_lo), skip_group_check=True)
                if kt == KT - 1:
                    ins.then_inc(slab_done, 1)

            def projection(k0=KT, hi=big_hi, lo=big_lo, cols=TOK, fresh=False, each=None):
                begin(n.s, n.g)
                for kt in range(KT):
                    if fresh:
                        pe.wait_ge(act_ready, n.a + kt + 1)
                    eighth(n.s, n.g, kt, hi, lo, k0, cols)
                    if each:
                        each(kt)
                n.s += 1
                n.g += 1
                if fresh:
                    n.a += KT

            def first_projection(own=False):
                def each(kt):
                    if kt:
                        stats(kt - 1, n.c)
                projection(fresh=True, each=each)
                stats(KT - 1, n.c)
                n.c += 1

            def memory_v(layer, h):
                pe.wait_ge(freed, MEM_SLABS * layer + MEM_H + h + 1)
                if MEM_H * layer + h >= 2:
                    pe.wait_ge(vm_done, MEM_H * layer + h - 1)
                for t in range(2):
                    ins = pe.transpose(ps[:, 4 + h % 2, t * P:(t + 1) * P], mv_t[:, h % 2, t * P:(t + 1) * P], mats[:, 0])
                ins.then_inc(mv_used, 1)

            pe.wait_ge(const_in, 32)
            for layer in range(2):
                if layer == 0:
                    def each(kt):
                        if kt:
                            stats(kt - 1, 0, N_MEM)
                    projection(0, m_hi, m_lo, N_MEM, fresh=True, each=each)
                    stats(KT - 1, 0, N_MEM)
                    n.c += 1
                else:
                    projection(0, m_hi, m_lo, N_MEM, fresh=True)
                for k in range(1, MEM_SLABS):
                    projection(0, m_hi, m_lo, N_MEM)
                    if k > MEM_H:
                        memory_v(layer, k - MEM_H - 1)
                memory_v(layer, MEM_H - 1)

            first_projection()
            for k in range(KV_SLABS - 1):
                projection()
            for b in range(BLOCKS):
                pe.wait_ge(freed, n.g)
                if b >= 2:
                    pe.wait_ge(va_done, b - 1)
                c0, c1 = block_cols(b)
                for k in range(2):
                    ins = pe.transpose(ps[0:c1 - c0, S_BANK + b % 2, k * P:(k + 1) * P], v_t[:, k, c0:c1], mats[:, 0])
                ins.then_inc(vt_done, 1)
            for j in range(QT):
                projection()
            g_q = n.g - QT

            def scores(t):
                n_, j, u = n.n + t, t // UNITS_J, t % UNITS_J
                if t == 0:
                    pe.wait_ge(cur_ready, at(loop, cur_ready, 1))
                if u == 0:
                    pe.wait_ge(freed, at(loop, freed, g_q + j + 1))
                if t >= 2:
                    pe.wait_ge(biased, at(loop, biased, n_ - 1))
                bank = S_BANK + t % 2
                if u == 0:
                    alone(pe)
                    for e in range(2):
                        if e:
                            pe.wait_ge(s_half, at(loop, s_half, j + 1))
                            alone(pe)
                        ins = pe.matmul(ps[0:DEC, bank, e * 2 * P:e * 2 * P + P + DEC], q_t[e * HD:(e + 1) * HD, j, 0:DEC],
                                        k_cur[e * HD:(e + 1) * HD, 0:P + DEC], start=True, stop=True)
                        if e == 0:
                            ins.then_inc(s_half, 1)
                else:
                    e = (u - 1) // 2
                    for b in range(2):
                        i = 2 * ((u - 1) % 2) + b
                        keys = (DEC + i * P, DEC + (i + 2) * P)
                        c = 0
                        if i == 0:
                            keys, c = (P + DEC, P + DEC + P), P
                        ins = pe.matmul(ps[:, bank, b * 2 * P + c:(b + 1) * 2 * P],
                                        q_t[e * HD:(e + 1) * HD, j, DEC + i * P:DEC + (i + 1) * P],
                                        k_cur[e * HD:(e + 1) * HD, keys[0]:keys[1]], start=True, stop=True)
                ins.then_inc(s_done, 1)

            def transposes(t):
                n_, u = n.n + t, t % UNITS_J
                pe.wait_ge(normed, at(loop, normed, n_ + 1))
                if t >= 1:
                    pe.wait_ge(pt_done, at(loop, pt_done, n_))
                r = n_ % 4
                if u == 0:
                    alone(pe)
                    for e in range(2):
                        pe.transpose(ps[:, T_BANK, e * DEC:(e + 1) * DEC], prob[0:DEC, r, e, 0:P], mats[0:DEC, 0, 0:DEC])
                    for e in range(2):
                        ins = pe.transpose(ps[0:DEC, T_BANK, (2 + e) * DEC:(3 + e) * DEC], prob[0:DEC, r, e, P:P + DEC],
                                           mats[0:DEC, 0, 0:DEC])
                else:
                    tiles = [(0, 1), (1, 0), (1, 1)] if u % 2 else [(0, 0), (0, 1), (1, 0), (1, 1)]
                    for k, (b, key) in enumerate(tiles):
                        ins = pe.transpose(ps[:, T_BANK, k * P:(k + 1) * P], prob[:, r, b, key * P:(key + 1) * P], mats[:, 0])
                ins.then_inc(t_done, 1)

            def values(t):
                n_, j, u = n.n + t, t // UNITS_J, t % UNITS_J
                pe.wait_ge(pt_done, at(loop, pt_done, n_ + 1))
                r = n_ % 2
                if u == 0:
                    if t:
                        pe.wait_ge(o_done, at(loop, o_done, n.j + 2 * j))
                    for e in range(2):
                        o = ps[e * HD:(e + 1) * HD, O_BANK, 0:DEC]
                        pe.matmul(o, v_cur[:, 0], p_t[:, r, e * DEC:(e + 1) * DEC], start=True, stop=False)
                        ins = pe.matmul(o, v_cur[0:DEC, 1], p_t[0:DEC, r, (2 + e) * DEC:(3 + e) * DEC], start=False, stop=True)
                else:
                    if u == 1:
                        pe.wait_ge(o_done, at(loop, o_done, n.j + 2 * j + 1))
                    e = (u - 1) // 2
                    o = ps[e * HD:(e + 1) * HD, O_BANK, :]
                    def product(v, a, b, p0, start):
                        return pe.matmul(o[:, a:b], v_cur[:, 2 + v], p_t[:, r, p0:p0 + b - a], start=start, stop=True,
                                         skip_group_check=True)
                    if u % 2:
                        product(0, 0, 2 * P, 0, True)
                        ins = product(1, P, 2 * P, 2 * P, False)
                    else:
                        product(1, 2 * P, 3 * P, 0, True)
                        product(2, 2 * P, 4 * P, P, False)
                        ins = product(3, 3 * P, 4 * P, 3 * P, False)
                ins.then_inc(v_done, 1)

            loop.per = ATT_PER
            with pe.Fori(0, KVH) as g:
                loop.i = g
                for kind, t in STEPS:
                    if kind == "S":
                        scores(t)
                    elif kind == "T":
                        transposes(t)
                    elif kind == "V":
                        values(t)
                    else:
                        if t % KT == 0:
                            begin(n.s + t // KT, n.g + t // KT)
                        eighth(n.s + t // KT, n.g + t // KT, t % KT, big_hi, big_lo, KT)
                loop.i = None
            n.s += KVH * QT
            n.g += KVH * QT
            n.n += KVH * UNITS
            n.j += 2 * KVH * QT

            def cross(q_src, km, vm, kms, vms):
                def scores(c):
                    n_, h, u = n.n + c, c // 3, c % 3
                    pe.wait_ge(exp_done, n_ - 1)
                    keys = km if u else kms
                    for b in range(2 if u else 1):
                        c0, c1 = block_cols(0 if u == 0 else 2 * u - 1 + b)
                        ins = pe.matmul(ps[0:c1 - c0, S_BANK + n_ % 2, b * N_MEM:(b + 1) * N_MEM], q_src[:, h, c0:c1],
                                        keys[:, h], start=True, stop=True)
                    ins.then_inc(s_done, 1)

                def transposes(c):
                    n_, u = n.n + c, c % 3
                    pe.wait_ge(normed, n_ + 1)
                    pe.wait_ge(pt_done, n_)
                    w = P if u else DEC
                    for key in range(2):
                        for b in range(2 if u else 1):
                            k = key * (2 if u else 1) + b
                            ins = pe.transpose(ps[:, T_BANK, k * w:(k + 1) * w], prob[0:w, n_ % 4, b, key * P:(key + 1) * P],
                                               mats[0:w, 0, 0:w])
                    ins.then_inc(t_done, 1)

                def values(c):
                    n_, h, u = n.n + c, c // 3, c % 3
                    pe.wait_ge(pt_done, n_ + 1)
                    pe.wait_ge(o_done, n.j + c)
                    w = 2 * P if u else DEC
                    v = vm if u else vms
                    for key in range(2):
                        ins = pe.matmul(ps[:, O_BANK, 0:w], v[:, key, h * P:(h + 1) * P],
                                        p_t[:, n_ % 2, key * w:(key + 1) * w], start=(key == 0), stop=(key == 1))
                    ins.then_inc(v_done, 1)

                pe.wait_ge(kms_in, 32 * (n.f + 1))
                pe.wait_ge(freed, n.g)
                for c in range(X_UNITS + LAG_PV):
                    if c < X_UNITS:
                        scores(c)
                    if 0 <= c - LAG_T < X_UNITS:
                        transposes(c - LAG_T)
                    if c >= LAG_PV:
                        values(c - LAG_PV)
                n.n += X_UNITS
                n.j += X_UNITS

            def out_projection():
                def group(m, s, g, fresh=False):
                    for part in range(2):
                        begin(s + part, g, first=(part == 0))
                        for kt in range(KT):
                            if fresh:
                                pe.wait_ge(act_ready, n.a + KT * part + kt + 1)
                            eighth(s + part, g, kt, big_hi, big_lo, KT * part, start=(part == 0), stop=(part == 1))

                group(0, n.s, n.g, fresh=True)
                n.a += MIX_T
                group(1, n.s + 2, n.g + 1)
                stats(0, n.c)
                loop.per = OUT_PER
                with pe.Fori(0, KT // 2 - 1) as i:
                    loop.i = i
                    for m in range(2, 4):
                        group(m, n.s + 2 * m, n.g + m)
                        stats(m - 1, n.c)
                    loop.i = None
                n.s += OUT_SLABS
                n.g += KT
                stats(KT - 1, n.c)
                n.c += 1

            def ffn():
                def up(fresh=False):
                    for m in range(KT):
                        if m == 0 and fresh:
                            first_projection()
                        else:
                            projection()

                def down(a, last=False):
                    for m in range(KT):
                        begin(n.s, n.g)
                        for kt in range(KT):
                            if m == 0:
                                pe.wait_ge(act_ready, at(loop, act_ready, a + kt + 1))
                            eighth(n.s, n.g, kt, big_hi, big_lo, 0)
                        n.s += 1
                        n.g += 1
                        if last and m:
                            stats(m - 1, n.c)
                    if last:
                        stats(KT - 1, n.c)
                        n.c += 1

                up(fresh=True)
                loop.per = FF_PER
                with pe.Fori(0, FF_CHUNKS - 1) as i:
                    loop.i = i
                    down(n.a)
                    up()
                    loop.i = None
                    n.s -= SLABS_FF
                    n.g -= SLABS_FF
                n.s += (FF_CHUNKS - 1) * SLABS_FF
                n.g += (FF_CHUNKS - 1) * SLABS_FF
                n.a += (FF_CHUNKS - 1) * KT
                down(n.a, last=True)
                n.a += KT

            cross(q_t, km0, vm0, kms, vms)
            n.f += 1
            out_projection()
            ffn()

            first_projection()
            for k in range(PAIR_SLABS):
                projection()
                if k == 0:
                    pe.wait_ge(freed, n.g - 1)
                    for b in range(BLOCKS):
                        c0 = block_cols(b)[0]
                        ins = pe.transpose(ps[:, 4, b * 32:(b + 1) * 32], th[0:32, c0:c0 + P], mats[0:32, 0, 0:32])
                    ins.then_inc(dt_moved, 1)
                elif k == 2:
                    pe.wait_ge(dt_step, 8)
                    for m, mat in enumerate((2, 3, 1)):
                        pe.matmul(ps[:, 4 + m, 0:HEADS], mats[0:DEC, mat], hs[0:DEC, 1, 0], start=True, stop=True)
                        ins = pe.matmul(ps[:, 4 + m, HEADS:BLOCKS * HEADS], mats[:, mat],
                                        hs[:, 1, 1:].rearrange("p b h -> p (b h)"), start=True, stop=True)
                    ins.then_inc(dt_moved, 1)

            def turn(eighths):
                for kind, b in ssd_steps(eighths):
                    rows = DEC if b == 0 else P
                    c0, c1 = conv_cols(b) if kind not in "KGQN" else (0, 0)
                    if kind == "K":
                        if b % KT == 0:
                            begin(n.s + b // KT, n.g + b // KT)
                        eighth(n.s + b // KT, n.g + b // KT, b % KT, big_hi, big_lo, KT)
                    elif kind == "A":
                        if b == 0:
                            pe.wait_ge(u_done, at(loop, u_done, UT))
                            pe.wait_ge(groot_done, at(loop, groot_done, 0))
                        if b >= 2:
                            pe.wait_ge(xtok_done, at(loop, xtok_done, b - 1))
                            pe.wait_ge(cbm_done, at(loop, cbm_done, b - 1))
                        alone(pe)
                        bank = 4 + 2 * (b % 2)
                        for m in range(XT):
                            pe.transpose(ps[0:rows, bank, m * P:(m + 1) * P], u[:, m, c0:c1], mats[:, 0])
                        for m in range(2):
                            pe.transpose(ps[0:rows, bank + 1, m * P:(m + 1) * P], u[:, XT + m, c0:c1], mats[:, 0])
                        for m in range(2):
                            ins = pe.matmul(ps[0:rows, bank + 1, 2 * P + m * rows:2 * P + (m + 1) * rows], u[:, XT + m, c0:c1],
                                            u[:, XT + 2 + m, c0:c1], start=True, stop=True)
                        ins.then_inc(tok_done, 1)
                    elif kind == "seg":
                        pe.wait_ge(wseg_done, at(loop, wseg_done, b + 1))
                        if b == 0:
                            pe.wait_ge(xtok_done, at(loop, xtok_done, BLOCKS))
                            pe.wait_ge(cbm_done, at(loop, cbm_done, BLOCKS))
                        else:
                            pe.wait_ge(dec_done, at(loop, dec_done, b))
                            pe.wait_ge(state_done, at(loop, state_done, b))
                        alone(pe)
                        for m in range(2):
                            ins = pe.matmul(ps[0:rows, 4 + m, 0:3 * rows], mats[0:rows, 3, 0:rows],
                                            wseg[0:rows, 3 * m:3 * m + 3, 0:rows], start=True, stop=True)
                        ins.then_inc(seg_done, 1)
                    elif kind == "off" and b != 1:
                        if b == 0:
                            pe.wait_ge(h_loaded, at(loop, h_loaded, 16))
                            pe.wait_ge(c_done, at(loop, c_done, 1))
                        else:
                            pe.wait_ge(state_done, at(loop, state_done, b))
                        pe.wait_ge(yoff_done, at(loop, yoff_done, later(b) - 1))
                        alone(pe)
                        h = h_next if b == 0 else state[:, 1]
                        for m in range(2):
                            ins = pe.matmul(ps[0:rows, 7, m * 192:(m + 1) * 192], c_cur[:, m, c0:c1],
                                            h[:, m * 192:(m + 1) * 192], start=True, stop=True)
                        ins.then_inc(off_done, 1)
                    elif kind == "st":
                        pe.wait_ge(dec_done, at(loop, dec_done, b + 1))
                        pe.wait_ge(xd_done, at(loop, xd_done, b + 1))
                        alone(pe)
                        for m in range(2):
                            ins = pe.matmul(ps[:, 4, m * 192:(m + 1) * 192], btok[0:rows, b, m], xd[0:rows, 1, 3 * m:3 * m + 3],
                                            start=True, stop=True)
                        ins.then_inc(st_done, 1)
                    elif kind == "diag":
                        pe.wait_ge(decm_done, at(loop, decm_done, b + 1))
                        pe.wait_ge(gate_done, at(loop, gate_done, b))
                        alone(pe)
                        for h in range(PH):
                            ins = pe.matmul(ps[h % 2 * HD:(h % 2 + 1) * HD, 6, h // 2 * rows:(h // 2 + 1) * rows],
                                            xd[0:rows, 0, h], dec[0:rows, h, 0:rows], start=(h < 2), stop=False,
                                            skip_group_check=True)
                        ins.then_inc(diag_done, 1)
                    elif kind == "acc":
                        pe.wait_ge(ytok_done, at(loop, ytok_done, b + 1))
                        alone(pe)
                        for m in range(XT):
                            ins = pe.matmul(ps[:, 6, m * rows:(m + 1) * rows], ytok[0:rows, m * P:(m + 1) * P],
                                            mats[0:rows, 0, 0:rows], start=False, stop=True, skip_group_check=True)
                        ins.then_inc(acc_done, 1)
                    elif kind == "G":
                        pe.wait_ge(gsq_done, at(loop, gsq_done, 1))
                        pe.wait_ge(state_done, at(loop, state_done, BLOCKS))
                        for m in range(2):
                            for h in range(2):
                                c0, c1 = h * HALF, (h + 1) * HALF
                                o = ps[:, 4 + 2 * m + h, 0:HALF]
                                r0 = m * HD
                                alone(pe)
                                pe.matmul(o, mats[:, 1], gsq[:, 2 * m, c0:c1], start=True, stop=False)
                                ins = pe.matmul(o, mats[r0:r0 + HD, 1], gsq[r0:r0 + HD, 1, c0:c1], start=False, stop=True)
                        ins.then_inc(gsum_done, 1)

            loop.per = SSM_PER
            with pe.Fori(0, PAIRS - 1) as i:
                loop.i = i
                turn(PAIR_SLABS * KT)
                loop.i = None
            loop.i = PAIRS - 1
            turn(CQ_SLABS * KT)
            loop.i = None
            n.s += (PAIRS - 1) * PAIR_SLABS + CQ_SLABS
            n.g += (PAIRS - 1) * PAIR_SLABS + CQ_SLABS
            pe.wait_ge(groot_done, at(loop, groot_done, PAIRS))
            cross(mix[:, MIX_T - MEM_H:], kvm1, vm1, kms1, vms1)
            out_projection()
            ffn()


        @block.vector
        def _(dve):
            loop, n = Loop(), Count()
            prime(dve, "vector")
            own = Own(dve, dve_self)

            def rest(dst, src, hi, w=None):
                dve.wait_ge(act_hi, at(loop, act_hi, n.a + 1))
                n.a += 1
                if w is None:
                    ins = dve.tensor_tensor(dst, src, hi.bitcast(F32), ALU.subtract)
                else:
                    ins = dve.scalar_tensor_tensor(out=dst, in0=src, scalar=par[:, w:w + 1], in1=hi.bitcast(F32),
                                                   op0=ALU.mult, op1=ALU.subtract)
                ins.then_inc(act_ready, 1)

            def reciprocal(ap):
                n.c += 1
                dve.wait_ge(root_done, n.c)
                dve.reciprocal(ap, ap).then_inc(rstd_ready, 1)
                dve.wait_ge(rstd_ready, n.c)

            def group(slabs_=1):
                n.s += slabs_
                dve.wait_ge(slab_done, at(loop, slab_done, n.s))
                b = 2 * (n.g % 2)
                n.g += 1
                return ps[:, b:b + 2, 0:HALF]

            def copy(dst, src):
                return dve.tensor_scalar(dst, src, 1.0, None, ALU.mult)

            def make_act(w, post=None):
                for m in range(KT + 1):
                    if post is not None and m < KT:
                        dve.scalar_tensor_tensor(out=mix[:, m], in0=mix[:, m], scalar=par[:, post + m:post + m + 1],
                                                 in1=rstd[:, 0], op0=ALU.mult, op1=ALU.mult).then_inc(scaled, 1)
                    if m and w is not None:
                        rest(big_lo[:, KT + m - 1], x[:, m - 1], big_hi[:, KT + m - 1], w + m - 1)
                if w is not None:
                    reciprocal(rstd[:, 1])

            dve.wait_ge(const_in, 32)
            dve.wait_ge(mem_arrived, 16)
            for layer in range(2):
                for m in range(KT):
                    rest(m_lo[:, m], mraw[:, m], m_hi[:, m], C_MEM + KT * layer + m)
                if layer == 0:
                    reciprocal(rm[:])
                for k in range(MEM_SLABS):
                    src = group()[:, 0, 0:N_MEM]
                    h = k - MEM_H
                    if k < MEM_H:
                        dst = (kvm1 if layer else km0)[:, k]
                    else:
                        dst = mv_t[:, h % 2]
                        if MEM_H * layer + h >= 2:
                            dve.wait_ge(mv_used, MEM_H * layer + h - 1)
                    dve.tensor_tensor(dst, src, rm[:], ALU.mult).then_inc(freed, 1)
            dve.wait_ge(x_arrived, 16)
            make_act(C_MIX_PRE)

            for k in range(KVH):
                c0 = P
                b = group()
                dve.tensor_tensor(k_all[:, k, P:P + HALF], b[:, 0], rstd[:, 1, 0:HALF], ALU.mult)
                dve.tensor_tensor(k_all[:, k, P + HALF:], b[:, 1], rstd[:, 1, HALF:], ALU.mult).then_inc(freed, 1)
            for k in range(2):
                dve.tensor_tensor(halves(v_t[:, k]), group(), halves(rstd[:, 1]), ALU.mult).then_inc(freed, 1)
            for b in range(BLOCKS):
                dve.wait_ge(vt_done, b + 1)
                rows = DEC if b == 0 else P
                src = ps[0:rows, S_BANK + b % 2, :]
                dve.tensor_copy(v_all[0:rows, 1 + b, 0:2, :], src[:, 0:P].rearrange("p (h d) -> p h d", h=2))
                dve.tensor_copy(v_all[0:rows, 1 + b, 2, :], src[:, P + HD:2 * P]).then_inc(va_done, 1)

            def query_tile(j, dst):
                dve.scalar_tensor_tensor(out=halves(dst), in0=group(), scalar=float(HD) ** -0.5,
                                         in1=halves(rstd[:, 1]), op0=ALU.mult, op1=ALU.mult).then_inc(freed, 1)

            for j in range(QT):
                query_tile(j, q_t[:, j])
            dve.wait_ge(cache_in, 32)

            def bias_max(t):
                n_, j, u = n.n + t, t // UNITS_J, t % UNITS_J
                r, bank = n_ % 4, S_BANK + t % 2
                dve.wait_ge(s_done, at(loop, s_done, n_ + 1))
                if u == 0:
                    dve.wait_ge(bias_in[j % 2], at(loop, bias_in[j % 2], 16 * (j // 2 + 1)))
                if t >= 4:
                    dve.wait_ge(t_done, at(loop, t_done, n_ - 3))
                alone(dve)
                for b in range(2):
                    if u == 0:
                        rows, e, c0, c1 = DEC, b, 0, P + DEC
                    else:
                        rows, e, c0, c1 = P, (u - 1) // 2, P if u % 2 and b == 0 else 0, 2 * P
                    ins = dve.tensor_tensor_reduce(prob[0:rows, r, b, c0:c1], ps[0:rows, bank, b * 2 * P + c0:b * 2 * P + c1],
                                                   bias[0:rows, j % 2, e, c0:c1], 1.0,
                                                   sink_cur[0:rows, 2 * j + e:2 * j + e + 1], ALU.add, ALU.max,
                                                   stat[0:rows, r, 0, b:b + 1])
                ins.then_inc(biased, 1)
                rows = P if u else DEC
                dve.wait_ge(biased, at(loop, biased, n_ + 1))
                dve.tensor_scalar(stat[0:rows, r, 1, :], stat[0:rows, r, 0, :], -1.0, None, ALU.mult).then_inc(max_done, 1)

            def normalise(n_, rows, parts, sink=True, sums=2):
                r = n_ % 4
                dve.wait_ge(exp_done, at(loop, exp_done, n_ + 1))
                total = stat[0:rows, r, 2, 0:sums]
                if sink:
                    own.mark(dve.tensor_tensor(total, total, stat[0:rows, r, 3, 0:sums], ALU.add))
                    own.wait(loop)
                own.mark(dve.reciprocal(total, total))
                own.wait(loop)
                for b, c0, c1 in parts:
                    ap = prob[0:rows, r, b, c0:c1]
                    ins = dve.tensor_scalar(ap, ap, stat[0:rows, r, 2, b:b + 1], None, ALU.mult)
                ins.then_inc(normed, 1)

            def norm(t):
                u = t % UNITS_J
                if u == 0:
                    normalise(n.n + t, DEC, [(0, 0, P + DEC), (1, 0, P + DEC)])
                else:
                    normalise(n.n + t, P, [(0, P if u % 2 else 0, 2 * P), (1, 0, 2 * P)])

            ATT_PER["dve_self"] = 2 * UNITS
            loop.per = ATT_PER
            with dve.Fori(0, KVH) as g:
                loop.i = g
                k_g = k_all[:, bass.ds(g, 1), :].rearrange("p h c -> p (h c)")
                v_g = v_all[:, :, bass.ds(g, 1), :].rearrange("p b h d -> p b (h d)")
                copy(k_cur[:], k_g)
                copy(v_cur[:, 0], v_g[:, 0])
                copy(v_cur[0:DEC, 1], v_g[0:DEC, 1])
                copy(v_cur[:, 2:], v_g[:, 2:])
                copy(sink_cur[:], par[:, bass.ds(g * GROUP + C_SINK, GROUP)]).then_inc(cur_ready, 1)
                dve.wait_ge(cur_ready, at(loop, cur_ready, 1))
                start = own.n
                for kind, t in STEPS:
                    if kind == "S":
                        bias_max(t)
                        if t:
                            norm(t - 1)
                    elif kind == "T" and t == UNITS - LAG_T:
                        norm(UNITS - 1)
                    elif kind == "K" and t % KT == KT - 1:
                        query_tile(t // KT, q_t[:, t // KT])
                    elif kind == "V" and t % UNITS_J in (0, UNITS_J - 1):
                        dve.wait_ge(v_done, at(loop, v_done, n.n + t + 1))
                        c0, c1 = (0, DEC) if t % UNITS_J == 0 else (DEC, TOK)
                        dst = mix[:, bass.ds(g * QT + t // UNITS_J, 1), c0:c1].rearrange("p t c -> p (t c)")
                        copy(dst, ps[:, O_BANK, 0:c1 - c0]).then_inc(o_done, 1)
                loop.i = None
                assert own.n - start == ATT_PER["dve_self"]
                n.s -= QT
                n.g -= QT
            own.n += (KVH - 1) * ATT_PER["dve_self"]
            n.s += KVH * QT
            n.g += KVH * QT
            n.n += KVH * UNITS
            for i in range(2):
                dve.wait_ge(bias_in[i], 16 * (KVH * QT // 2 + 1))

            def cross():
                def maximum(c):
                    n_, u = n.n + c, c % 3
                    rows, r, blocks = P if u else DEC, n_ % 4, 2 if u else 1
                    dve.wait_ge(s_done, n_ + 1)
                    own.mark(dve.tensor_reduce(stat[0:rows, r, 0, 0:blocks],
                                               ps[0:rows, S_BANK + n_ % 2, 0:blocks * N_MEM].rearrange("p (b c) -> p b c", b=blocks),
                                               AX.X, ALU.max))
                    own.wait(loop)
                    dve.tensor_scalar(stat[0:rows, r, 1, 0:blocks], stat[0:rows, r, 0, 0:blocks], -X_SCALE, None,
                                      ALU.mult).then_inc(max_done, 1)

                for c in range(X_UNITS + LAG_PV + 1):
                    if c < X_UNITS:
                        maximum(c)
                    if 1 <= c <= X_UNITS:
                        u = (c - 1) % 3
                        normalise(n.n + c - 1, P if u else DEC, [(b, 0, 2 * P) for b in range(2 if u else 1)], False,
                                  2 if u else 1)
                    if c > LAG_PV:
                        k = c - LAG_PV - 1
                        h, u = k // 3, k % 3
                        dve.wait_ge(v_done, n.n + k + 1)
                        c0, c1 = (0, DEC) if u == 0 else (DEC + (u - 1) * 2 * P, DEC + u * 2 * P)
                        dve.tensor_copy(mix[:, MIX_T - MEM_H + h, c0:c1], ps[:, O_BANK, 0:c1 - c0]).then_inc(o_done, 1)
                n.n += X_UNITS

            def out_projection(layer):
                for k in range(MIX_T):
                    rest(big_lo[:, k], mix[:, k], big_hi[:, k], norm_weight(layer, k))

                def one(m, dst):
                    src = group(2)
                    dve.wait_ge(sq_ready, at(loop, sq_ready, KT * n.c + m + 1))
                    copy(halves(dst), src).then_inc(freed, 1)

                for m in range(2):
                    one(m, mix[:, m])
                loop.per = OUT_PER
                with dve.Fori(0, KT // 2 - 1) as i:
                    loop.i = i
                    for m in range(2, 4):
                        one(m, mix[:, bass.ds(i * 2 + m, 1), :].rearrange("p t c -> p (t c)"))
                    loop.i = None
                    n.s -= 4
                    n.g -= 2
                n.s += OUT_SLABS - 4
                n.g += KT - 2
                reciprocal(rstd[:, 0])

            def ffn():
                def up():
                    for m in range(KT + 1):
                        if m < KT:
                            src = group()
                            if m >= 2:
                                dve.wait_ge(hid_done, at(loop, hid_done, n.x + m - 1))
                                dve.wait_ge(act_hi, at(loop, act_hi, n.a - (1 if m else 0)))
                            dve.scalar_tensor_tensor(out=halves(relu[:, m % 2]), in0=src, scalar=0.0,
                                                     in1=halves(rstd[:, 1]), op0=ALU.max, op1=ALU.mult).then_inc(freed, 1)
                        if m:
                            dve.wait_ge(hid_done, at(loop, hid_done, n.x + m))
                            rest(big_lo[:, m - 1], hid[:, (m - 1) % 2], big_hi[:, m - 1])

                def down():
                    for m in range(KT):
                        src = group()
                        if m == 0:
                            dve.wait_ge(zeroed, 1 + KT * (n.f + 1))
                        dve.wait_ge(freed, at(loop, freed, n.g - 1))
                        dve.tensor_tensor(halves(mix[:, m]), src, halves(mix[:, m]), ALU.add).then_inc(freed, 1)

                up()
                n.x += KT
                loop.per = FF_PER
                with dve.Fori(0, FF_CHUNKS - 1) as i:
                    loop.i = i
                    down()
                    up()
                    loop.i = None
                    n.s -= SLABS_FF
                    n.g -= SLABS_FF
                    n.a -= KT
                n.s += (FF_CHUNKS - 1) * SLABS_FF
                n.g += (FF_CHUNKS - 1) * SLABS_FF
                n.a += (FF_CHUNKS - 1) * KT
                n.x += (FF_CHUNKS - 1) * KT
                down()
                n.f += 1
                reciprocal(rstd[:, 0])

            cross()
            out_projection(0)
            make_act(C_FF_PRE, C_MIX_POST)
            ffn()
            make_act(C_MIX_PRE + KT, C_FF_POST)

            src = group()
            dve.tensor_tensor(halves(th[0:32, 0:TOK]), src[0:32], halves(rstd[0:32, 1]), ALU.mult)
            for k in range(2):
                ins = dve.memset(xp[:, k, PAST + DEC:PAST + DEC + PAST], 0.0)
            ins.then_inc(freed, 1)

            def pair_par(gp):
                p = par[:, bass.ds(gp * (UT * TAPS) + C_CONV, UT * TAPS)].rearrange("p (t c) -> p t c", t=UT)
                dve.tensor_scalar(cpar[:, :, 0:CONV_W + 1], p[:, :, 0:CONV_W + 1], 0.5, None, ALU.mult)
                return copy(cpar[:, :, CONV_W + 1:], p[:, :, CONV_W + 1:])

            def slab_end(k, cq):
                if cq:
                    query_tile(k, mix[:, MIX_T - MEM_H + k])
                    return
                src = group()
                if k < UT:
                    if n.k or k >= 2:
                        dve.wait_ge(conv_done, at(loop, conv_done, n.k * 3 * UT + 3 * (k - 1)) if k else
                                    at(loop, conv_done, n.k * 3 * UT))
                        dve.wait_ge(tails_done, at(loop, tails_done, n.k * UT + max(k - 1, 0)))
                    alone(dve)
                    x_ = xp[:, k % 2]
                    copy(x_[:, 0:PAST], cpar[:, k, CONV_W + 1:])
                    dve.tensor_tensor(x_[:, PAST:PAST + DEC], src[:, 0, 0:DEC], rstd[:, 1, 0:DEC], ALU.mult)
                    dve.tensor_tensor(x_[:, 2 * PAST + DEC:2 * PAST + HALF], src[:, 0, DEC:], rstd[:, 1, DEC:HALF], ALU.mult)
                    dve.tensor_tensor(x_[:, 2 * PAST + HALF:], src[:, 1], rstd[:, 1, HALF:], ALU.mult).then_inc(freed, 1)
                else:
                    if n.k:
                        dve.wait_ge(gate_done, at(loop, gate_done, BLOCKS))
                    dve.scalar_tensor_tensor(out=halves(zs[:, k - UT]), in0=src, scalar=0.5, in1=halves(rstd[:, 1]),
                                             op0=ALU.mult, op1=ALU.mult).then_inc(freed, 1)
                if k:
                    silu(k - 1)
                if k < UT:
                    dve.wait_ge(tap_done, at(loop, tap_done, n.k * UT + k + 1))
                    for j in range(1, CONV_W):
                        if j > 1:
                            dve.wait_ge(conv_done, at(loop, conv_done, n.k * 3 * UT + 3 * k + j - 1))
                        dve.scalar_tensor_tensor(out=u[:, k], in0=xp[:, k % 2, j:j + UC], scalar=cpar[:, k, j:j + 1],
                                                 in1=u[:, k], op0=ALU.mult, op1=ALU.add).then_inc(conv_done, 1)

            def silu(k):
                dve.wait_ge(tanh_done, at(loop, tanh_done, n.k * PAIR_SLABS + k + 1))
                dst, w = (u[:, k], UC) if k < UT else (zs[:, k - UT], TOK)
                dve.scalar_tensor_tensor(out=dst, in0=th[:, 0:w], scalar=1.0, in1=dst, op0=ALU.add, op1=ALU.mult).then_inc(u_done, 1)

            n.k = 0
            own.mark(pair_par(0))
            own.wait(loop)
            for k in range(PAIR_SLABS):
                slab_end(k, False)
                if k == 0:
                    dve.wait_ge(dt_moved, 1)
                    dve.tensor_tensor(dts[:, 0], ps[:, 4, 0:BLOCKS * 32].rearrange("p (b h) -> p b h", b=BLOCKS)[:, :, 0:HEADS],
                                      par[:, C_DTB:C_DTB + HEADS].unsqueeze(1).to_broadcast([P, BLOCKS, HEADS]), ALU.add).then_inc(dt_step, 1)
                    dve.wait_ge(dt_step, 1)
                    dve.scalar_tensor_tensor(out=dts[:, 1], in0=dts[:, 0], scalar=-1.0, in1=dts[:, 0], op0=ALU.mult,
                                             op1=ALU.min).then_inc(dt_step, 1)
                    dve.tensor_scalar(hs[:, 0], dts[:, 0], 0.0, None, ALU.max).then_inc(dt_step, 1)
                elif k == 1:
                    dve.wait_ge(dt_fn, 2)
                    dve.tensor_scalar(dts[:, 2], dts[:, 1], 1.0, None, ALU.add).then_inc(dt_step, 1)
                    dve.wait_ge(dt_step, 4)
                    dve.tensor_scalar(dts[:, 0], dts[:, 2], 1.0, None, ALU.is_equal).then_inc(dt_step, 1)
                    dve.wait_ge(dt_step, 5)
                    dve.wait_ge(dt_fn, 3)
                    dve.tensor_tensor(dts[:, 3], dts[:, 3], dts[:, 0], ALU.add)
                    own.mark(dve.scalar_tensor_tensor(out=dts[:, 2], in0=dts[:, 2], scalar=-1.0, in1=dts[:, 0],
                                                      op0=ALU.add, op1=ALU.add))
                    own.wait(loop)
                    own.mark(dve.reciprocal(dts[:, 2], dts[:, 2]))
                    own.mark(dve.tensor_tensor(dts[:, 3], dts[:, 3], dts[:, 1], ALU.mult))
                    own.wait(loop)
                    own.mark(dve.tensor_tensor(dts[:, 3], dts[:, 3], dts[:, 2], ALU.mult))
                    own.wait(loop)
                    dve.tensor_tensor(hs[:, 0], hs[:, 0], dts[:, 3], ALU.add).then_inc(dt_step, 1)
                    dve.wait_ge(dt_step, 6)
                    dve.tensor_tensor(hs[:, 1], hs[:, 0], ea[:].unsqueeze(1).to_broadcast([P, BLOCKS, HEADS]),
                                      ALU.mult).then_inc(dt_step, 1)
                    dve.wait_ge(dt_step, 7)
                    dve.tensor_scalar(hs[:, 1], hs[:, 1], -1.0, None, ALU.mult).then_inc(dt_step, 1)
                elif k == 2:
                    dve.wait_ge(dt_fn, 4)
                    dve.tensor_tensor(hs[:, 3], hs[:, 3], hs[:, 0], ALU.mult).then_inc(dt_step, 1)
            silu(PAIR_SLABS - 1)
            dve.wait_ge(dt_step, 9)

            def turn(gp, cq):
                eighths = (CQ_SLABS if cq else PAIR_SLABS) * KT
                dve.wait_ge(ytok_done, at(loop, ytok_done, 0))
                dve.wait_ge(gate_done, at(loop, gate_done, 0))
                dve.wait_ge(tap_done, at(loop, tap_done, UT))
                dve.wait_ge(conv_done, at(loop, conv_done, 3 * UT))
                alone(dve)
                hv = hs[:].rearrange("p k b h -> p (k b) h")
                copy(heads_cur[:].rearrange("p k b h -> p (k b) h"), hv[:, :, bass.ds(gp * PH, PH)])
                if not cq:
                    pair_par(gp + 1)
                copy(skips[:], par[:, bass.ds(gp * N_PAIR + (C_PAIR + XT), PH)]).then_inc(cur_done, 1)
                dve.wait_ge(cur_done, at(loop, cur_done, 1))
                for kind, b in ssd_steps(eighths):
                    rows = DEC if b == 0 else P
                    if kind == "K":
                        if b % KT == KT - 1:
                            slab_end(b // KT, cq)
                    elif kind == "A":
                        dve.wait_ge(tok_done, at(loop, tok_done, b + 1))
                        if b == 0:
                            dve.wait_ge(st_done, at(loop, st_done, 0))
                            dve.wait_ge(decm_done, at(loop, decm_done, 0))
                        bank = 5 + 2 * (b % 2)
                        copy(btok[0:rows, b], ps[0:rows, bank, 0:2 * P].rearrange("p (g c) -> p g c", g=2))
                        dve.tensor_tensor(cbm[0:rows, b, :, 0:rows],
                                          ps[0:rows, bank, 2 * P:2 * P + 2 * rows].rearrange("p (g c) -> p g c", g=2),
                                          mats[0:rows, 2, 0:rows].unsqueeze(1).to_broadcast([rows, 2, rows]),
                                          ALU.mult).then_inc(cbm_done, 1)
                    elif kind == "seg":
                        dve.wait_ge(dec_done, at(loop, dec_done, b + 1))
                        if b == 0:
                            dve.wait_ge(cbm_done, at(loop, cbm_done, BLOCKS))
                        alone(dve)
                        d = dec[0:rows, :, 0:rows].rearrange("p (g h) q -> p g h q", g=2)
                        dve.tensor_tensor(d, d, cbm[0:rows, b, :, 0:rows].unsqueeze(2).to_broadcast([rows, 2, 3, rows]),
                                          ALU.mult).then_inc(decm_done, 1)
                    elif kind == "off" and b != 1:
                        dve.wait_ge(off_done, at(loop, off_done, later(b)))
                        dve.wait_ge(acc_done, at(loop, acc_done, b))
                        alone(dve)
                        dve.tensor_tensor(ytok[0:rows].rearrange("p (h d) -> p h d", h=PH),
                                          ps[0:rows, 7, 0:PH * HD].rearrange("p (h d) -> p h d", h=PH),
                                          heads_cur[0:rows, 2, b].unsqueeze(2).to_broadcast([rows, PH, HD]),
                                          ALU.mult).then_inc(yoff_done, 1)
                    elif kind == "st":
                        dve.wait_ge(st_done, at(loop, st_done, b + 1))
                        dve.wait_ge(state_done, at(loop, state_done, b))
                        if b == 0:
                            dve.wait_ge(h_stored, at(loop, h_stored, 0))
                        if b != 1:
                            dve.wait_ge(hbd_done, at(loop, hbd_done, later(b)))
                        alone(dve)
                        dst, new = state[:, min(b, 1)], ps[:, 4, 0:PH * HD]
                        (copy(dst, new) if b == 1 else dve.tensor_tensor(dst, hbd, new, ALU.add)).then_inc(state_done, 1)
                    elif kind == "acc":
                        dve.wait_ge(acc_done, at(loop, acc_done, b + 1))
                        if b == 0:
                            dve.wait_ge(u_done, at(loop, u_done, PAIR_SLABS))
                            dve.wait_ge(gnorm_done, at(loop, gnorm_done, 0))
                        alone(dve)
                        c0, c1 = block_cols(b)
                        dve.tensor_tensor(mix[:, YG:YG + XT, c0:c1], ps[:, 6, 0:XT * rows].rearrange("p (t c) -> p t c", t=XT),
                                          zs[:, :, c0:c1], ALU.mult).then_inc(gate_done, 1)
                    elif kind == "N":
                        dve.wait_ge(groot_done, at(loop, groot_done, 1))
                        dve.reciprocal(grs[:], grs[:]).then_inc(grec_done, 1)
                        dve.wait_ge(grec_done, at(loop, grec_done, 1))
                        alone(dve)
                        for m, k, r0, r1 in ((0, 0, 0, P), (1, 0, 0, HD), (1, 1, HD, P), (2, 1, 0, P)):
                            dst = mix[r0:r1, bass.ds(gp * XT + m, 1), :].rearrange("p t c -> p (t c)")
                            ins = dve.tensor_tensor(dst, mix[r0:r1, YG + m], grs[r0:r1, k], ALU.mult)
                        ins.then_inc(gnorm_done, 1)
                if not cq:
                    silu(PAIR_SLABS - 1)

            loop.per = SSM_PER
            n.k = 1
            with dve.Fori(0, PAIRS - 1) as i:
                loop.i = i
                turn(i, False)
                loop.i = None
                n.s -= PAIR_SLABS
                n.g -= PAIR_SLABS
            loop.i = PAIRS - 1
            turn(PAIRS - 1, True)
            loop.i = None
            n.s += (PAIRS - 1) * PAIR_SLABS
            n.g += (PAIRS - 1) * PAIR_SLABS
            cross()
            out_projection(1)
            make_act(C_FF_PRE + KT, C_MIX_POST + KT)
            ffn()
            make_act(None, C_FF_POST + KT)


        @block.gpsimd
        def _(pool):
            loop, n = Loop(), Count()
            prime(pool, "gpsimd")

            def split_lo(s):
                if s >= ALL_SLABS:
                    return
                pool.wait_ge(hi_done, at(loop, hi_done, s + 1))
                pool.tensor_tensor(w_lo[:, s % 2], raw[:, s % 2], w_hi[:, s % 2].bitcast(F32), ALU.subtract).then_inc(lo_done, 1)

            def slabs_lo(count, turns=1):
                if turns == 1:
                    for k in range(count):
                        split_lo(n.s + k)
                else:
                    loop.per = {"hi_done": count}
                    with pool.Fori(0, turns) as i:
                        loop.i = i
                        for k in range(count):
                            split_lo(n.s + k)
                        loop.i = None
                n.s += count * turns

            def add_post(clear):
                for m in range(KT):
                    pool.wait_ge(scaled, KT * n.x + m + 1)
                    pool.tensor_tensor(x[:, m], x[:, m], mix[:, m], ALU.add).then_inc(x_done, 1)
                    if clear:
                        pool.wait_ge(x_done, KT * n.x + m + 1)
                        pool.memset(mix[:, m], 0.0).then_inc(zeroed, 1)
                n.x += 1

            def ffn():
                def up():
                    for m in range(KT):
                        split_lo(n.s)
                        n.s += 1
                        n.g += 1
                        pool.wait_ge(freed, at(loop, freed, n.g))
                        if m >= 2:
                            pool.wait_ge(act_ready, at(loop, act_ready, n.a + m - 1))
                        pool.tensor_tensor(hid[:, m % 2], relu[:, m % 2], relu[:, m % 2], ALU.mult).then_inc(hid_done, 1)
                    n.a += KT

                def down():
                    for m in range(KT):
                        split_lo(n.s)
                        n.s += 1
                        n.g += 1

                up()
                loop.per = FF_PER
                with pool.Fori(0, FF_CHUNKS - 1) as i:
                    loop.i = i
                    down()
                    up()
                    loop.i = None
                    n.s -= SLABS_FF
                    n.g -= SLABS_FF
                    n.a -= KT
                n.s += (FF_CHUNKS - 1) * SLABS_FF
                n.g += (FF_CHUNKS - 1) * SLABS_FF
                n.a += (FF_CHUNKS - 1) * KT
                down()

            pool.memset(eps[:], EPS).then_inc(zeroed, 1)
            slabs_lo(2)
            slabs_lo(8)
            slabs_lo(8)
            slabs_lo(KV_SLABS + QT)
            slabs_lo(QT, KVH)
            slabs_lo(4, OUT_SLABS // 4)
            add_post(True)
            n.a = 3 * KT + MIX_T + KT
            n.g = 2 * MEM_SLABS + ATTN_SLABS + KT
            ffn()
            add_post(False)

            def slab_end(k, gp=None):
                split_lo(n.s)
                n.s += 1
                n.g += 1
                if gp is None or k >= UT:
                    return
                pool.wait_ge(freed, at(loop, freed, n.g))
                alone(pool)
                for m, c in enumerate((DEC, UC)):
                    dst = tails[:].rearrange("p g t m c -> p g (t m c)")[:, bass.ds(gp, 1), (k * 2 + m) * PAST:(k * 2 + m + 1) * PAST]
                    ins = pool.tensor_copy(dst.rearrange("p g c -> p (g c)"), xp[:, k % 2, c:c + PAST])
                ins.then_inc(tails_done, 1)

            slab_end(UT)
            for k in range(PAIR_SLABS):
                slab_end(k, 0)

            def wide(ap, rows):
                return ap.unsqueeze(2).to_broadcast([rows, PH, HD])

            def turn(gp, cq):
                def sums(b):
                    rows = DEC if b == 0 else P
                    if b == 0:
                        pool.wait_ge(cur_done, at(loop, cur_done, 1))
                        pool.wait_ge(gnorm_done, at(loop, gnorm_done, 0))
                    pool.wait_ge(seg_done, at(loop, seg_done, b))
                    alone(pool)
                    pool.tensor_tensor(wseg[0:rows, :, 0:rows], mats[0:rows, 2, 0:rows].unsqueeze(1).to_broadcast([rows, PH, rows]),
                                       heads_cur[0:rows, 1, b].unsqueeze(2).to_broadcast([rows, PH, rows]),
                                       ALU.mult).then_inc(wseg_done, 1)

                def scaled_x(b):
                    rows = DEC if b == 0 else P
                    pool.wait_ge(xtok_done, at(loop, xtok_done, b + 1))
                    pool.wait_ge(diag_done, at(loop, diag_done, b))
                    pool.wait_ge(ytok_done, at(loop, ytok_done, b))
                    alone(pool)
                    xb = xtok[0:rows, b].rearrange("p (h d) -> p h d", h=PH)
                    if b != 1:
                        pool.tensor_tensor(xd[0:rows, 2], xb, wide(skips[0:rows], rows), ALU.mult)
                    pool.tensor_tensor(xd[0:rows, 1], xb, wide(heads_cur[0:rows, 3, b], rows), ALU.mult)
                    pool.tensor_tensor(xd[0:rows, 0], xb, wide(heads_cur[0:rows, 0, b], rows), ALU.mult).then_inc(xd_done, 1)

                eighths = (CQ_SLABS if cq else PAIR_SLABS) * KT
                for kind, b in ssd_steps(eighths):
                    rows = DEC if b == 0 else P
                    if kind == "K":
                        if b % KT == KT - 1:
                            slab_end(b // KT, None if cq else gp + 1)
                    elif kind == "A" and b == 0:
                        sums(0)
                    elif kind == "A" and b == 1:
                        scaled_x(0)
                    elif kind == "seg":
                        if b != 1:
                            if b == 0:
                                pool.wait_ge(h_loaded, at(loop, h_loaded, 16))
                            pool.wait_ge(state_done, at(loop, state_done, b))
                            alone(pool)
                            h = (h_next[:] if b == 0 else state[:, 1]).rearrange("p (h d) -> p h d", h=PH)
                            pool.tensor_tensor(hbd.rearrange("p (h d) -> p h d", h=PH), h, wide(heads_cur[:, 4, b], P),
                                               ALU.mult).then_inc(hbd_done, 1)
                        if b < BLOCKS - 1:
                            sums(b + 1)
                    elif kind == "diag":
                        y = ytok[0:rows].rearrange("p (h d) -> p h d", h=PH)
                        if b == 1:
                            pool.wait_ge(acc_done, at(loop, acc_done, b))
                            alone(pool)
                            pool.tensor_tensor(y, xtok[0:rows, b].rearrange("p (h d) -> p h d", h=PH), wide(skips[0:rows], rows),
                                               ALU.mult).then_inc(ytok_done, 1)
                        else:
                            pool.wait_ge(yoff_done, at(loop, yoff_done, later(b)))
                            pool.wait_ge(xd_done, at(loop, xd_done, b + 1))
                            alone(pool)
                            pool.tensor_tensor(y, y, xd[0:rows, 2], ALU.add).then_inc(ytok_done, 1)
                        if b < BLOCKS - 1:
                            scaled_x(b + 1)

            loop.per = SSM_PER
            with pool.Fori(0, PAIRS - 1) as i:
                loop.i = i
                turn(i, False)
                loop.i = None
                n.s -= PAIR_SLABS
                n.g -= PAIR_SLABS
            loop.i = PAIRS - 1
            turn(PAIRS - 1, True)
            loop.i = None
            n.s += (PAIRS - 1) * PAIR_SLABS
            n.g += (PAIRS - 1) * PAIR_SLABS + KT
            slabs_lo(4, OUT_SLABS // 4)
            add_post(True)
            n.a += KT + MIX_T + KT
            ffn()
            add_post(False)


        @block.sync
        def _(sp):
            loop, n = Loop(), Count()
            prime(sp, "sync")
            sp.dma_start(mraw[:], mem_in).then_inc(mem_arrived, 16)
            sp.dma_start(par[:], par_in).then_inc(const_in, 16)
            sp.dma_start(mats[:], mats_in).then_inc(const_in, 16)

            def load_slab(src, s):
                if s >= 2:
                    sp.wait_ge(lo_done, at(loop, lo_done, s - 1))
                sp.dma_start(raw[:, s % 2].rearrange("p k c -> p (k c)"), src).then_inc(raw_in[s % 2], 16)

            def load_slabs(count, turns=1):
                if turns == 1:
                    for _ in range(count):
                        load_slab(slabs[n.s], n.s)
                        n.s += 1
                    return
                loop.per = {"lo_done": count}
                with sp.Fori(0, turns) as i:
                    for k in range(count):
                        src = slabs[bass.ds(sp.snap(i * count + (n.s + k)), 1)].rearrange("s p c -> (s p) c")
                        loop.i = i
                        load_slab(src, n.s + k)
                        loop.i = None
                n.s += count * turns

            load_slabs(2)
            sp.dma_start(x[:], x_in).then_inc(x_arrived, 16)
            load_slabs(2)
            load_slabs(4, 3)
            sp.wait_ge(slab_done, 2 * MEM_SLABS)
            sp.wait_ge(mv_used, 2 * MEM_H)
            sp.dma_start(k_all[:, :, 0:P], ck_in).then_inc(cache_in, 16)
            sp.dma_start(v_all[:, 0], cv_in).then_inc(cache_in, 16)
            sp.dma_start(kms[:], mk_in[0]).then_inc(kms_in, 16)
            sp.dma_start(vms[:], mv_in[0]).then_inc(kms_in, 16)
            load_slabs(KV_SLABS + QT + 2)
            for j in range(2):
                sp.dma_start(bias[:, j], alibi[j]).then_inc(bias_in[j], 16)
            loop.per = ATT_PER
            with sp.Fori(0, KVH) as g:
                for j in range(QT):
                    tables = alibi[bass.ds(sp.snap(g * QT + (j + 2)), 1)].rearrange("t p e c -> (t p) e c")
                    src = slabs[bass.ds(sp.snap(g * QT + (n.s + j)), 1)].rearrange("s p c -> (s p) c")
                    loop.i = g
                    load_slab(src, n.s + j)
                    sp.wait_ge(biased, at(loop, biased, UNITS_J * (j + 1)))
                    sp.dma_start(bias[:, j % 2], tables).then_inc(bias_in[j % 2], 16)
                    loop.i = None
            n.s += KVH * QT
            load_slabs(2)
            load_slabs(4, 3)
            load_slabs(SLABS_FF, FF_CHUNKS)
            load_slabs(1)
            dt_slab = 2 * MEM_SLABS + ATTN_SLABS + OUT_SLABS + FF_SLABS
            load_slabs(PAIR_SLABS)
            sp.wait_ge(freed, dt_slab - KT + 1)
            sp.dma_start(h_next[:], h_in[0]).then_inc(h_loaded, 16)
            loop.per = SSM_PER
            with sp.Fori(0, PAIRS - 1) as i:
                for k in range(PAIR_SLABS):
                    src = slabs[bass.ds(sp.snap(i * PAIR_SLABS + (n.s + k)), 1)].rearrange("s p c -> (s p) c")
                    h_src = h_in[bass.ds(sp.snap(i + 1), 1)].rearrange("g p c -> (g p) c")
                    h_dst = h_out[bass.ds(sp.snap(i), 1)].rearrange("g p s c -> (g p) s c")
                    loop.i = i
                    load_slab(src, n.s + k)
                    if k == PAIR_SLABS // 2:
                        sp.wait_ge(off_done, at(loop, off_done, 1))
                        sp.wait_ge(hbd_done, at(loop, hbd_done, 1))
                        sp.dma_start(h_next[:], h_src).then_inc(h_loaded, 16)
                    if k == PAIR_SLABS - 1:
                        sp.wait_ge(state_done, at(loop, state_done, BLOCKS))
                        sp.dma_start(h_dst, state[:]).then_inc(h_stored, 16)
                    loop.i = None
            n.s += (PAIRS - 1) * PAIR_SLABS
            load_slabs(CQ_SLABS)
            sp.wait_ge(u_done, PAIRS * PAIR_SLABS)
            sp.wait_ge(tails_done, PAIRS * UT)
            sp.dma_start(kms1[:], mk_in[1]).then_inc(kms_in, 16)
            sp.dma_start(vms1[:], mv_in[1]).then_inc(kms_in, 16)
            sp.dma_start(conv_out, tails[:]).then_inc(h_stored, 16)
            load_slabs(2)
            sp.wait_ge(state_done, at(loop, state_done, PAIRS * BLOCKS))
            sp.dma_start(h_out[PAIRS - 1], state[:]).then_inc(h_stored, 16)
            load_slabs(2)
            load_slabs(4, 3)
            load_slabs(SLABS_FF, FF_CHUNKS)
            n.x = 4
            sp.wait_ge(x_done, KT * n.x)
            sp.dma_start(y_out, x[:]).then_inc(stored, 16)
            stores[0] += 1
            sp.wait_ge(stored, 16 * stores[0])
            sp.wait_ge(h_stored, at(loop, h_stored, 16 * (PAIRS + 1)))


def _conv_tiles(np):
    b, c = INNER // P, INNER // P + SGROUPS
    return np.array([t for g in range(PAIRS) for t in (3 * g, 3 * g + 1, 3 * g + 2, b + 2 * g, b + 2 * g + 1,
                                                       c + 2 * g, c + 2 * g + 1)])


def _layout(i, np):
    f = np.float32

    def tiles(w):
        k, c = w.shape
        return w.reshape(KT, P, c // P, P).transpose(2, 1, 0, 3).reshape(c // P, P, KT * P)

    def deep(w):
        return [tiles(w[c * D_MODEL:(c + 1) * D_MODEL]) for c in range(w.shape[0] // D_MODEL)]

    wa, ws = i["w_in_attn"][0], i["w_in_ssm"][0]
    parts = [tiles(i["w_mem_kv"][0]), tiles(i["w_mem_kv"][1])]
    k0, v0 = Q_W, Q_W + KV_W
    for h in range(KVH):
        w = wa[:, k0 + h * HD:k0 + (h + 1) * HD]
        parts.append(tiles(np.concatenate([w, w], 1)))
    parts += [tiles(wa[:, v0:v0 + P]), tiles(wa[:, v0 + HD:v0 + HD + P])]
    parts += [tiles(wa[:, :Q_W]), tiles(wa[:, Q_W + 2 * KV_W:])]

    def tail(layer):
        wo = np.stack(deep(i["w_out"][layer]), 1).reshape(-1, P, KT * P)
        up, down = i["w_up"][layer], i["w_down"][layer]
        out = [wo]
        for c in range(FF_CHUNKS):
            out += [tiles(up[:, c * D_MODEL:(c + 1) * D_MODEL]), tiles(down[c * D_MODEL:(c + 1) * D_MODEL])]
        return out

    parts += tail(0)
    zx, cx, dx = INNER, INNER + CONV_DIM, INNER + CONV_DIM + HEADS
    parts.append(tiles(np.concatenate([ws[:, cx:dx], np.zeros((D_MODEL, P - HEADS), f)], 1)))
    for g in range(PAIRS):
        w = XT * P
        cols = [slice(zx + g * w, zx + (g + 1) * w),
                slice(zx + INNER + g * 2 * P, zx + INNER + (g + 1) * 2 * P),
                slice(zx + INNER + SGROUPS * STATE + g * 2 * P, zx + INNER + SGROUPS * STATE + (g + 1) * 2 * P),
                slice(g * w, (g + 1) * w)]
        parts += [tiles(ws[:, c]) for c in cols]
    parts.append(tiles(ws[:, dx:]))
    parts += tail(1)
    slabs = np.concatenate(parts, 0)
    assert slabs.shape[0] == ALL_SLABS, slabs.shape

    def columns(a):
        a = a.reshape(-1, P)
        return a.T

    x = np.concatenate([i["x_sample"][0], i["x_prompt"][0]], 0)
    x = x.reshape(TOK, KT, P).transpose(2, 1, 0)
    wide = lambda a: np.broadcast_to(a.reshape(1, -1), (P, a.size))
    mem = i["mem_prompt"][0].reshape(N_MEM, KT, P).transpose(2, 1, 0)
    conv = np.concatenate([i["conv_w"][0], i["conv_b"][0][None], i["state_conv"][0, 0]], 0)
    conv = conv.reshape(TAPS, CONV_DIM // P, P)[:, _conv_tiles(np)].transpose(2, 1, 0)
    pairs = np.concatenate([i["ssm_norm"][0].reshape(PAIRS, XT, P).transpose(2, 0, 1),
                            wide(i["d_skip"]).reshape(P, PAIRS, PH)], 2)
    par = np.concatenate([columns(i[k]) for k in ("norm_mix_pre", "norm_mix_post", "norm_ffn_pre", "norm_ffn_post",
                                                  "mem_norm")]
                         + [wide(i[k]) for k in ("attn_sinks", "dt_bias", "a_log")]
                         + [conv.reshape(P, -1), pairs.reshape(P, -1)], 1)
    t = np.arange(P)
    mats = np.stack([np.eye(P), np.ones((P, P)), t[:, None] <= t[None], t[:, None] > t[None]], 1)
    r, c = np.arange(P)[:, None], np.arange(2 * P)[None]
    dist = np.abs(P + r - c).astype(f)
    seen = np.where(r < HD, c < P + HD, c >= HD)
    slopes = (2.0 ** (-8.0 * np.arange(1, HEADS + 1) / HEADS)).astype(f)
    tables = np.where(seen, -slopes[:, None, None] * dist, f(-1e30)).reshape(HEADS // 2, 2, P, 2 * P).transpose(0, 2, 1, 3)
    tables = np.concatenate([tables, tables[:2]], 0)
    ck = i["cache_swa_k"][0, 0].transpose(2, 1, 0)
    ck = np.concatenate([ck, ck], 0)
    cv = i["cache_swa_v"][0, 0]
    mk = i["cache_mem_k"][:, 0].transpose(0, 3, 2, 1)
    mv = i["cache_mem_v"][:, 0].reshape(2, 2, P, MEM_H, MEM_D).transpose(0, 2, 1, 3, 4).reshape(2, P, 2, MEM_W)
    h0 = i["state_ssm"][0, 0].reshape(PAIRS, PH * HD, STATE).transpose(0, 2, 1)
    out = dict(slabs=slabs, x=x, mem=mem, par=par, mats=mats, alibi=tables, ck=ck, cv=cv, mk=mk, mv=mv, h=h0)
    return {k: np.ascontiguousarray(v, dtype=f) for k, v in out.items()}


_OUTS = dict(y=(P, KT, TOK), swk=(HD, KVH, DEC + P), swv=(DEC + P, KVH, HD), h=(PAIRS, P, 2, PH * HD),
             conv=(P, PAIRS, UT, 2, PAST), mk=(2, P, MEM_H, N_MEM), mv=(2, P, 2, MEM_W))


def kernel(**inputs):
    import numpy as np
    import concourse.bacc as bacc
    from concourse.bass_utils import run_bass_kernel_spmd

    nc = bacc.Bacc("TRN2", target_bir_lowering=False, num_devices=1)
    arrays = _layout({k: np.asarray(v) for k, v in inputs.items()}, np)
    ins = [nc.dram_tensor(f"in_{k}", a.shape, F32, kind="ExternalInput").ap() for k, a in arrays.items()]
    outs = [nc.dram_tensor(f"out_{k}", s, F32, kind="ExternalOutput").ap() for k, s in _OUTS.items()]
    build(nc, *ins, outs)
    r = run_bass_kernel_spmd(nc, [{f"in_{k}": a for k, a in arrays.items()}], core_ids=[0]).results[0]
    o = {k: r[f"out_{k}"] for k in _OUTS}
    y = o["y"].transpose(2, 1, 0).reshape(TOK, D_MODEL)
    swk = o["swk"].transpose(2, 1, 0)
    swv = o["swv"]
    h = o["h"].transpose(2, 0, 3, 1).reshape(2, HEADS, HD, STATE)
    conv = o["conv"].reshape(P, PAIRS * UT, 2, PAST)[:, np.argsort(_conv_tiles(np))]
    conv = conv.transpose(2, 3, 1, 0).reshape(2, PAST, CONV_DIM)
    mk = o["mk"].transpose(0, 3, 2, 1)[:, None]
    mv = o["mv"].reshape(2, P, 2, MEM_H, MEM_D).transpose(0, 2, 1, 3, 4).reshape(2, 1, N_MEM, MEM_H, MEM_D)
    pair = lambda a: a[None, None]
    return (y[None, DEC:], y[None, :DEC], pair(swk[DEC:]), pair(swv[DEC:]), pair(h[1]), pair(conv[1]), mk, mv,
            pair(swk[:DEC]), pair(swv[:DEC]), pair(h[0]), pair(conv[0]))
```

```python
from contextlib import ExitStack

import concourse.bass as bass
from concourse import mybir

F32 = mybir.dt.float32
F32R = mybir.dt.float32r
ALU = mybir.AluOpType
ACT = mybir.ActivationFunctionType
AX = mybir.AxisListType

P = 128
D_MODEL, SEQ, DEC = 1024, 512, 64
TOK = DEC + SEQ
HALF = TOK // 2
KT = D_MODEL // P
HEADS, KVH, HD = 24, 3, 64
GROUP = HEADS // KVH
Q_W, KV_W = HEADS * HD, KVH * HD
N_MEM, MEM_H, MEM_D = 256, 4, 128
MEM_W = MEM_H * MEM_D
INNER, SGROUPS, STATE, CONV_W = 1536, 8, 128, 4
CONV_DIM = INNER + 2 * SGROUPS * STATE
MIX_T = (Q_W + MEM_W) // P
D_FF = 4 * D_MODEL
FF_CHUNKS = D_FF // D_MODEL
EPS = 1e-6
BLOCKS = 5
QT = GROUP // 2
SLABS_FF = 2 * KT


def block_cols(b):
    return (0, DEC) if b == 0 else (DEC + (b - 1) * P, DEC + b * P)


class Loop:
    i, per = None, {}


PRIMED = {"tensor": ("seg_done", "diag_done", "off_done", "acc_done", "st_done", "gsum_done"),
          "scalar": ("groot_done", "h_stored"),
          "vector": ("gnorm_done", "yoff_done", "decm_done", "y_done", "state_done", "gated_done"),
          "gpsimd": ("ytok_done", "hbd_done"), "sync": ()}
PRIMED_NAMES = sum(PRIMED.values(), ())


def at(loop, sem, value):
    value += sem.name in PRIMED_NAMES
    if loop.i is None:
        return value
    assert value > 0, sem.name
    return value + loop.i * loop.per[sem.name]


MEM_SLABS = 2 * MEM_W // P
KV_SLABS = KVH + 2
Q_SLABS = (Q_W + MEM_W) // P
OUT_SLABS = 2 * KT
FF_SLABS = FF_CHUNKS * SLABS_FF
PAIRS = SGROUPS // 2
PH = 2 * HEADS // SGROUPS
XT = PH * HD // P
PAIR_SLABS = XT + XT + 2 + 2
CQ_SLABS = MEM_W // P
ATTN_SLABS = KV_SLABS + Q_SLABS
SSM_SLABS = 1 + PAIRS * PAIR_SLABS + CQ_SLABS
ALL_SLABS = 2 * MEM_SLABS + ATTN_SLABS + SSM_SLABS + 2 * (OUT_SLABS + FF_SLABS)

C_MIX_PRE, C_MIX_POST, C_FF_PRE, C_FF_POST, C_MEM = 0, 16, 32, 48, 64
C_SINK, C_DTB, C_ALOG = 80, 104, 128
UT = XT + 4
TAPS = CONV_W + 1 + CONV_W - 1
C_CONV = 152
C_PAIR = C_CONV + PAIRS * UT * TAPS
N_PAIR = XT + PH
N_PAR = C_PAIR + PAIRS * N_PAIR

UNITS_J = 5
UNITS = QT * UNITS_J
LAG_T, LAG_PV = 3, 4
SPAN = P + DEC + SEQ

LN_EXP = "natural_log_exp_and_others"
SCALE_AHEAD = 2
PRE_WIDTHS = (KT // 2, KT // 4, KT // 8)
MEM_AHEAD = [(0, 1)] + [(m,) for m in range(2, KT)] + [()]
X_SUM_SLAB = 4
Y_POOL = 5
ARTANH_TERMS = 8

PAST = CONV_W - 1
XP = PAST + DEC + PAST + SEQ
UC = XP - PAST


def conv_cols(b):
    c0, c1 = block_cols(b)
    return (c0, c1) if b == 0 else (c0 + PAST, c1 + PAST)


def turn_tiles(last):
    return [("z", j) for j in range(XT)] + [("q", h) for h in range(CQ_SLABS)] * last + [("u", t) for t in range(UT)] * (not last)


FIRST_TILES = [("u", t) for t in range(UT)]


def ssd_steps(last):
    steps, k, eighths = [], 0, len(turn_tiles(last)) * KT

    def fill(upto):
        nonlocal k
        while k < min(upto, eighths):
            steps.append(("K", k))
            k += 1

    lead = 2 * KT
    start, end = lead + BLOCKS, eighths - 2 * KT
    for b in range(BLOCKS):
        fill(lead + b)
        steps.append(("A", b))
    fill(start)
    gap = 0
    for b in range(BLOCKS):
        for kind in ("seg", "off", "st", "diag", "acc"):
            if kind != "off":
                gap += 1
                fill(start + (end - start) * gap // (4 * BLOCKS + 1))
            steps.append((kind, b))
    steps.append(("Q", 0))
    fill(eighths - 10)
    steps.append(("G", 0))
    fill(eighths - 6)
    steps.append(("N", 0))
    fill(eighths)
    return steps


def attention_steps():
    steps, k, total = [], 0, UNITS + LAG_PV
    for t in range(total):
        if t < UNITS:
            steps.append(("S", t))
        if 0 <= t - LAG_T < UNITS:
            steps.append(("T", t - LAG_T))
        while k < QT * KT and (k - 1) * (total - 1) <= t * QT * KT and k + 1 < KT * (1 + (t + 1) // UNITS_J):
            steps.append(("K", k))
            k += 1
        if 0 <= t - LAG_PV < UNITS:
            steps.append(("V", t - LAG_PV))
    while k < QT * KT:
        steps.append(("K", k))
        k += 1
    return steps


def build(nc, slabs, x_in, mem_in, par_in, mats_in, alibi, ck_in, cv_in, mk_in, mv_in, h_in, outs):
    (y_out, swk_out, swv_out, h_out, conv_out, memk_out, memv_out) = outs
    ctx = ExitStack()
    with ctx:

        def sb_at(name, shape, dt, offset):
            return nc.alloc_sbuf_tensor_at(name, shape, dt, offset=offset)

        class Area:
            def __init__(self, start, end):
                self.p, self.end = start, end

            def take(self, name, shape, dt=F32):
                size = 4
                for n in shape[1:]:
                    size *= n
                start = (self.p + 31) // 32 * 32
                assert start + size <= self.end, (name, start + size - self.end)
                self.p = start + size
                return sb_at(name, shape, dt, start)

        main = Area(nc.sbuf_base, nc.sbuf_usable_end)
        x = main.take("x", [P, KT, TOK])
        raw = main.take("raw", [P, 2, KT, P])
        w_hi = main.take("w_hi", [P, 2, KT, P], F32R)
        w_lo = main.take("w_lo", [P, 2, KT, P], F32R)
        mix = main.take("mix", [P, MIX_T, TOK])
        rstd = main.take("rstd", [P, 2, TOK])
        sq = main.take("sq", [P, 2, TOK])
        sq_sum = main.take("sq_sum", [P, TOK])
        par = main.take("par", [P, N_PAR])
        mats = main.take("mats", [P, 4, P])
        eps = main.take("eps", [P, 1])
        kvm1 = main.take("kvm1", [P, MEM_SLABS // 2, N_MEM])
        vm1 = main.take("vm1", [P, 2, MEM_W])
        main.p = (main.p + 31) // 32 * 32
        big_start = main.p
        big_hi = main.take("big_hi", [P, MIX_T, TOK], F32R)
        big_lo = main.take("big_lo", [P, MIX_T, TOK], F32R)
        spare = main.p
        half = KT * TOK * 4
        area_a = (big_start, big_start + half)
        area_b = (big_start + 2 * half, big_start + 3 * half)
        area_c = (spare, nc.sbuf_usable_end)
        ff = Area(*area_c)
        relu = ff.take("relu", [P, 2, TOK])
        hid = ff.take("hid", [P, 2, TOK])
        ma = Area(*area_a)
        mraw = ma.take("mraw", [P, KT, N_MEM])
        mv_t = ma.take("mv_t", [P, 2, N_MEM])
        mb = Area(*area_b)
        m_hi = mb.take("m_hi", [P, KT, N_MEM], F32R)
        m_lo = mb.take("m_lo", [P, KT, N_MEM], F32R)
        m_hi1 = ma.take("m_hi1", [P, KT, N_MEM], F32R)
        a1, a2, a3 = Area(*area_a), Area(*area_b), Area(*area_c)
        k_all = a1.take("k_all", [P, KVH, SPAN])
        k_cur = a1.take("k_cur", [P, SPAN])
        v_all = a1.take("v_all", [P, BLOCKS + 1, KVH, HD])
        v_cur = a1.take("v_cur", [P, BLOCKS + 1, HD])
        q_t = a2.take("q_t", [P, QT, TOK])
        v_t = a2.take("v_t", [P, 2, TOK])
        bias = a2.take("bias", [P, 2, 2, 2 * P])
        km0 = a3.take("km0", [P, MEM_H, N_MEM])
        vm0 = a3.take("vm0", [P, 2, MEM_W])
        q_s = a3.take("q_s", [P, QT, 2 * DEC])
        v_s = a3.take("v_s", [P, 2, 2, HD])
        kms = a3.take("kms", [P, MEM_H, N_MEM])
        vms = a3.take("vms", [P, 2, MEM_W])
        p_t = a3.take("p_t", [P, 2, 4 * P])
        rm = a3.take("rm", [P, N_MEM])
        m_lo1 = sb_at("m_lo1", [P, KT, N_MEM], F32R, (a3.p + 31) // 32 * 32)
        prob = a3.take("prob", [P, 4, 2, 2 * P])
        sink_cur = a3.take("sink_cur", [P, GROUP])
        stat = a3.take("stat", [P, 4, 4, 2])

        c1, c2, c3 = Area(*area_a), Area(*area_b), Area(*area_c)
        u = c1.take("u", [P, UT, UC])
        heads_cur = c1.take("heads_cur", [P, 5, BLOCKS, PH])
        tails = c1.take("tails", [P, PAIRS, UT, 2, PAST])
        cpar = c1.take("cpar", [P, UT, TAPS])
        skips = c1.take("skips", [P, PH])
        gsq = sb_at("gsq", [P, XT, TOK], F32, (c2.p + 31) // 32 * 32)
        xtok = c2.take("xtok", [P, BLOCKS, XT * P])
        btok = c2.take("btok", [P, BLOCKS, 2, P])
        cbm = c2.take("cbm", [P, BLOCKS, 2, P])
        late = Area(*area_c)
        kms1 = late.take("kms1", [P, MEM_H, N_MEM])
        vms1 = late.take("vms1", [P, 2, MEM_W])
        xp = c3.take("xp", [P, 2, XP])
        th = c3.take("th", [P, UC])
        c3.p = max(c3.p, late.p)
        state = c3.take("state", [P, 2, PH * HD])
        h_next = c3.take("h_next", [P, PH * HD])
        ytok = c3.take("ytok", [P, PH * HD])
        hs = c3.take("hs", [P, 5, BLOCKS, HEADS])
        ea = c3.take("ea", [P, HEADS])
        zs = c3.take("zs", [P, XT, TOK])
        c_cur = c3.take("c_cur", [P, 2, UC])
        grs = sb_at("grs", [P, 2, TOK], F32, (c3.p + 31) // 32 * 32)
        dts = sb_at("dts", [P, 4, BLOCKS, HEADS], F32, (c3.p + 31) // 32 * 32)
        wseg = c3.take("wseg", [P, PH, P])
        dec = c3.take("dec", [P, PH, P])
        xd = sq[:].rearrange("p s c -> p (s c)").rearrange("p (k h d) -> p k h d", k=3, h=PH)
        hbd = rstd[:, 0, 0:PH * HD]
        YG = MIX_T - MEM_H - XT
        ps = ctx.enter_context(nc.psum_tensor("ps", [P, 8, 512], F32))
        S_BANK, T_BANK, O_BANK, STAT_BANK = 4, 6, 7, 6

        def sem(name):
            return ctx.enter_context(nc.semaphore(name))

        raw_in = [sem(f"raw_in{i}") for i in range(2)]
        hi_done, lo_done = sem("hi_done"), sem("lo_done")
        slab_done = sem("slab_done")
        freed = sem("freed")
        act_hi = sem("act_hi")
        act_ready = sem("act_ready")
        sq_ready, sq_used = sem("sq_ready"), sem("sq_used")
        pre_sq, pre_added = sem("pre_sq"), sem("pre_added")
        summed = sem("summed")
        root_done, rstd_ready = sem("root_done"), sem("rstd_ready")
        scaled = sem("scaled")
        x_done = sem("x_done")
        y_added = sem("y_added")
        zeroed = sem("zeroed")
        hid_done = sem("hid_done")
        x_arrived = [sem(f"x_arrived{i}") for i in range(2)]
        mem_arrived, const_in, cache_in = [sem(f"mem_arrived{i}") for i in range(2)], sem("const_in"), sem("cache_in")
        mv_used, vm_done = sem("mv_used"), sem("vm_done")
        vt_done, va_done = sem("vt_done"), sem("va_done")
        cur_ready = sem("cur_ready")
        bias_in = [sem(f"bias_in{i}") for i in range(2)]
        s_done, biased = sem("s_done"), sem("biased")
        max_done, exp_done, normed = sem("max_done"), sem("exp_done"), sem("normed")
        t_done, pt_done = sem("t_done"), sem("pt_done")
        v_done, o_done = sem("v_done"), sem("o_done")
        kms_in, nobody = sem("kms_in"), sem("nobody")
        mats_arrived = sem("mats_arrived")
        dt_moved, dt_step, dt_fn = sem("dt_moved"), sem("dt_step"), sem("dt_fn")
        tap_done, conv_done = sem("tap_done"), sem("conv_done")
        tanh_done, u_done = sem("tanh_done"), sem("u_done")
        tails_done = sem("tails_done")
        cur_done = sem("cur_done")
        tok_done, xtok_done, cbm_done, c_done = sem("tok_done"), sem("xtok_done"), sem("cbm_done"), sem("c_done")
        wseg_done, seg_done = sem("wseg_done"), sem("seg_done")
        dec_done, decm_done = sem("dec_done"), sem("decm_done")
        xd_done, diag_done = sem("xd_done"), sem("diag_done")
        off_done, yoff_done, ytok_done = sem("off_done"), sem("yoff_done"), sem("ytok_done")
        st_done, hbd_done, state_done = sem("st_done"), sem("hbd_done"), sem("state_done")
        acc_done, y_done = sem("acc_done"), sem("y_done")
        gsq_done, gsum_done, groot_done, gnorm_done = sem("gsq_done"), sem("gsum_done"), sem("groot_done"), sem("gnorm_done")
        h_loaded, h_stored, grec_done = sem("h_loaded"), sem("h_stored"), sem("grec_done")
        gated_done, conv_stored = sem("gated_done"), sem("conv_stored")
        dve_self = sem("dve_self")
        stored = sem("stored")
        stores = [0]

        def norm_weight(layer, k):
            return C_PAIR + k // XT * N_PAIR + k % XT if layer and k < INNER // P else None

        def halves(ap):
            return ap.rearrange("p (h c) -> p h c", h=2)

        class Count:
            def __init__(self):
                self.s = self.g = self.a = self.c = self.n = self.j = self.x = self.f = self.k = self.p = self.q = 0

        class Own:
            def __init__(self, eng, sem_):
                self.eng, self.sem, self.n = eng, sem_, 0

            def mark(self, ins):
                self.n += 1
                return ins.then_inc(self.sem, 1)

            def wait(self, loop, n=None):
                self.eng.wait_ge(self.sem, at(loop, self.sem, self.n if n is None else n))

        FF_PER = {"hi_done": SLABS_FF, "lo_done": SLABS_FF, "slab_done": SLABS_FF, "freed": SLABS_FF,
                  "raw_in0": 8 * SLABS_FF, "raw_in1": 8 * SLABS_FF, "act_ready": KT, "act_hi": KT,
                  "hid_done": KT}
        OUT_PER = {"hi_done": 4, "lo_done": 4, "slab_done": 4, "freed": 2, "raw_in0": 32, "raw_in1": 32,
                   "sq_ready": 2, "sq_used": 2}
        ATT_PER = {"hi_done": QT, "lo_done": QT, "slab_done": QT, "freed": QT, "raw_in0": 8 * QT,
                   "raw_in1": 8 * QT, "bias_in0": 8 * QT, "bias_in1": 8 * QT, "s_done": UNITS,
                   "biased": UNITS, "max_done": UNITS, "exp_done": UNITS, "normed": UNITS,
                   "t_done": UNITS, "pt_done": UNITS, "v_done": UNITS, "o_done": 2 * QT,
                   "cur_ready": 1, "dve_self": 0}
        STEPS = attention_steps()
        SSM_PER = {"hi_done": PAIR_SLABS, "lo_done": PAIR_SLABS, "slab_done": PAIR_SLABS, "freed": PAIR_SLABS,
                   "raw_in0": 8 * PAIR_SLABS, "raw_in1": 8 * PAIR_SLABS, "tap_done": UT, "conv_done": 3 * UT,
                   "tanh_done": PAIR_SLABS, "u_done": PAIR_SLABS, "tails_done": UT, "cur_done": 1,
                   "c_done": 1, "gsq_done": 1, "gsum_done": 1, "groot_done": 1, "gnorm_done": 1, "grec_done": 1, "gated_done": 1,
                   "h_loaded": 16, "h_stored": 16}
        for s_ in (tok_done, xtok_done, cbm_done, wseg_done, seg_done, dec_done, decm_done, xd_done, diag_done,
                   ytok_done, st_done, state_done, acc_done, y_done):
            SSM_PER[s_.name] = BLOCKS
        for s_ in (off_done, yoff_done, hbd_done):
            SSM_PER[s_.name] = BLOCKS - 1

        def later(b):
            return b + 1 if b == 0 else b

        def alone(eng):
            eng.sem_inc(nobody, 1)
        X_UNITS, X_SCALE = 3 * MEM_H, (HD / MEM_D) ** 0.5
        O_TOTAL = [2 * QT * KVH + X_UNITS, 2 * QT * KVH + 2 * X_UNITS]

        def prime(eng, name):
            for s in (seg_done, diag_done, off_done, acc_done, st_done, gsum_done, groot_done, gnorm_done, yoff_done,
                      decm_done, y_done, state_done, ytok_done, hbd_done, h_stored, gated_done):
                if s.name in PRIMED[name]:
                    eng.sem_inc(s, 1)

        block = ctx.enter_context(nc.Block())

        @block.scalar
        def _(act):
            loop, n = Loop(), Count()
            prime(act, "scalar")

            def split_hi(s):
                if s >= ALL_SLABS:
                    return
                act.wait_ge(raw_in[s % 2], at(loop, raw_in[s % 2], 16 * (s // 2 + 1)))
                if s >= 2:
                    act.wait_ge(slab_done, at(loop, slab_done, s - 1))
                act.activation(w_hi[:, s % 2], raw[:, s % 2], ACT.Copy).then_inc(hi_done, 1)

            def next_slab():
                split_hi(n.s + 2)
                n.s += 1

            def square(src, m):
                if m >= 2:
                    act.wait_ge(sq_used, at(loop, sq_used, KT * n.p + m - 1))
                dst = sq[:, m % 2]
                if len(src.shape) == 3:
                    dst = halves(dst)
                act.activation(dst, src, ACT.Square).then_inc(sq_ready, 1)

            def root(c, dst, psum):
                act.wait_ge(summed, c + 1)
                act.activation(dst, psum, ACT.Ln, bias=eps[:, 0:1], scale=1.0 / D_MODEL).then_inc(root_done, 1)
                act.wait_ge(root_done, c + 1)
                act.activation(dst, dst, ACT.Exp, scale=-0.5).then_inc(rstd_ready, 1)

            def act_tile(w, m):
                act.activation(big_hi[:, KT + m], x[:, m], ACT.Copy, scale=par[:, w + m:w + m + 1]).then_inc(act_hi, 1)
                act.activation(mix[:, KT + m], x[:, m], ACT.Square).then_inc(pre_sq, 1)

            def make_act(w):
                for m in range(KT):
                    act.wait_ge(x_done, KT * n.x + m + 1)
                    act_tile(w, m)
                n.x += 1

            def pre_root():
                root(n.c, halves(rstd[:, 1]), ps[:, STAT_BANK:STAT_BANK + 2, 0:HALF])
                n.c += 1

            def post_root():
                root(n.c, halves(rstd[:, 0]), ps[:, STAT_BANK:STAT_BANK + 2, 0:HALF])
                n.c += 1
                n.p += 1

            act.preload_act_table_set(LN_EXP)
            act.wait_ge(zeroed, 1)
            act.wait_ge(const_in, 16)
            def mem_tile(dst, w, m):
                act.activation(dst[:, m], mraw[:, m], ACT.Copy, scale=par[:, w + m:w + m + 1]).then_inc(act_hi, 1)

            for layer in range(2):
                if layer == 0:
                    for m in range(KT):
                        if m in (0, 2):
                            act.wait_ge(mem_arrived[m // 2], 16)
                        mem_tile(m_hi, C_MEM, m)
                        if m in (1, 4):
                            split_hi(m // 4)
                    for m in range(KT):
                        act.activation(mix[:, KT + m, 0:N_MEM], mraw[:, m], ACT.Square).then_inc(pre_sq, 1)
                n.a += KT
                if layer == 0:
                    root(0, rm[:], ps[:, STAT_BANK, 0:N_MEM])
                    n.c += 1
                v_dst = vm1 if layer else vm0
                for k in range(MEM_SLABS):
                    next_slab()
                    if layer and k == X_SUM_SLAB:
                        pre_root()
                    if k >= MEM_H:
                        h = k - MEM_H
                        act.wait_ge(mv_used, MEM_H * layer + h + 1)
                        act.activation(v_dst[:, :, h * P:(h + 1) * P],
                                       ps[:, 4 + h % 2, 0:2 * P].rearrange("p (t d) -> p t d", t=2),
                                       ACT.Copy).then_inc(vm_done, 1)
                    if layer == 0:
                        for m in MEM_AHEAD[k]:
                            mem_tile(m_hi1, C_MEM + KT, m)
                        if k in (1, 1 + KT // 2):
                            act.wait_ge(x_arrived[k // (KT // 2)], 16)
                        if k:
                            act_tile(C_MIX_PRE, k - 1)
                if layer == 0:
                    act_tile(C_MIX_PRE, KT - 1)
                act.wait_ge(freed, MEM_SLABS * (layer + 1))
                act.dma_start(memk_out[layer], (kvm1 if layer else km0)[:]).then_inc(stored, 16)
                act.wait_ge(vm_done, MEM_H * (layer + 1))
                act.dma_start(memv_out[layer], v_dst[:]).then_inc(stored, 16)
                stores[0] += 2

            n.g += 2 * MEM_SLABS + ATTN_SLABS
            for k in range(KV_SLABS):
                next_slab()
            for j in range(QT):
                next_slab()

            def exps(t):
                n_, j, u = n.n + t, t // UNITS_J, t % UNITS_J
                r = n_ % 4
                act.wait_ge(max_done, at(loop, max_done, n_ + 1))
                if u == 0:
                    parts = [(0, prob[:, r, 0, 0:DEC + P])]
                else:
                    e = (u - 1) // 2
                    parts = [(b, prob[:, r, b, P if u % 2 and b == 0 else 0:2 * P]) for b in range(2)]
                for b, ap in parts:
                    act.activation(ap, ap, ACT.Exp, bias=stat[:, r, 1, b:b + 1], accum_out=stat[:, r, 2, b:b + 1])
                if u == 0:
                    for e in range(2):
                        half = slice(e * DEC, (e + 1) * DEC)
                        ins = act.activation(stat[half, r, 3, 0:1], stat[half, r, 0, 0:1], ACT.Exp,
                                             scale=-1.0, bias=sink_cur[half, 2 * j + e:2 * j + e + 1])
                else:
                    ins = act.activation(stat[:, r, 3, :], stat[:, r, 0, :], ACT.Exp, scale=-1.0,
                                         bias=sink_cur[:, 2 * j + e:2 * j + e + 1])
                ins.then_inc(exp_done, 1)

            def copy_t(t):
                n_, u = n.n + t, t % UNITS_J
                act.wait_ge(t_done, at(loop, t_done, n_ + 1))
                if t >= 2:
                    act.wait_ge(v_done, at(loop, v_done, n_ - 1))
                if u == 0:
                    act.activation(p_t[:, n_ % 2, 0:P], ps[:, T_BANK, 0:P], ACT.Copy)
                    act.activation(p_t[0:DEC, n_ % 2, P:2 * P], ps[0:DEC, T_BANK, P:2 * P], ACT.Copy).then_inc(pt_done, 1)
                else:
                    w = 3 * P if u % 2 else 4 * P
                    act.activation(p_t[:, n_ % 2, 0:w], ps[:, T_BANK, 0:w], ACT.Copy).then_inc(pt_done, 1)

            loop.per = ATT_PER
            with act.Fori(0, KVH) as g:
                loop.i = g
                for kind, t in STEPS:
                    if kind == "S" and t < LAG_T:
                        exps(t)
                    elif kind == "T":
                        copy_t(t)
                        if t + LAG_T < UNITS:
                            exps(t + LAG_T)
                    elif kind == "K" and t % KT == KT - 1:
                        next_slab()
                loop.i = None
                n.s -= QT
            n.s += KVH * QT
            n.n += KVH * UNITS
            act.dma_start(swk_out[:, :, 0:DEC], k_all[0:HD, :, P:P + DEC]).then_inc(stored, 16)
            act.dma_start(swk_out[:, :, DEC:], k_all[0:HD, :, SPAN - P:]).then_inc(stored, 16)
            act.dma_start(swv_out[0:DEC], v_all[0:DEC, 1]).then_inc(stored, 16)
            act.dma_start(swv_out[DEC:], v_all[:, BLOCKS]).then_inc(stored, 16)
            stores[0] += 4

            def cross():
                def exps(c):
                    n_, u = n.n + c, c % 3
                    act.wait_ge(max_done, n_ + 1)
                    rows = P if u else DEC
                    for b in range(2 if u else 1):
                        ins = act.activation(prob[0:rows, n_ % 4, b], ps[0:rows, S_BANK + n_ % 2, b * N_MEM:(b + 1) * N_MEM],
                                             ACT.Exp, bias=stat[0:rows, n_ % 4, 1, b:b + 1], scale=X_SCALE,
                                             accum_out=stat[0:rows, n_ % 4, 2, b:b + 1])
                    ins.then_inc(exp_done, 1)

                def copy_t(c):
                    n_, w = n.n + c, 4 * P if c % 3 else 2 * DEC
                    act.wait_ge(t_done, n_ + 1)
                    act.wait_ge(v_done, n_ - 1)
                    act.activation(p_t[:, n_ % 2, 0:w], ps[:, T_BANK, 0:w], ACT.Copy).then_inc(pt_done, 1)

                for c in range(X_UNITS + LAG_T):
                    if c >= LAG_T:
                        copy_t(c - LAG_T)
                    if c < X_UNITS:
                        exps(c)
                n.n += X_UNITS
                n.j += X_UNITS

            def out_projection(layer):
                act.wait_ge(o_done, O_TOTAL[layer])
                act.wait_ge(stored, 16 * stores[0])
                for k in range(MIX_T):
                    w = norm_weight(layer, k)
                    scale = 1.0 if w is None else par[:, w:w + 1]
                    act.activation(big_hi[:, k], mix[:, k], ACT.Copy, scale=scale).then_inc(act_hi, 1)
                n.a += MIX_T

                def group(m, g):
                    next_slab()
                    act.wait_ge(slab_done, at(loop, slab_done, n.s + 1))
                    square(ps[:, 2 * (g % 2):2 * (g % 2) + 2, 0:HALF], m)
                    next_slab()

                for m in range(2):
                    group(m, n.g + m)
                loop.per = OUT_PER
                with act.Fori(0, KT // 2 - 1) as i:
                    loop.i = i
                    for m in range(2, 4):
                        group(m, n.g + m)
                    loop.i = None
                    n.s -= 4
                n.s += OUT_SLABS - 4
                n.g += KT
                post_root()

            def ffn():
                def up(first=False):
                    for m in range(KT):
                        next_slab()
                        if first and m == 0:
                            pre_root()
                        n.g += 1
                        act.wait_ge(freed, at(loop, freed, n.g))
                        act.activation(big_hi[:, m], relu[:, m % 2], ACT.Square).then_inc(act_hi, 1)

                def down(last):
                    for m in range(KT):
                        next_slab()
                        n.g += 1
                        if last:
                            act.wait_ge(freed, n.g)
                            square(mix[:, m], m)

                up(first=True)
                loop.per = FF_PER
                with act.Fori(0, FF_CHUNKS - 1) as i:
                    loop.i = i
                    down(False)
                    up()
                    loop.i = None
                    n.s -= SLABS_FF
                    n.g -= SLABS_FF
                n.s += (FF_CHUNKS - 1) * SLABS_FF
                n.g += (FF_CHUNKS - 1) * SLABS_FF
                down(True)
                n.f += 1
                post_root()

            cross()
            out_projection(0)
            make_act(C_FF_PRE)
            ffn()
            make_act(C_MIX_PRE + KT)

            def slab_end(tiles, k):
                next_slab()
                if k:
                    tanh(tiles, k - 1)
                n.g += 1
                kind, t = tiles[k]
                if kind == "u":
                    act.wait_ge(freed, at(loop, freed, n.g))
                    if n.k:
                        act.wait_ge(tok_done, at(loop, tok_done, BLOCKS))
                        act.wait_ge(c_done, at(loop, c_done, 1))
                    act.activation(u[:, t], xp[:, t % 2, 0:UC], ACT.Identity, bias=cpar[:, t, CONV_W:CONV_W + 1],
                                   scale=cpar[:, t, 0:1]).then_inc(tap_done, 1)

            def tanh(tiles, k):
                kind, t = tiles[k]
                if kind == "q":
                    return
                if kind == "u":
                    act.wait_ge(conv_done, at(loop, conv_done, 3 * (n.k + t + 1)))
                else:
                    act.wait_ge(freed, at(loop, freed, n.g))
                if n.k or k:
                    act.wait_ge(u_done, at(loop, u_done, n.k + k))
                src, w = (u[:, t], UC) if kind == "u" else (zs[:, t], TOK)
                act.activation(th[:, 0:w], src, ACT.Tanh).then_inc(tanh_done, 1)

            next_slab()
            pre_root()
            n.g += 1
            for k in range(UT):
                slab_end(FIRST_TILES, k)
                if k == 0:
                    act.activation(ea[:], par[:, C_ALOG:C_ALOG + HEADS], ACT.Exp).then_inc(dt_fn, 1)
                    act.wait_ge(dt_step, 2)
                    act.activation(dts[:, 1], dts[:, 1], ACT.Exp).then_inc(dt_fn, 1)
                elif k == 3:
                    act.wait_ge(dt_moved, 2)
                    for m in range(3):
                        ins = act.activation(hs[:, 2 + m], ps[:, 4 + m, 0:BLOCKS * HEADS].rearrange("p (b h) -> p b h", b=BLOCKS),
                                             ACT.Exp)
                    ins.then_inc(dt_fn, 1)
            tanh(FIRST_TILES, UT - 1)

            def turn(gp, last):
                for kind, b in ssd_steps(last):
                    rows = DEC if b == 0 else P
                    if kind == "K":
                        if b % KT == KT - 1:
                            slab_end(turn_tiles(last), b // KT)
                    elif kind == "A":
                        act.wait_ge(tok_done, at(loop, tok_done, b + 1))
                        if b == 0:
                            act.wait_ge(gsum_done, at(loop, gsum_done, 0))
                            act.wait_ge(off_done, at(loop, off_done, 0))
                        act.activation(xtok[0:rows, b], ps[0:rows, 4 + 2 * (b % 2), 0:XT * P], ACT.Copy).then_inc(xtok_done, 1)
                        if b < 2:
                            ins = act.activation(c_cur[:, b], u[:, XT + 2 + b], ACT.Copy)
                            if b:
                                ins.then_inc(c_done, 1)
                    elif kind == "seg":
                        act.wait_ge(seg_done, at(loop, seg_done, b + 1))
                        act.wait_ge(diag_done, at(loop, diag_done, b))
                        if b == 0:
                            act.wait_ge(gnorm_done, at(loop, gnorm_done, 0))
                        for m in range(2):
                            ins = act.activation(dec[0:rows, 3 * m:3 * m + 3, 0:rows],
                                                 ps[0:rows, 4 + m, 0:3 * rows].rearrange("p (h q) -> p h q", h=3), ACT.Exp)
                        ins.then_inc(dec_done, 1)
                    elif kind == "Q":
                        act.wait_ge(gated_done, at(loop, gated_done, 1))
                        for m in range(XT):
                            ins = act.activation(gsq[:, m], mix[:, YG + m], ACT.Square)
                        ins.then_inc(gsq_done, 1)
                    elif kind == "G":
                        act.preload_act_table_set(LN_EXP)
                        act.wait_ge(gsum_done, at(loop, gsum_done, 1))
                        act.activation(grs[:].rearrange("p g (h c) -> p (g h) c", h=2), ps[:, 4:8, 0:HALF], ACT.Ln,
                                       bias=eps[:, 0:1], scale=SGROUPS / INNER).then_inc(groot_done, 1)
                        act.wait_ge(groot_done, at(loop, groot_done, 1))
                        act.activation(grs[:], grs[:], ACT.Exp, scale=-0.5).then_inc(grec_done, 1)
                        dst = h_out[PAIRS - 1] if last else h_out[bass.ds(act.snap(gp), 1)].rearrange("g p s c -> (g p) s c")
                        act.wait_ge(state_done, at(loop, state_done, BLOCKS))
                        act.dma_start(dst, state[:]).then_inc(h_stored, 16)
                tanh(turn_tiles(last), len(turn_tiles(last)) - 1)

            loop.per = SSM_PER
            n.k = UT
            with act.Fori(0, PAIRS - 1) as i:
                loop.i = i
                turn(i, False)
                loop.i = None
                n.s -= PAIR_SLABS
                n.g -= PAIR_SLABS
            loop.i = PAIRS - 1
            turn(PAIRS - 1, True)
            loop.i = None
            n.s += (PAIRS - 1) * PAIR_SLABS
            n.g += (PAIRS - 1) * PAIR_SLABS
            cross()
            act.wait_ge(conv_stored, 16)
            act.wait_ge(h_stored, at(loop, h_stored, 16 * PAIRS))
            out_projection(1)
            make_act(C_FF_PRE + KT)
            ffn()


        @block.tensor
        def _(pe):
            loop, n = Loop(), Count()
            prime(pe, "tensor")

            def feature_sum(src, cols=TOK):
                if n.c:
                    pe.wait_ge(root_done, n.c)
                for h in range(2 if cols == TOK else 1):
                    w = HALF if cols == TOK else cols
                    ins = pe.matmul(ps[:, STAT_BANK + h, 0:w], mats[:, 1], src[:, h * w:(h + 1) * w], start=True, stop=True)
                ins.then_inc(summed, 1)
                n.c += 1

            def pre_sum(cols=TOK):
                n.q += 1
                pe.wait_ge(pre_added, n.q)
                feature_sum(mix[:, KT], cols)

            def post_sum():
                n.p += 1
                pe.wait_ge(sq_used, KT * n.p)
                feature_sum(sq_sum)

            def begin(s, g, first=True):
                pe.wait_ge(lo_done, at(loop, lo_done, s + 1))
                if first and g >= 2:
                    pe.wait_ge(freed, at(loop, freed, g - 1))

            def eighth(s, g, kt, hi, lo, k0=0, cols=TOK, start=True, stop=True, tile=None):
                spans = [(0, HALF), (HALF, TOK)] if cols == TOK else [(0, cols)]
                for w, a in ((w_hi, hi), (w_lo, hi), (w_hi, lo)):
                    if tile is not None and w is w_hi:
                        ready = act_hi if a is hi else act_ready
                        pe.wait_ge(ready, at(loop, ready, tile + 1))
                    for h, (lo_c, hi_c) in enumerate(spans):
                        ins = pe.matmul(ps[:, 2 * (g % 2) + h, 0:hi_c - lo_c], w[:, s % 2, kt],
                                        a[:, k0 + kt, lo_c:hi_c],
                                        start=(start and kt == 0 and w is w_hi and a is hi),
                                        stop=(stop and kt == KT - 1 and a is lo), skip_group_check=True)
                if kt == KT - 1:
                    ins.then_inc(slab_done, 1)

            def projection(k0=KT, hi=big_hi, lo=big_lo, cols=TOK, fresh=False, each=None):
                begin(n.s, n.g)
                for kt in range(KT):
                    eighth(n.s, n.g, kt, hi, lo, k0, cols, tile=n.a + kt if fresh else None)
                    if each:
                        each(kt)
                n.s += 1
                n.g += 1
                if fresh:
                    n.a += KT

            def second_projection(*args):
                projection(*args, each=lambda kt: pre_sum(N_MEM if args and not n.q else TOK) if kt == KT // 2 else None)

            def memory_v(layer, h):
                pe.wait_ge(freed, MEM_SLABS * layer + MEM_H + h + 1)
                if MEM_H * layer + h >= 2:
                    pe.wait_ge(vm_done, MEM_H * layer + h - 1)
                for t in range(2):
                    ins = pe.transpose(ps[:, 4 + h % 2, t * P:(t + 1) * P], mv_t[:, h % 2, t * P:(t + 1) * P], mats[:, 0])
                ins.then_inc(mv_used, 1)

            pe.wait_ge(mats_arrived, 16)
            for layer in range(2):
                ops = (0, m_hi1, m_lo1, N_MEM) if layer else (0, m_hi, m_lo, N_MEM)
                if layer == 0:
                    projection(*ops, fresh=True)
                else:
                    pe.wait_ge(act_ready, n.a + KT + 6)
                    projection(*ops)
                for k in range(1, MEM_SLABS):
                    if k == (X_SUM_SLAB if layer else 1):
                        second_projection(*ops)
                    else:
                        projection(*ops)
                    if k > MEM_H:
                        memory_v(layer, k - MEM_H - 1)
                memory_v(layer, MEM_H - 1)
            pe.wait_ge(act_ready, 3 * KT)
            n.a = 3 * KT

            for k in range(KV_SLABS):
                projection()
            for b in range(BLOCKS):
                pe.wait_ge(freed, n.g)
                if b >= 2:
                    pe.wait_ge(va_done, b - 1)
                c0, c1 = block_cols(b)
                for k in range(2):
                    ins = pe.transpose(ps[0:c1 - c0, S_BANK + b % 2, k * P:(k + 1) * P], v_t[:, k, c0:c1], mats[:, 0])
                ins.then_inc(vt_done, 1)
            for j in range(QT):
                projection()
            g_q = n.g - QT

            def scores(t):
                n_, j, u = n.n + t, t // UNITS_J, t % UNITS_J
                if t == 0:
                    pe.wait_ge(cur_ready, at(loop, cur_ready, 1))
                if u == 0:
                    pe.wait_ge(freed, at(loop, freed, g_q + j + 1))
                if t >= 2:
                    pe.wait_ge(biased, at(loop, biased, n_ - 1))
                bank = S_BANK + t % 2
                if u == 0:
                    ins = pe.matmul(ps[:, bank, 0:P + DEC], q_s[:, j], k_cur[:, 0:P + DEC], start=True, stop=True)
                else:
                    e = (u - 1) // 2
                    for b in range(2):
                        i = 2 * ((u - 1) % 2) + b
                        keys = (DEC + i * P, DEC + (i + 2) * P)
                        c = 0
                        if i == 0:
                            keys, c = (P + DEC, P + DEC + P), P
                        ins = pe.matmul(ps[:, bank, b * 2 * P + c:(b + 1) * 2 * P],
                                        q_t[e * HD:(e + 1) * HD, j, DEC + i * P:DEC + (i + 1) * P],
                                        k_cur[e * HD:(e + 1) * HD, keys[0]:keys[1]], start=True, stop=True)
                ins.then_inc(s_done, 1)

            def transposes(t):
                n_, u = n.n + t, t % UNITS_J
                pe.wait_ge(normed, at(loop, normed, n_ + 1))
                if t >= 1:
                    pe.wait_ge(pt_done, at(loop, pt_done, n_))
                r = n_ % 4
                if u == 0:
                    pe.transpose(ps[:, T_BANK, 0:P], prob[:, r, 0, 0:P], mats[:, 0])
                    ins = pe.transpose(ps[0:DEC, T_BANK, P:2 * P], prob[:, r, 0, P:P + DEC], mats[:, 0])
                else:
                    tiles = [(0, 1), (1, 0), (1, 1)] if u % 2 else [(0, 0), (0, 1), (1, 0), (1, 1)]
                    for k, (b, key) in enumerate(tiles):
                        ins = pe.transpose(ps[:, T_BANK, k * P:(k + 1) * P], prob[:, r, b, key * P:(key + 1) * P], mats[:, 0])
                ins.then_inc(t_done, 1)

            def values(t):
                n_, j, u = n.n + t, t // UNITS_J, t % UNITS_J
                pe.wait_ge(pt_done, at(loop, pt_done, n_ + 1))
                r = n_ % 2
                if u == 0:
                    if t:
                        pe.wait_ge(o_done, at(loop, o_done, n.j + 2 * j))
                    o = ps[:, O_BANK, 0:2 * DEC]
                    pe.matmul(o, v_s[:, 0].rearrange("p a d -> p (a d)"), p_t[:, r, 0:P], start=True, stop=False)
                    ins = pe.matmul(o, v_s[0:DEC, 1].rearrange("p a d -> p (a d)"), p_t[0:DEC, r, P:2 * P], start=False, stop=True)
                else:
                    if u == 1:
                        pe.wait_ge(o_done, at(loop, o_done, n.j + 2 * j + 1))
                    e = (u - 1) // 2
                    o = ps[e * HD:(e + 1) * HD, O_BANK, :]
                    def product(v, a, b, p0, start):
                        return pe.matmul(o[:, a:b], v_cur[:, 2 + v], p_t[:, r, p0:p0 + b - a], start=start, stop=True,
                                         skip_group_check=True)
                    if u % 2:
                        product(0, 0, 2 * P, 0, True)
                        ins = product(1, P, 2 * P, 2 * P, False)
                    else:
                        product(1, 2 * P, 3 * P, 0, True)
                        product(2, 2 * P, 4 * P, P, False)
                        ins = product(3, 3 * P, 4 * P, 3 * P, False)
                ins.then_inc(v_done, 1)

            loop.per = ATT_PER
            with pe.Fori(0, KVH) as g:
                loop.i = g
                for kind, t in STEPS:
                    if kind == "S":
                        scores(t)
                    elif kind == "T":
                        transposes(t)
                    elif kind == "V":
                        values(t)
                    else:
                        if t % KT == 0:
                            begin(n.s + t // KT, n.g + t // KT)
                        eighth(n.s + t // KT, n.g + t // KT, t % KT, big_hi, big_lo, KT)
                loop.i = None
            n.s += KVH * QT
            n.g += KVH * QT
            n.n += KVH * UNITS
            n.j += 2 * KVH * QT

            def cross(q_src, km, vm, kms, vms):
                def scores(c):
                    n_, h, u = n.n + c, c // 3, c % 3
                    pe.wait_ge(exp_done, n_ - 1)
                    keys = km if u else kms
                    for b in range(2 if u else 1):
                        c0, c1 = block_cols(0 if u == 0 else 2 * u - 1 + b)
                        ins = pe.matmul(ps[0:c1 - c0, S_BANK + n_ % 2, b * N_MEM:(b + 1) * N_MEM], q_src[:, h, c0:c1],
                                        keys[:, h], start=True, stop=True)
                    ins.then_inc(s_done, 1)

                def transposes(c):
                    n_, u = n.n + c, c % 3
                    pe.wait_ge(normed, n_ + 1)
                    pe.wait_ge(pt_done, n_)
                    w = P if u else DEC
                    for key in range(2):
                        for b in range(2 if u else 1):
                            k = key * (2 if u else 1) + b
                            ins = pe.transpose(ps[:, T_BANK, k * w:(k + 1) * w], prob[0:w, n_ % 4, b, key * P:(key + 1) * P],
                                               mats[0:w, 0, 0:w])
                    ins.then_inc(t_done, 1)

                def values(c):
                    n_, h, u = n.n + c, c // 3, c % 3
                    pe.wait_ge(pt_done, n_ + 1)
                    pe.wait_ge(o_done, n.j + c)
                    w = 2 * P if u else DEC
                    v = vm if u else vms
                    for key in range(2):
                        ins = pe.matmul(ps[:, O_BANK, 0:w], v[:, key, h * P:(h + 1) * P],
                                        p_t[:, n_ % 2, key * w:(key + 1) * w], start=(key == 0), stop=(key == 1))
                    ins.then_inc(v_done, 1)

                pe.wait_ge(kms_in, 32 * (n.f + 1))
                pe.wait_ge(freed, n.g)
                for c in range(X_UNITS + LAG_PV):
                    if c < X_UNITS:
                        scores(c)
                    if 0 <= c - LAG_T < X_UNITS:
                        transposes(c - LAG_T)
                    if c >= LAG_PV:
                        values(c - LAG_PV)
                n.n += X_UNITS
                n.j += X_UNITS

            def out_projection():
                def group(m, s, g, fresh=False):
                    for part in range(2):
                        begin(s + part, g, first=(part == 0))
                        for kt in range(KT):
                            eighth(s + part, g, kt, big_hi, big_lo, KT * part, start=(part == 0), stop=(part == 1),
                                   tile=n.a + KT * part + kt if fresh else None)

                group(0, n.s, n.g, fresh=True)
                n.a += MIX_T
                group(1, n.s + 2, n.g + 1)
                loop.per = OUT_PER
                with pe.Fori(0, KT // 2 - 1) as i:
                    loop.i = i
                    for m in range(2, 4):
                        group(m, n.s + 2 * m, n.g + m)
                    loop.i = None
                n.s += OUT_SLABS
                n.g += KT
                post_sum()

            def ffn():
                def up(fresh=False):
                    for m in range(KT):
                        if m == 0 and fresh:
                            projection(fresh=True)
                        elif m == 1 and fresh:
                            second_projection()
                        else:
                            projection()

                def down(a, last=False):
                    for m in range(KT):
                        begin(n.s, n.g)
                        for kt in range(KT):
                            eighth(n.s, n.g, kt, big_hi, big_lo, 0, tile=a + kt if m == 0 else None)
                        n.s += 1
                        n.g += 1
                    if last:
                        post_sum()

                up(fresh=True)
                loop.per = FF_PER
                with pe.Fori(0, FF_CHUNKS - 1) as i:
                    loop.i = i
                    down(n.a)
                    up()
                    loop.i = None
                    n.s -= SLABS_FF
                    n.g -= SLABS_FF
                n.s += (FF_CHUNKS - 1) * SLABS_FF
                n.g += (FF_CHUNKS - 1) * SLABS_FF
                n.a += (FF_CHUNKS - 1) * KT
                down(n.a, last=True)
                n.a += KT

            cross(q_t, km0, vm0, kms, vms)
            n.f += 1
            out_projection()
            ffn()

            projection(fresh=True)
            for k in range(UT):
                projection() if k else second_projection()
                if k == 0:
                    pe.wait_ge(freed, n.g - 1)
                    for b in range(BLOCKS):
                        c0 = block_cols(b)[0]
                        ins = pe.transpose(ps[:, 4, b * 32:(b + 1) * 32], th[0:32, c0:c0 + P], mats[0:32, 0, 0:32])
                    ins.then_inc(dt_moved, 1)
                elif k == 3:
                    pe.wait_ge(dt_step, 6)
                    for m, mat in enumerate((2, 3, 1)):
                        pe.matmul(ps[:, 4 + m, 0:HEADS], mats[0:DEC, mat], hs[0:DEC, 1, 0], start=True, stop=True)
                        ins = pe.matmul(ps[:, 4 + m, HEADS:BLOCKS * HEADS], mats[:, mat],
                                        hs[:, 1, 1:].rearrange("p b h -> p (b h)"), start=True, stop=True)
                    ins.then_inc(dt_moved, 1)

            def turn(last):
                for kind, b in ssd_steps(last):
                    rows = DEC if b == 0 else P
                    c0, c1 = conv_cols(b) if kind not in "KGQN" else (0, 0)
                    if kind == "K":
                        if b % KT == 0:
                            begin(n.s + b // KT, n.g + b // KT)
                        eighth(n.s + b // KT, n.g + b // KT, b % KT, big_hi, big_lo, KT)
                    elif kind == "A":
                        if b == 0:
                            pe.wait_ge(u_done, at(loop, u_done, UT))
                            pe.wait_ge(groot_done, at(loop, groot_done, 0))
                        if b >= 2:
                            pe.wait_ge(xtok_done, at(loop, xtok_done, b - 1))
                            pe.wait_ge(cbm_done, at(loop, cbm_done, b - 1))
                        alone(pe)
                        bank = 4 + 2 * (b % 2)
                        for m in range(XT):
                            pe.transpose(ps[0:rows, bank, m * P:(m + 1) * P], u[:, m, c0:c1], mats[:, 0])
                        for m in range(2):
                            pe.transpose(ps[0:rows, bank + 1, m * P:(m + 1) * P], u[:, XT + m, c0:c1], mats[:, 0])
                        for m in range(2):
                            ins = pe.matmul(ps[0:rows, bank + 1, 2 * P + m * rows:2 * P + (m + 1) * rows], u[:, XT + m, c0:c1],
                                            u[:, XT + 2 + m, c0:c1], start=True, stop=True)
                        ins.then_inc(tok_done, 1)
                    elif kind == "seg":
                        pe.wait_ge(wseg_done, at(loop, wseg_done, b + 1))
                        if b == 0:
                            pe.wait_ge(xtok_done, at(loop, xtok_done, BLOCKS))
                            pe.wait_ge(cbm_done, at(loop, cbm_done, BLOCKS))
                        else:
                            pe.wait_ge(dec_done, at(loop, dec_done, b))
                            pe.wait_ge(state_done, at(loop, state_done, b))
                        alone(pe)
                        for m in range(2):
                            ins = pe.matmul(ps[0:rows, 4 + m, 0:3 * rows], mats[0:rows, 3, 0:rows],
                                            wseg[0:rows, 3 * m:3 * m + 3, 0:rows], start=True, stop=True)
                        ins.then_inc(seg_done, 1)
                    elif kind == "off" and b != 1:
                        if b == 0:
                            pe.wait_ge(h_loaded, at(loop, h_loaded, 16))
                            pe.wait_ge(c_done, at(loop, c_done, 1))
                        else:
                            pe.wait_ge(state_done, at(loop, state_done, b))
                        pe.wait_ge(yoff_done, at(loop, yoff_done, later(b) - 1))
                        alone(pe)
                        h = h_next if b == 0 else state[:, 1]
                        for m in range(2):
                            ins = pe.matmul(ps[0:rows, 7, m * 192:(m + 1) * 192], c_cur[:, m, c0:c1],
                                            h[:, m * 192:(m + 1) * 192], start=True, stop=True)
                        ins.then_inc(off_done, 1)
                    elif kind == "st":
                        pe.wait_ge(dec_done, at(loop, dec_done, b + 1))
                        pe.wait_ge(xd_done, at(loop, xd_done, b + 1))
                        alone(pe)
                        for m in range(2):
                            ins = pe.matmul(ps[:, 4, m * 192:(m + 1) * 192], btok[0:rows, b, m], xd[0:rows, 1, 3 * m:3 * m + 3],
                                            start=True, stop=True)
                        ins.then_inc(st_done, 1)
                    elif kind == "diag":
                        pe.wait_ge(decm_done, at(loop, decm_done, b + 1))
                        pe.wait_ge(y_done, at(loop, y_done, b))
                        alone(pe)
                        for h in range(PH):
                            ins = pe.matmul(ps[h % 2 * HD:(h % 2 + 1) * HD, 6, h // 2 * rows:(h // 2 + 1) * rows],
                                            xd[0:rows, 0, h], dec[0:rows, h, 0:rows], start=(h < 2), stop=False,
                                            skip_group_check=True)
                        ins.then_inc(diag_done, 1)
                    elif kind == "acc":
                        pe.wait_ge(ytok_done, at(loop, ytok_done, b + 1))
                        alone(pe)
                        for m in range(XT):
                            ins = pe.matmul(ps[:, 6, m * rows:(m + 1) * rows], ytok[0:rows, m * P:(m + 1) * P],
                                            mats[0:rows, 0, 0:rows], start=False, stop=True, skip_group_check=True)
                        ins.then_inc(acc_done, 1)
                    elif kind == "G":
                        pe.wait_ge(gsq_done, at(loop, gsq_done, 1))
                        pe.wait_ge(state_done, at(loop, state_done, BLOCKS))
                        for m in range(2):
                            for h in range(2):
                                c0, c1 = h * HALF, (h + 1) * HALF
                                o = ps[:, 4 + 2 * m + h, 0:HALF]
                                r0 = m * HD
                                alone(pe)
                                pe.matmul(o, mats[:, 1], gsq[:, 2 * m, c0:c1], start=True, stop=False)
                                ins = pe.matmul(o, mats[r0:r0 + HD, 1], gsq[r0:r0 + HD, 1, c0:c1], start=False, stop=True)
                        ins.then_inc(gsum_done, 1)

            loop.per = SSM_PER
            with pe.Fori(0, PAIRS - 1) as i:
                loop.i = i
                turn(False)
                loop.i = None
            loop.i = PAIRS - 1
            turn(True)
            loop.i = None
            n.s += (PAIRS - 1) * PAIR_SLABS + XT + CQ_SLABS
            n.g += (PAIRS - 1) * PAIR_SLABS + XT + CQ_SLABS
            pe.wait_ge(groot_done, at(loop, groot_done, PAIRS))
            cross(mix[:, MIX_T - MEM_H:], kvm1, vm1, kms1, vms1)
            out_projection()
            ffn()


        @block.vector
        def _(dve):
            loop, n = Loop(), Count()
            prime(dve, "vector")
            own = Own(dve, dve_self)

            def rest(dst, src, hi, w=None):
                dve.wait_ge(act_hi, at(loop, act_hi, n.a + 1))
                n.a += 1
                if w is None:
                    ins = dve.tensor_tensor(dst, src, hi.bitcast(F32), ALU.subtract)
                else:
                    ins = dve.scalar_tensor_tensor(out=dst, in0=src, scalar=par[:, w:w + 1], in1=hi.bitcast(F32),
                                                   op0=ALU.mult, op1=ALU.subtract)
                ins.then_inc(act_ready, 1)

            def norm_ready():
                n.c += 1
                dve.wait_ge(rstd_ready, n.c)

            def pre_add(width, cols=TOK):
                if width == KT // 2:
                    n.q += 1
                    dve.wait_ge(pre_sq, KT * n.q)
                else:
                    own.wait(loop)
                a, b = mix[:, KT:KT + width, 0:cols], mix[:, KT + width:KT + 2 * width, 0:cols]
                ins = dve.tensor_tensor(a, a, b, ALU.add)
                if width > 1:
                    own.mark(ins)
                else:
                    ins.then_inc(pre_added, 1)

            def pre_sum(cols=TOK):
                for width in PRE_WIDTHS:
                    pre_add(width, cols)

            def post_add(m):
                if m == 0:
                    return
                dve.wait_ge(sq_ready, at(loop, sq_ready, KT * n.p + m + 1))
                if m > 1:
                    dve.wait_ge(sq_used, at(loop, sq_used, KT * n.p + m))
                a = sq[:, 0] if m == 1 else sq_sum[:]
                dve.tensor_tensor(sq_sum[:], a, sq[:, m % 2], ALU.add).then_inc(sq_used, 2 if m == 1 else 1)

            def group(slabs_=1):
                n.s += slabs_
                dve.wait_ge(slab_done, at(loop, slab_done, n.s))
                b = 2 * (n.g % 2)
                n.g += 1
                return ps[:, b:b + 2, 0:HALF]

            def copy(dst, src):
                return dve.tensor_scalar(dst, src, 1.0, None, ALU.mult)

            def make_act(w, post):
                for m in range(KT + SCALE_AHEAD):
                    if m < KT:
                        dve.scalar_tensor_tensor(out=mix[:, m], in0=mix[:, m], scalar=par[:, post + m:post + m + 1],
                                                 in1=rstd[:, 0], op0=ALU.mult, op1=ALU.mult).then_inc(scaled, 1)
                    if m >= SCALE_AHEAD:
                        k = m - SCALE_AHEAD
                        rest(big_lo[:, KT + k], x[:, k], big_hi[:, KT + k], w + k)
                pre_sum()
                norm_ready()

            dve.wait_ge(const_in, 16)
            for layer in range(2):
                for m in range(KT if layer == 0 else 0):
                    if m in (0, 2):
                        dve.wait_ge(mem_arrived[m // 2], 16)
                    rest(m_lo[:, m], mraw[:, m], m_hi[:, m], C_MEM + m)
                if layer == 0:
                    pre_sum(N_MEM)
                    norm_ready()
                for k in range(MEM_SLABS):
                    src = group()[:, 0, 0:N_MEM]
                    h = k - MEM_H
                    if k < MEM_H:
                        dst = (kvm1 if layer else km0)[:, k]
                    else:
                        dst = mv_t[:, h % 2]
                        if MEM_H * layer + h >= 2:
                            dve.wait_ge(mv_used, MEM_H * layer + h - 1)
                    dve.tensor_tensor(dst, src, rm[:], ALU.mult).then_inc(freed, 1)
                    s = n.s + 1
                    if s < 2 * MEM_SLABS:
                        dve.wait_ge(hi_done, s + 1)
                        if s == 2:
                            dve.wait_ge(lo_done, 2)
                        dve.tensor_tensor(w_lo[:, s % 2], raw[:, s % 2], w_hi[:, s % 2].bitcast(F32), ALU.subtract).then_inc(lo_done, 1)
                    if layer and k < len(PRE_WIDTHS):
                        pre_add(PRE_WIDTHS[k])
                    for m in MEM_AHEAD[k] if layer == 0 else ():
                        rest(m_lo1[:, m], mraw[:, m], m_hi1[:, m], C_MEM + KT + m)
                    if layer == 0 and k:
                        if k in (1, 1 + KT // 2):
                            dve.wait_ge(x_arrived[k // (KT // 2)], 16)
                        rest(big_lo[:, KT + k - 1], x[:, k - 1], big_hi[:, KT + k - 1], C_MIX_PRE + k - 1)
                if layer == 0:
                    rest(big_lo[:, 2 * KT - 1], x[:, KT - 1], big_hi[:, 2 * KT - 1], C_MIX_PRE + KT - 1)
            norm_ready()

            for k in range(KVH):
                b = group()
                dve.tensor_tensor(k_all[:, k, P:P + HALF], b[:, 0], rstd[:, 1, 0:HALF], ALU.mult)
                dve.tensor_tensor(k_all[:, k, P + HALF:], b[:, 1], rstd[:, 1, HALF:], ALU.mult).then_inc(freed, 1)
            for k in range(2):
                dve.tensor_tensor(halves(v_t[:, k]), group(), halves(rstd[:, 1]), ALU.mult).then_inc(freed, 1)
            for b in range(BLOCKS):
                dve.wait_ge(vt_done, b + 1)
                rows = DEC if b == 0 else P
                src = ps[0:rows, S_BANK + b % 2, :]
                dve.tensor_copy(v_all[0:rows, 1 + b, 0:2, :], src[:, 0:P].rearrange("p (h d) -> p h d", h=2))
                dve.tensor_copy(v_all[0:rows, 1 + b, 2, :], src[:, P + HD:2 * P]).then_inc(va_done, 1)

            def query_tile(j, dst, sample=None):
                src, scale = group(), float(HD) ** -0.5
                for e in range(2 if sample is not None else 0):
                    half = slice(e * HD, (e + 1) * HD)
                    dve.scalar_tensor_tensor(out=sample[half, e * DEC:(e + 1) * DEC], in0=src[half, 0, 0:DEC], scalar=scale,
                                             in1=rstd[half, 1, 0:DEC], op0=ALU.mult, op1=ALU.mult)
                dve.scalar_tensor_tensor(out=halves(dst), in0=src, scalar=scale,
                                         in1=halves(rstd[:, 1]), op0=ALU.mult, op1=ALU.mult).then_inc(freed, 1)

            own.mark(dve.memset(q_s[:], 0.0))
            own.wait(loop)
            for j in range(QT - 1):
                query_tile(j, q_t[:, j], q_s[:, j])
            dve.wait_ge(cache_in, 32)

            def bias_max(t):
                n_, j, u = n.n + t, t // UNITS_J, t % UNITS_J
                r, bank = n_ % 4, S_BANK + t % 2
                dve.wait_ge(s_done, at(loop, s_done, n_ + 1))
                if u == 0:
                    dve.wait_ge(bias_in[j % 2], at(loop, bias_in[j % 2], 16 * (j // 2 + 1)))
                if t >= 4:
                    dve.wait_ge(t_done, at(loop, t_done, n_ - 3))
                alone(dve)
                for b in range(2):
                    if u == 0:
                        half, e, k, c0, c1, d = slice(b * DEC, (b + 1) * DEC), b, 0, 0, P + DEC, b * DEC
                    else:
                        half, e, k, c0, c1, d = slice(0, P), (u - 1) // 2, b, P if u % 2 and b == 0 else 0, 2 * P, 0
                    ins = dve.tensor_tensor_reduce(prob[half, r, k, c0:c1], ps[half, bank, k * 2 * P + c0:k * 2 * P + c1],
                                                   bias[half, j % 2, e, c0 + d:c1 + d], 1.0,
                                                   sink_cur[half, 2 * j + e:2 * j + e + 1], ALU.add, ALU.max,
                                                   stat[half, r, 0, k:k + 1])
                ins.then_inc(biased, 1)
                sums = 2 if u else 1
                dve.wait_ge(biased, at(loop, biased, n_ + 1))
                dve.tensor_scalar(stat[:, r, 1, 0:sums], stat[:, r, 0, 0:sums], -1.0, None, ALU.mult).then_inc(max_done, 1)

            def normalise(n_, rows, parts, sink=True, sums=2):
                r = n_ % 4
                dve.wait_ge(exp_done, at(loop, exp_done, n_ + 1))
                total = stat[0:rows, r, 2, 0:sums]
                if sink:
                    own.mark(dve.tensor_tensor(total, total, stat[0:rows, r, 3, 0:sums], ALU.add))
                    own.wait(loop)
                own.mark(dve.reciprocal(total, total))
                own.wait(loop)
                for b, c0, c1 in parts:
                    ap = prob[0:rows, r, b, c0:c1]
                    ins = dve.tensor_scalar(ap, ap, stat[0:rows, r, 2, b:b + 1], None, ALU.mult)
                ins.then_inc(normed, 1)

            def norm(t):
                u = t % UNITS_J
                if u == 0:
                    normalise(n.n + t, P, [(0, 0, P + DEC)], sums=1)
                else:
                    normalise(n.n + t, P, [(0, P if u % 2 else 0, 2 * P), (1, 0, 2 * P)])

            ATT_PER["dve_self"] = 2 * UNITS
            loop.per = ATT_PER
            with dve.Fori(0, KVH) as g:
                loop.i = g
                k_g = k_all[:, bass.ds(g, 1), :].rearrange("p h c -> p (h c)")
                v_g = v_all[:, :, bass.ds(g, 1), :].rearrange("p b h d -> p b (h d)")
                copy(k_cur[:], k_g)
                for e in range(2):
                    copy(v_s[:, 0, e], v_g[:, 0])
                    copy(v_s[0:DEC, 1, e], v_g[0:DEC, 1])
                copy(v_cur[:, 2:], v_g[:, 2:])
                copy(sink_cur[:], par[:, bass.ds(g * GROUP + C_SINK, GROUP)]).then_inc(cur_ready, 1)
                dve.wait_ge(cur_ready, at(loop, cur_ready, 1))
                start = own.n
                query_tile(QT - 1, q_t[:, QT - 1], q_s[:, QT - 1])
                for kind, t in STEPS:
                    if kind == "S":
                        bias_max(t)
                        if t:
                            norm(t - 1)
                    elif kind == "T" and t == UNITS - LAG_T:
                        norm(UNITS - 1)
                    elif kind == "K" and t % KT == KT - 1 and t // KT < QT - 1:
                        query_tile(t // KT, q_t[:, t // KT], q_s[:, t // KT])
                    elif kind == "V" and t % UNITS_J in (0, UNITS_J - 1):
                        dve.wait_ge(v_done, at(loop, v_done, n.n + t + 1))
                        dst = mix[:, bass.ds(g * QT + t // UNITS_J, 1)].rearrange("p t c -> p (t c)")
                        if t % UNITS_J:
                            copy(dst[:, DEC:TOK], ps[:, O_BANK]).then_inc(o_done, 1)
                            continue
                        copy(dst[0:HD, 0:DEC], ps[0:HD, O_BANK, 0:DEC])
                        copy(dst[HD:P, 0:DEC], ps[HD:P, O_BANK, DEC:2 * DEC]).then_inc(o_done, 1)
                loop.i = None
                assert own.n - start == ATT_PER["dve_self"]
                n.s -= QT
                n.g -= QT
            own.n += (KVH - 1) * ATT_PER["dve_self"]
            n.s += KVH * QT
            n.g += KVH * QT
            n.n += KVH * UNITS
            query_tile(QT - 1, q_t[:, QT - 1])
            for i in range(2):
                dve.wait_ge(bias_in[i], 16 * (KVH * QT // 2 + 1))

            def cross():
                def maximum(c):
                    n_, u = n.n + c, c % 3
                    rows, r, blocks = P if u else DEC, n_ % 4, 2 if u else 1
                    dve.wait_ge(s_done, n_ + 1)
                    own.mark(dve.tensor_reduce(stat[0:rows, r, 0, 0:blocks],
                                               ps[0:rows, S_BANK + n_ % 2, 0:blocks * N_MEM].rearrange("p (b c) -> p b c", b=blocks),
                                               AX.X, ALU.max))
                    own.wait(loop)
                    dve.tensor_scalar(stat[0:rows, r, 1, 0:blocks], stat[0:rows, r, 0, 0:blocks], -X_SCALE, None,
                                      ALU.mult).then_inc(max_done, 1)

                for c in range(X_UNITS + LAG_PV + 1):
                    if c > LAG_PV:
                        k = c - LAG_PV - 1
                        h, u = k // 3, k % 3
                        dve.wait_ge(v_done, n.n + k + 1)
                        c0, c1 = (0, DEC) if u == 0 else (DEC + (u - 1) * 2 * P, DEC + u * 2 * P)
                        dve.tensor_copy(mix[:, MIX_T - MEM_H + h, c0:c1], ps[:, O_BANK, 0:c1 - c0]).then_inc(o_done, 1)
                    if c < X_UNITS:
                        maximum(c)
                    if 1 <= c <= X_UNITS:
                        u = (c - 1) % 3
                        normalise(n.n + c - 1, P if u else DEC, [(b, 0, 2 * P) for b in range(2 if u else 1)], False,
                                  2 if u else 1)
                n.n += X_UNITS

            def out_projection(layer):
                for k in range(MIX_T):
                    rest(big_lo[:, k], mix[:, k], big_hi[:, k], norm_weight(layer, k))

                def one(m, dst):
                    src = group(2)
                    dve.wait_ge(sq_ready, at(loop, sq_ready, KT * n.p + m + 1))
                    post_add(m)
                    copy(halves(dst), src).then_inc(freed, 1)

                for m in range(2):
                    one(m, mix[:, m])
                loop.per = OUT_PER
                with dve.Fori(0, KT // 2 - 1) as i:
                    loop.i = i
                    for m in range(2, 4):
                        one(m, mix[:, bass.ds(i * 2 + m, 1), :].rearrange("p t c -> p (t c)"))
                    loop.i = None
                    n.s -= 4
                    n.g -= 2
                n.s += OUT_SLABS - 4
                n.g += KT - 2
                n.p += 1
                norm_ready()

            def ffn():
                def up():
                    for m in range(KT + 1):
                        if m < KT:
                            src = group()
                            if m >= 2:
                                dve.wait_ge(hid_done, at(loop, hid_done, n.x + m - 1))
                                dve.wait_ge(act_hi, at(loop, act_hi, n.a - (1 if m else 0)))
                            dve.scalar_tensor_tensor(out=halves(relu[:, m % 2]), in0=src, scalar=0.0,
                                                     in1=halves(rstd[:, 1]), op0=ALU.max, op1=ALU.mult).then_inc(freed, 1)
                        if m:
                            dve.wait_ge(hid_done, at(loop, hid_done, n.x + m))
                            rest(big_lo[:, m - 1], hid[:, (m - 1) % 2], big_hi[:, m - 1])

                def down(last=False):
                    for m in range(KT):
                        src = group()
                        if m == 0:
                            dve.wait_ge(zeroed, 1 + KT * (n.f + 1))
                        dve.wait_ge(freed, at(loop, freed, n.g - 1))
                        dve.tensor_tensor(halves(mix[:, m]), src, halves(mix[:, m]), ALU.add).then_inc(freed, 1)
                        if last and m:
                            post_add(m - 1)
                    if last:
                        post_add(KT - 1)

                up()
                n.x += KT
                loop.per = FF_PER
                with dve.Fori(0, FF_CHUNKS - 1) as i:
                    loop.i = i
                    down()
                    up()
                    loop.i = None
                    n.s -= SLABS_FF
                    n.g -= SLABS_FF
                    n.a -= KT
                n.s += (FF_CHUNKS - 1) * SLABS_FF
                n.g += (FF_CHUNKS - 1) * SLABS_FF
                n.a += (FF_CHUNKS - 1) * KT
                n.x += (FF_CHUNKS - 1) * KT
                down(last=True)
                n.p += 1
                n.f += 1
                norm_ready()

            cross()
            out_projection(0)
            make_act(C_FF_PRE, C_MIX_POST)
            ffn()
            make_act(C_MIX_PRE + KT, C_FF_POST)

            src = group()
            dve.tensor_tensor(halves(th[0:32, 0:TOK]), src[0:32], halves(rstd[0:32, 1]), ALU.mult)
            for k in range(2):
                ins = dve.memset(xp[:, k, PAST + DEC:PAST + DEC + PAST], 0.0)
            ins.then_inc(freed, 1)

            def pair_par(gp):
                p = par[:, bass.ds(gp * (UT * TAPS) + C_CONV, UT * TAPS)].rearrange("p (t c) -> p t c", t=UT)
                dve.tensor_scalar(cpar[:, :, 0:CONV_W + 1], p[:, :, 0:CONV_W + 1], 0.5, None, ALU.mult)
                return copy(cpar[:, :, CONV_W + 1:], p[:, :, CONV_W + 1:])

            def slab_end(tiles, k):
                kind, t = tiles[k]
                if kind == "q":
                    query_tile(t, mix[:, MIX_T - MEM_H + t])
                    if t == 0:
                        silu(tiles, k - 1)
                    return
                src = group()
                if kind == "u":
                    if n.k or t >= 2:
                        dve.wait_ge(conv_done, at(loop, conv_done, 3 * (n.k + max(t - 1, 0))))
                        dve.wait_ge(tails_done, at(loop, tails_done, n.k + max(t - 1, 0)))
                    alone(dve)
                    x_ = xp[:, t % 2]
                    copy(x_[:, 0:PAST], cpar[:, t, CONV_W + 1:])
                    dve.tensor_tensor(x_[:, PAST:PAST + DEC], src[:, 0, 0:DEC], rstd[:, 1, 0:DEC], ALU.mult)
                    dve.tensor_tensor(x_[:, 2 * PAST + DEC:2 * PAST + HALF], src[:, 0, DEC:], rstd[:, 1, DEC:HALF], ALU.mult)
                    dve.tensor_tensor(x_[:, 2 * PAST + HALF:], src[:, 1], rstd[:, 1, HALF:], ALU.mult).then_inc(freed, 1)
                else:
                    if t == 0:
                        dve.wait_ge(gated_done, at(loop, gated_done, 0))
                        alone(dve)
                    dve.scalar_tensor_tensor(out=halves(zs[:, t]), in0=src, scalar=0.5, in1=halves(rstd[:, 1]),
                                             op0=ALU.mult, op1=ALU.mult).then_inc(freed, 1)
                if k:
                    silu(tiles, k - 1)
                if kind == "u":
                    dve.wait_ge(tap_done, at(loop, tap_done, n.k + t + 1))
                    for j in range(1, CONV_W):
                        if j > 1:
                            dve.wait_ge(conv_done, at(loop, conv_done, 3 * (n.k + t) + j - 1))
                        dve.scalar_tensor_tensor(out=u[:, t], in0=xp[:, t % 2, j:j + UC], scalar=cpar[:, t, j:j + 1],
                                                 in1=u[:, t], op0=ALU.mult, op1=ALU.add).then_inc(conv_done, 1)

            def silu(tiles, k):
                kind, t = tiles[k]
                dve.wait_ge(tanh_done, at(loop, tanh_done, n.k + k + 1))
                dst, w = (u[:, t], UC) if kind == "u" else (zs[:, t], TOK)
                dve.scalar_tensor_tensor(out=dst, in0=th[:, 0:w], scalar=1.0, in1=dst, op0=ALU.add, op1=ALU.mult).then_inc(u_done, 1)

            n.k = 0
            own.mark(pair_par(0))
            own.wait(loop)
            for k in range(UT):
                slab_end(FIRST_TILES, k)
                if k == 0:
                    dve.wait_ge(dt_moved, 1)
                    dve.tensor_tensor(dts[:, 0], ps[:, 4, 0:BLOCKS * 32].rearrange("p (b h) -> p b h", b=BLOCKS)[:, :, 0:HEADS],
                                      par[:, C_DTB:C_DTB + HEADS].unsqueeze(1).to_broadcast([P, BLOCKS, HEADS]), ALU.add).then_inc(dt_step, 1)
                    dve.wait_ge(dt_step, 1)
                    dve.scalar_tensor_tensor(out=dts[:, 1], in0=dts[:, 0], scalar=-1.0, in1=dts[:, 0], op0=ALU.mult,
                                             op1=ALU.min).then_inc(dt_step, 1)
                    dve.tensor_scalar(hs[:, 0], dts[:, 0], 0.0, None, ALU.max).then_inc(dt_step, 1)
                elif k == 1:
                    dve.wait_ge(dt_fn, 2)

                    def then(ins):
                        own.mark(ins)
                        own.wait(loop)

                    v, t, sq_t, poly = (dts[:, m] for m in (1, 1, 2, 3))
                    then(dve.tensor_scalar(sq_t, v, 2.0, None, ALU.add))
                    then(dve.reciprocal(sq_t, sq_t))
                    then(dve.tensor_tensor(t, v, sq_t, ALU.mult))
                    then(dve.tensor_tensor(sq_t, t, t, ALU.mult))
                    then(dve.tensor_scalar(poly, sq_t, 1.0 / (2 * ARTANH_TERMS + 1), None, ALU.mult))
                    for m in range(ARTANH_TERMS - 1, 0, -1):
                        then(dve.scalar_tensor_tensor(out=poly, in0=poly, scalar=1.0 / (2 * m + 1), in1=sq_t,
                                                      op0=ALU.add, op1=ALU.mult))
                    then(dve.scalar_tensor_tensor(out=poly, in0=poly, scalar=1.0, in1=t, op0=ALU.add, op1=ALU.mult))
                    dve.scalar_tensor_tensor(out=hs[:, 0], in0=poly, scalar=2.0, in1=hs[:, 0], op0=ALU.mult,
                                             op1=ALU.add).then_inc(dt_step, 1)
                    dve.wait_ge(dt_step, 4)
                    dve.tensor_tensor(hs[:, 1], hs[:, 0], ea[:].unsqueeze(1).to_broadcast([P, BLOCKS, HEADS]),
                                      ALU.mult).then_inc(dt_step, 1)
                    dve.wait_ge(dt_step, 5)
                    dve.tensor_scalar(hs[:, 1], hs[:, 1], -1.0, None, ALU.mult).then_inc(dt_step, 1)
                elif k == 3:
                    dve.wait_ge(dt_fn, 3)
                    dve.tensor_tensor(hs[:, 3], hs[:, 3], hs[:, 0], ALU.mult).then_inc(dt_step, 1)
            silu(FIRST_TILES, UT - 1)
            dve.wait_ge(dt_step, 7)

            def turn(gp, last):
                dve.wait_ge(ytok_done, at(loop, ytok_done, 0))
                dve.wait_ge(y_done, at(loop, y_done, 0))
                dve.wait_ge(tap_done, at(loop, tap_done, UT))
                dve.wait_ge(conv_done, at(loop, conv_done, 3 * UT))
                alone(dve)
                hv = hs[:].rearrange("p k b h -> p (k b) h")
                copy(heads_cur[:].rearrange("p k b h -> p (k b) h"), hv[:, :, bass.ds(gp * PH, PH)])
                if not last:
                    pair_par(gp + 1)
                copy(skips[:], par[:, bass.ds(gp * N_PAIR + (C_PAIR + XT), PH)]).then_inc(cur_done, 1)
                dve.wait_ge(cur_done, at(loop, cur_done, 1))
                for kind, b in ssd_steps(last):
                    rows = DEC if b == 0 else P
                    if kind == "K":
                        if b % KT == KT - 1:
                            slab_end(turn_tiles(last), b // KT)
                    elif kind == "A":
                        dve.wait_ge(tok_done, at(loop, tok_done, b + 1))
                        if b == 0:
                            dve.wait_ge(st_done, at(loop, st_done, 0))
                            dve.wait_ge(decm_done, at(loop, decm_done, 0))
                        bank = 5 + 2 * (b % 2)
                        copy(btok[0:rows, b], ps[0:rows, bank, 0:2 * P].rearrange("p (g c) -> p g c", g=2))
                        dve.tensor_tensor(cbm[0:rows, b, :, 0:rows],
                                          ps[0:rows, bank, 2 * P:2 * P + 2 * rows].rearrange("p (g c) -> p g c", g=2),
                                          mats[0:rows, 2, 0:rows].unsqueeze(1).to_broadcast([rows, 2, rows]),
                                          ALU.mult).then_inc(cbm_done, 1)
                    elif kind == "seg":
                        dve.wait_ge(dec_done, at(loop, dec_done, b + 1))
                        if b == 0:
                            dve.wait_ge(cbm_done, at(loop, cbm_done, BLOCKS))
                        alone(dve)
                        d = dec[0:rows, :, 0:rows].rearrange("p (g h) q -> p g h q", g=2)
                        dve.tensor_tensor(d, d, cbm[0:rows, b, :, 0:rows].unsqueeze(2).to_broadcast([rows, 2, 3, rows]),
                                          ALU.mult).then_inc(decm_done, 1)
                    elif kind == "off" and b != 1:
                        dve.wait_ge(off_done, at(loop, off_done, later(b)))
                        dve.wait_ge(acc_done, at(loop, acc_done, b))
                        alone(dve)
                        dve.tensor_tensor(ytok[0:rows].rearrange("p (h d) -> p h d", h=PH),
                                          ps[0:rows, 7, 0:PH * HD].rearrange("p (h d) -> p h d", h=PH),
                                          heads_cur[0:rows, 2, b].unsqueeze(2).to_broadcast([rows, PH, HD]),
                                          ALU.mult).then_inc(yoff_done, 1)
                    elif kind == "st":
                        dve.wait_ge(st_done, at(loop, st_done, b + 1))
                        dve.wait_ge(state_done, at(loop, state_done, b))
                        if b == 0:
                            dve.wait_ge(h_stored, at(loop, h_stored, 0))
                        if b != 1:
                            dve.wait_ge(hbd_done, at(loop, hbd_done, later(b)))
                        alone(dve)
                        dst, new = state[:, min(b, 1)], ps[:, 4, 0:PH * HD]
                        (copy(dst, new) if b == 1 else dve.tensor_tensor(dst, hbd, new, ALU.add)).then_inc(state_done, 1)
                    elif kind == "acc":
                        dve.wait_ge(acc_done, at(loop, acc_done, b + 1))
                        if b == 0:
                            dve.wait_ge(gnorm_done, at(loop, gnorm_done, 0))
                        alone(dve)
                        c0, c1 = block_cols(b)
                        copy(mix[:, YG:YG + XT, c0:c1], ps[:, 6, 0:XT * rows].rearrange("p (t c) -> p t c", t=XT)).then_inc(y_done, 1)
                    elif kind == "Q":
                        dve.wait_ge(y_done, at(loop, y_done, BLOCKS))
                        dve.wait_ge(u_done, at(loop, u_done, UT + XT))
                        alone(dve)
                        dve.tensor_tensor(mix[:, YG:YG + XT], mix[:, YG:YG + XT], zs[:], ALU.mult).then_inc(gated_done, 1)
                    elif kind == "N":
                        dve.wait_ge(grec_done, at(loop, grec_done, 1))
                        alone(dve)
                        for m, k, r0, r1 in ((0, 0, 0, P), (1, 0, 0, HD), (1, 1, HD, P), (2, 1, 0, P)):
                            dst = mix[r0:r1, bass.ds(gp * XT + m, 1), :].rearrange("p t c -> p (t c)")
                            ins = dve.tensor_tensor(dst, mix[r0:r1, YG + m], grs[r0:r1, k], ALU.mult)
                        ins.then_inc(gnorm_done, 1)
                if not last:
                    silu(turn_tiles(last), PAIR_SLABS - 1)

            loop.per = SSM_PER
            n.k = UT
            with dve.Fori(0, PAIRS - 1) as i:
                loop.i = i
                turn(i, False)
                loop.i = None
                n.s -= PAIR_SLABS
                n.g -= PAIR_SLABS
            loop.i = PAIRS - 1
            turn(PAIRS - 1, True)
            loop.i = None
            n.s += (PAIRS - 1) * PAIR_SLABS
            n.g += (PAIRS - 1) * PAIR_SLABS
            cross()
            out_projection(1)
            make_act(C_FF_PRE + KT, C_MIX_POST + KT)
            ffn()
            for m in range(KT):
                ins = dve.scalar_tensor_tensor(out=mix[:, m], in0=mix[:, m], scalar=par[:, C_FF_POST + KT + m:C_FF_POST + KT + m + 1],
                                               in1=rstd[:, 0], op0=ALU.mult, op1=ALU.mult)
                if m < Y_POOL:
                    ins.then_inc(scaled, 1)
                    continue
                own.mark(ins)
                own.wait(loop)
                dve.tensor_tensor(x[:, m], x[:, m], mix[:, m], ALU.add).then_inc(y_added, 1)


        @block.gpsimd
        def _(pool):
            loop, n = Loop(), Count()
            prime(pool, "gpsimd")

            def split_lo(s):
                if s >= ALL_SLABS:
                    return
                pool.wait_ge(hi_done, at(loop, hi_done, s + 1))
                pool.tensor_tensor(w_lo[:, s % 2], raw[:, s % 2], w_hi[:, s % 2].bitcast(F32), ALU.subtract).then_inc(lo_done, 1)

            def slabs_lo(count, turns=1):
                if turns == 1:
                    for k in range(count):
                        split_lo(n.s + k)
                else:
                    loop.per = {"hi_done": count}
                    with pool.Fori(0, turns) as i:
                        loop.i = i
                        for k in range(count):
                            split_lo(n.s + k)
                        loop.i = None
                n.s += count * turns

            def add_post(clear, tiles=KT):
                for m in range(tiles):
                    pool.wait_ge(scaled, KT * n.x + m + 1)
                    pool.tensor_tensor(x[:, m], x[:, m], mix[:, m], ALU.add).then_inc(x_done, 1)
                n.x += 1
                if clear:
                    pool.wait_ge(x_done, KT * n.x)
                    for m in range(KT):
                        pool.memset(mix[:, m], 0.0).then_inc(zeroed, 1)

            def ffn():
                def up():
                    for m in range(KT):
                        split_lo(n.s)
                        n.s += 1
                        n.g += 1
                        pool.wait_ge(freed, at(loop, freed, n.g))
                        if m >= 2:
                            pool.wait_ge(act_ready, at(loop, act_ready, n.a + m - 1))
                        pool.tensor_tensor(hid[:, m % 2], relu[:, m % 2], relu[:, m % 2], ALU.mult).then_inc(hid_done, 1)
                    n.a += KT

                def down():
                    for m in range(KT):
                        split_lo(n.s)
                        n.s += 1
                        n.g += 1

                up()
                loop.per = FF_PER
                with pool.Fori(0, FF_CHUNKS - 1) as i:
                    loop.i = i
                    down()
                    up()
                    loop.i = None
                    n.s -= SLABS_FF
                    n.g -= SLABS_FF
                    n.a -= KT
                n.s += (FF_CHUNKS - 1) * SLABS_FF
                n.g += (FF_CHUNKS - 1) * SLABS_FF
                n.a += (FF_CHUNKS - 1) * KT
                down()

            pool.memset(eps[:], EPS).then_inc(zeroed, 1)
            slabs_lo(2)
            n.s = 2 * MEM_SLABS
            pool.wait_ge(lo_done, n.s)
            slabs_lo(2)
            slabs_lo(KV_SLABS + QT)
            slabs_lo(QT, KVH)
            slabs_lo(4, OUT_SLABS // 4)
            add_post(True)
            n.a = 3 * KT + MIX_T + KT
            n.g = 2 * MEM_SLABS + ATTN_SLABS + KT
            ffn()
            add_post(False)

            def slab_end(k, gp):
                split_lo(n.s)
                n.s += 1
                n.g += 1
                if k is None:
                    return
                pool.wait_ge(freed, at(loop, freed, n.g))
                alone(pool)
                for m, c in enumerate((DEC, UC)):
                    dst = tails[:].rearrange("p g t m c -> p g (t m c)")[:, bass.ds(gp, 1), (k * 2 + m) * PAST:(k * 2 + m + 1) * PAST]
                    ins = pool.tensor_copy(dst.rearrange("p g c -> p (g c)"), xp[:, k % 2, c:c + PAST])
                ins.then_inc(tails_done, 1)

            slab_end(None, None)
            for k in range(UT):
                slab_end(k, 0)

            def wide(ap, rows):
                return ap.unsqueeze(2).to_broadcast([rows, PH, HD])

            def turn(gp, last):
                def sums(b):
                    rows = DEC if b == 0 else P
                    if b == 0:
                        pool.wait_ge(cur_done, at(loop, cur_done, 1))
                        pool.wait_ge(gnorm_done, at(loop, gnorm_done, 0))
                    pool.wait_ge(seg_done, at(loop, seg_done, b))
                    alone(pool)
                    pool.tensor_tensor(wseg[0:rows, :, 0:rows], mats[0:rows, 2, 0:rows].unsqueeze(1).to_broadcast([rows, PH, rows]),
                                       heads_cur[0:rows, 1, b].unsqueeze(2).to_broadcast([rows, PH, rows]),
                                       ALU.mult).then_inc(wseg_done, 1)

                def scaled_x(b):
                    rows = DEC if b == 0 else P
                    pool.wait_ge(xtok_done, at(loop, xtok_done, b + 1))
                    pool.wait_ge(diag_done, at(loop, diag_done, b))
                    pool.wait_ge(ytok_done, at(loop, ytok_done, b))
                    alone(pool)
                    xb = xtok[0:rows, b].rearrange("p (h d) -> p h d", h=PH)
                    if b != 1:
                        pool.tensor_tensor(xd[0:rows, 2], xb, wide(skips[0:rows], rows), ALU.mult)
                    pool.tensor_tensor(xd[0:rows, 1], xb, wide(heads_cur[0:rows, 3, b], rows), ALU.mult)
                    pool.tensor_tensor(xd[0:rows, 0], xb, wide(heads_cur[0:rows, 0, b], rows), ALU.mult).then_inc(xd_done, 1)

                for kind, b in ssd_steps(last):
                    rows = DEC if b == 0 else P
                    if kind == "K":
                        if b % KT == KT - 1:
                            tile, t = turn_tiles(last)[b // KT]
                            slab_end(t if tile == "u" else None, gp + 1)
                    elif kind == "A" and b == 0:
                        sums(0)
                    elif kind == "A" and b == 1:
                        scaled_x(0)
                    elif kind == "seg":
                        if b != 1:
                            if b == 0:
                                pool.wait_ge(h_loaded, at(loop, h_loaded, 16))
                            pool.wait_ge(state_done, at(loop, state_done, b))
                            alone(pool)
                            h = (h_next[:] if b == 0 else state[:, 1]).rearrange("p (h d) -> p h d", h=PH)
                            pool.tensor_tensor(hbd.rearrange("p (h d) -> p h d", h=PH), h, wide(heads_cur[:, 4, b], P),
                                               ALU.mult).then_inc(hbd_done, 1)
                        if b < BLOCKS - 1:
                            sums(b + 1)
                    elif kind == "diag":
                        y = ytok[0:rows].rearrange("p (h d) -> p h d", h=PH)
                        if b == 1:
                            pool.wait_ge(acc_done, at(loop, acc_done, b))
                            alone(pool)
                            pool.tensor_tensor(y, xtok[0:rows, b].rearrange("p (h d) -> p h d", h=PH), wide(skips[0:rows], rows),
                                               ALU.mult).then_inc(ytok_done, 1)
                        else:
                            pool.wait_ge(yoff_done, at(loop, yoff_done, later(b)))
                            pool.wait_ge(xd_done, at(loop, xd_done, b + 1))
                            alone(pool)
                            pool.tensor_tensor(y, y, xd[0:rows, 2], ALU.add).then_inc(ytok_done, 1)
                        if b < BLOCKS - 1:
                            scaled_x(b + 1)

            loop.per = SSM_PER
            with pool.Fori(0, PAIRS - 1) as i:
                loop.i = i
                turn(i, False)
                loop.i = None
                n.s -= PAIR_SLABS
                n.g -= PAIR_SLABS
            loop.i = PAIRS - 1
            turn(PAIRS - 1, True)
            loop.i = None
            n.s += (PAIRS - 1) * PAIR_SLABS
            n.g += (PAIRS - 1) * PAIR_SLABS + KT
            slabs_lo(4, OUT_SLABS // 4)
            add_post(True)
            n.a += KT + MIX_T + KT
            ffn()
            add_post(False, Y_POOL)


        @block.sync
        def _(sp):
            loop, n = Loop(), Count()
            prime(sp, "sync")
            sp.dma_start(par[:], par_in).then_inc(const_in, 16)
            sp.dma_start(mraw[:, 0:2], mem_in[:, 0:2]).then_inc(mem_arrived[0], 16)

            def load_slab(src, s):
                if s >= 2:
                    sp.wait_ge(lo_done, at(loop, lo_done, s - 1))
                sp.dma_start(raw[:, s % 2].rearrange("p k c -> p (k c)"), src).then_inc(raw_in[s % 2], 16)

            def load_slabs(count, turns=1):
                if turns == 1:
                    for _ in range(count):
                        load_slab(slabs[n.s], n.s)
                        n.s += 1
                    return
                loop.per = {"lo_done": count}
                with sp.Fori(0, turns) as i:
                    for k in range(count):
                        src = slabs[bass.ds(sp.snap(i * count + (n.s + k)), 1)].rearrange("s p c -> (s p) c")
                        loop.i = i
                        load_slab(src, n.s + k)
                        loop.i = None
                n.s += count * turns

            load_slabs(1)
            sp.dma_start(mraw[:, 2:], mem_in[:, 2:]).then_inc(mem_arrived[1], 16)
            sp.dma_start(mats[:], mats_in).then_inc(mats_arrived, 16)
            load_slabs(3)
            sp.dma_start(x[:, 0:KT // 2], x_in[:, 0:KT // 2]).then_inc(x_arrived[0], 16)
            load_slabs(2)
            sp.dma_start(x[:, KT // 2:], x_in[:, KT // 2:]).then_inc(x_arrived[1], 16)
            load_slabs(2)
            load_slabs(4, 2)
            load_slabs(2)
            sp.wait_ge(slab_done, 2 * MEM_SLABS)
            sp.wait_ge(mv_used, 2 * MEM_H)
            sp.dma_start(k_all[:, :, 0:P], ck_in).then_inc(cache_in, 16)
            sp.dma_start(v_all[:, 0], cv_in).then_inc(cache_in, 16)
            load_slabs(2)
            sp.dma_start(kms[:], mk_in[0]).then_inc(kms_in, 16)
            sp.dma_start(vms[:], mv_in[0]).then_inc(kms_in, 16)
            load_slabs(KV_SLABS + QT - 2)
            for j in range(2):
                sp.dma_start(bias[:, j], alibi[j]).then_inc(bias_in[j], 16)
            loop.per = ATT_PER
            with sp.Fori(0, KVH) as g:
                for j in range(QT):
                    tables = alibi[bass.ds(sp.snap(g * QT + (j + 2)), 1)].rearrange("t p e c -> (t p) e c")
                    src = slabs[bass.ds(sp.snap(g * QT + (n.s + j)), 1)].rearrange("s p c -> (s p) c")
                    loop.i = g
                    load_slab(src, n.s + j)
                    sp.wait_ge(biased, at(loop, biased, UNITS_J * (j + 1)))
                    sp.dma_start(bias[:, j % 2], tables).then_inc(bias_in[j % 2], 16)
                    loop.i = None
            n.s += KVH * QT
            load_slabs(2)
            load_slabs(4, 3)
            load_slabs(SLABS_FF, FF_CHUNKS)
            load_slabs(1)
            dt_slab = 2 * MEM_SLABS + ATTN_SLABS + OUT_SLABS + FF_SLABS
            load_slabs(UT)
            sp.wait_ge(freed, dt_slab - KT + 1)
            sp.dma_start(h_next[:], h_in[0]).then_inc(h_loaded, 16)
            loop.per = SSM_PER
            with sp.Fori(0, PAIRS - 1) as i:
                for k in range(PAIR_SLABS):
                    src = slabs[bass.ds(sp.snap(i * PAIR_SLABS + (n.s + k)), 1)].rearrange("s p c -> (s p) c")
                    h_src = h_in[bass.ds(sp.snap(i + 1), 1)].rearrange("g p c -> (g p) c")
                    loop.i = i
                    load_slab(src, n.s + k)
                    if k == PAIR_SLABS // 2:
                        sp.wait_ge(off_done, at(loop, off_done, 1))
                        sp.wait_ge(hbd_done, at(loop, hbd_done, 1))
                        sp.dma_start(h_next[:], h_src).then_inc(h_loaded, 16)
                    loop.i = None
            n.s += (PAIRS - 1) * PAIR_SLABS
            load_slabs(XT + CQ_SLABS)
            sp.wait_ge(u_done, PAIRS * PAIR_SLABS)
            sp.wait_ge(tails_done, PAIRS * UT)
            sp.dma_start(kms1[:], mk_in[1]).then_inc(kms_in, 16)
            sp.dma_start(vms1[:], mv_in[1]).then_inc(kms_in, 16)
            sp.dma_start(conv_out, tails[:]).then_inc(conv_stored, 16)
            load_slabs(2)
            load_slabs(2)
            load_slabs(4, 3)
            load_slabs(SLABS_FF, FF_CHUNKS)
            for a, b in ((0, 2), (2, 4), (4, Y_POOL), (Y_POOL, KT - 1), (KT - 1, KT)):
                if b <= Y_POOL:
                    sp.wait_ge(x_done, 3 * KT + b)
                else:
                    sp.wait_ge(y_added, b - Y_POOL)
                sp.dma_start(y_out[:, a:b], x[:, a:b]).then_inc(stored, 16)
                stores[0] += 1
            sp.wait_ge(stored, 16 * stores[0])
            sp.wait_ge(conv_stored, 16)
            sp.wait_ge(h_stored, at(loop, h_stored, 16 * PAIRS))


def _conv_tiles(np):
    b, c = INNER // P, INNER // P + SGROUPS
    return np.array([t for g in range(PAIRS) for t in (3 * g, 3 * g + 1, 3 * g + 2, b + 2 * g, b + 2 * g + 1,
                                                       c + 2 * g, c + 2 * g + 1)])


def _layout(i, np):
    f = np.float32

    def tiles(w):
        k, c = w.shape
        return w.reshape(KT, P, c // P, P).transpose(2, 1, 0, 3).reshape(c // P, P, KT * P)

    def deep(w):
        return [tiles(w[c * D_MODEL:(c + 1) * D_MODEL]) for c in range(w.shape[0] // D_MODEL)]

    wa, ws = i["w_in_attn"][0], i["w_in_ssm"][0]
    parts = [tiles(i["w_mem_kv"][0]), tiles(i["w_mem_kv"][1])]
    k0, v0 = Q_W, Q_W + KV_W
    for h in range(KVH):
        w = wa[:, k0 + h * HD:k0 + (h + 1) * HD]
        parts.append(tiles(np.concatenate([w, w], 1)))
    parts += [tiles(wa[:, v0:v0 + P]), tiles(wa[:, v0 + HD:v0 + HD + P])]
    parts += [tiles(wa[:, :Q_W]), tiles(wa[:, Q_W + 2 * KV_W:])]

    def tail(layer):
        wo = np.stack(deep(i["w_out"][layer]), 1).reshape(-1, P, KT * P)
        up, down = i["w_up"][layer], i["w_down"][layer]
        out = [wo]
        for c in range(FF_CHUNKS):
            out += [tiles(up[:, c * D_MODEL:(c + 1) * D_MODEL]), tiles(down[c * D_MODEL:(c + 1) * D_MODEL])]
        return out

    parts += tail(0)
    zx, cx, dx = INNER, INNER + CONV_DIM, INNER + CONV_DIM + HEADS
    parts.append(tiles(np.concatenate([ws[:, cx:dx], np.zeros((D_MODEL, P - HEADS), f)], 1)))

    def z(g):
        return [slice(g * XT * P, (g + 1) * XT * P)]

    def xbc(g):
        return [slice(zx + g * XT * P, zx + (g + 1) * XT * P)] + [
            slice(at_ + g * 2 * P, at_ + (g + 1) * 2 * P) for at_ in (zx + INNER, zx + INNER + SGROUPS * STATE)]

    order = xbc(0)
    for g in range(PAIRS):
        order += z(g) + (xbc(g + 1) if g < PAIRS - 1 else [])
    parts += [tiles(ws[:, c]) for c in order]
    parts.append(tiles(ws[:, dx:]))
    parts += tail(1)
    slabs = np.concatenate(parts, 0)
    assert slabs.shape[0] == ALL_SLABS, slabs.shape

    def columns(a):
        a = a.reshape(-1, P)
        return a.T

    x = np.concatenate([i["x_sample"][0], i["x_prompt"][0]], 0)
    x = x.reshape(TOK, KT, P).transpose(2, 1, 0)
    wide = lambda a: np.broadcast_to(a.reshape(1, -1), (P, a.size))
    mem = i["mem_prompt"][0].reshape(N_MEM, KT, P).transpose(2, 1, 0)
    conv = np.concatenate([i["conv_w"][0], i["conv_b"][0][None], i["state_conv"][0, 0]], 0)
    conv = conv.reshape(TAPS, CONV_DIM // P, P)[:, _conv_tiles(np)].transpose(2, 1, 0)
    pairs = np.concatenate([i["ssm_norm"][0].reshape(PAIRS, XT, P).transpose(2, 0, 1),
                            wide(i["d_skip"]).reshape(P, PAIRS, PH)], 2)
    par = np.concatenate([columns(i[k]) for k in ("norm_mix_pre", "norm_mix_post", "norm_ffn_pre", "norm_ffn_post",
                                                  "mem_norm")]
                         + [wide(i[k]) for k in ("attn_sinks", "dt_bias", "a_log")]
                         + [conv.reshape(P, -1), pairs.reshape(P, -1)], 1)
    t = np.arange(P)
    mats = np.stack([np.eye(P), np.ones((P, P)), t[:, None] <= t[None], t[:, None] > t[None]], 1)
    r, c = np.arange(P)[:, None], np.arange(2 * P)[None]
    dist = np.abs(P + r - c).astype(f)
    seen = np.where(r < HD, c < P + HD, c >= HD)
    slopes = (2.0 ** (-8.0 * np.arange(1, HEADS + 1) / HEADS)).astype(f)
    tables = np.where(seen, -slopes[:, None, None] * dist, f(-1e30)).reshape(HEADS // 2, 2, P, 2 * P).transpose(0, 2, 1, 3)
    tables = np.concatenate([tables, tables[:2]], 0)
    ck = i["cache_swa_k"][0, 0].transpose(2, 1, 0)
    ck = np.concatenate([ck, ck], 0)
    cv = i["cache_swa_v"][0, 0]
    mk = i["cache_mem_k"][:, 0].transpose(0, 3, 2, 1)
    mv = i["cache_mem_v"][:, 0].reshape(2, 2, P, MEM_H, MEM_D).transpose(0, 2, 1, 3, 4).reshape(2, P, 2, MEM_W)
    h0 = i["state_ssm"][0, 0].reshape(PAIRS, PH * HD, STATE).transpose(0, 2, 1)
    out = dict(slabs=slabs, x=x, mem=mem, par=par, mats=mats, alibi=tables, ck=ck, cv=cv, mk=mk, mv=mv, h=h0)
    return {k: np.ascontiguousarray(v, dtype=f) for k, v in out.items()}


_OUTS = dict(y=(P, KT, TOK), swk=(HD, KVH, DEC + P), swv=(DEC + P, KVH, HD), h=(PAIRS, P, 2, PH * HD),
             conv=(P, PAIRS, UT, 2, PAST), mk=(2, P, MEM_H, N_MEM), mv=(2, P, 2, MEM_W))


def kernel(**inputs):
    import numpy as np
    import concourse.bacc as bacc
    from concourse.bass_utils import run_bass_kernel_spmd

    nc = bacc.Bacc("TRN2", target_bir_lowering=False, num_devices=1)
    arrays = _layout({k: np.asarray(v) for k, v in inputs.items()}, np)
    ins = [nc.dram_tensor(f"in_{k}", a.shape, F32, kind="ExternalInput").ap() for k, a in arrays.items()]
    outs = [nc.dram_tensor(f"out_{k}", s, F32, kind="ExternalOutput").ap() for k, s in _OUTS.items()]
    build(nc, *ins, outs)
    r = run_bass_kernel_spmd(nc, [{f"in_{k}": a for k, a in arrays.items()}], core_ids=[0]).results[0]
    o = {k: r[f"out_{k}"] for k in _OUTS}
    y = o["y"].transpose(2, 1, 0).reshape(TOK, D_MODEL)
    swk = o["swk"].transpose(2, 1, 0)
    swv = o["swv"]
    h = o["h"].transpose(2, 0, 3, 1).reshape(2, HEADS, HD, STATE)
    conv = o["conv"].reshape(P, PAIRS * UT, 2, PAST)[:, np.argsort(_conv_tiles(np))]
    conv = conv.transpose(2, 3, 1, 0).reshape(2, PAST, CONV_DIM)
    mk = o["mk"].transpose(0, 3, 2, 1)[:, None]
    mv = o["mv"].reshape(2, P, 2, MEM_H, MEM_D).transpose(0, 2, 1, 3, 4).reshape(2, 1, N_MEM, MEM_H, MEM_D)
    pair = lambda a: a[None, None]
    return (y[None, DEC:], y[None, :DEC], pair(swk[DEC:]), pair(swv[DEC:]), pair(h[1]), pair(conv[1]), mk, mv,
            pair(swk[:DEC]), pair(swv[:DEC]), pair(h[0]), pair(conv[0]))
```
